# Optimizing a Trainium2 kernel written in Bass

```python
import jax, jax.numpy as jnp
from jax import lax
import numpy as np

D_MODEL = 2048
BATCH = 1
SEQ = 256
DEPTH = 1

GRID_W = 64
D_ATTN = D_MODEL // 2
HEAD_DIM = 128
N_ATTN_HEADS = D_ATTN // HEAD_DIM
WIN_R = 8
WIN_C = 16
D_REC = D_MODEL - D_ATTN
REC_BLOCKS = 8
REC_BLOCK_W = D_REC // REC_BLOCKS
CONV_W = 4
C_RG = 8.0
D_IN_PROJ = 3 * D_ATTN + 2 * D_REC
D_FF = -(-8 * D_MODEL // (3 * 256)) * 256
D_PLE = 256
EPS = 1e-6
NEG_INF = -1e9


def rms_norm(x, g):
    x32 = x.astype(jnp.float32)
    y = x32 * lax.rsqrt(jnp.mean(x32 * x32, axis=-1, keepdims=True) + EPS)
    return (y * g.astype(jnp.float32)).astype(x.dtype)

def neighborhood_attention(q, k, v, rpb):
    B, S, H, Dh = q.shape
    rows = S // GRID_W
    kr = min(WIN_R, rows)
    cols = jnp.arange(GRID_W)
    cstart = jnp.clip(cols - WIN_C // 2, 0, GRID_W - WIN_C)
    col_ok = (cols[None, :] >= cstart[:, None]) & (cols[None, :] < cstart[:, None] + WIN_C)
    dc_idx = jnp.clip(cols[None, :] - cols[:, None] + WIN_C - 1, 0, 2 * WIN_C - 2)
    bias_col = jnp.where(col_ok[None, None], rpb.astype(jnp.float32)[:, :, dc_idx], NEG_INF)
    scale = HEAD_DIM ** -0.5
    qg = (q * scale).reshape(B, rows, GRID_W, H, Dh)
    kg = k.reshape(B, rows, GRID_W, H, Dh)
    vg = v.reshape(B, rows, GRID_W, H, Dh)

    def row_block(r):
        rstart = jnp.clip(r - kr // 2, 0, rows - kr)
        q_r = lax.dynamic_index_in_dim(qg, r, axis=1, keepdims=False)
        k_r = lax.dynamic_slice_in_dim(kg, rstart, kr, axis=1)
        v_r = lax.dynamic_slice_in_dim(vg, rstart, kr, axis=1)
        dr_idx = rstart + jnp.arange(kr) - r + WIN_R - 1
        bias = jnp.take(bias_col, dr_idx, axis=1)
        s = jnp.einsum('bqhd,bkwhd->bhkqw', q_r, k_r,
                       preferred_element_type=jnp.float32) + bias
        pr = jax.nn.softmax(s, axis=(2, 4)).astype(v.dtype)
        return jnp.einsum('bhkqw,bkwhd->bqhd', pr, v_r)

    out = lax.map(row_block, jnp.arange(rows))
    return out.transpose(1, 0, 2, 3, 4).reshape(B, S, H * Dh)

def linear_scan(a, b):
    def combine(l, r):
        return (l[0] * r[0], r[0] * l[1] + r[1])
    return lax.associative_scan(combine, (a, b), axis=1)[1]

def rglru_bidirectional(xr, conv_w, conv_b, w_a, b_a, w_i, b_i, lam):
    B, S, _ = xr.shape
    left = CONV_W // 2
    xp = jnp.pad(xr, ((0, 0), (left, CONV_W - 1 - left), (0, 0)))
    xc = conv_b + xp[:, 0:S] * conv_w[0]
    for j in range(1, CONV_W):
        xc = xc + xp[:, j:j + S] * conv_w[j]
    xb = xc.reshape(B, S, REC_BLOCKS, REC_BLOCK_W)
    r_gate = jax.nn.sigmoid(
        jnp.einsum('bsnc,zncd->zbsnd', xb, w_a).reshape(2, B, S, D_REC) + b_a[:, None, None, :])
    i_gate = jax.nn.sigmoid(
        jnp.einsum('bsnc,zncd->zbsnd', xb, w_i).reshape(2, B, S, D_REC) + b_i[:, None, None, :])
    log_a = -C_RG * r_gate.astype(jnp.float32) * jax.nn.softplus(-lam.astype(jnp.float32))[:, None, None, :]
    a = jnp.exp(log_a)
    bterm = jnp.sqrt(-jnp.expm1(2.0 * log_a)) * i_gate.astype(jnp.float32) * xc.astype(jnp.float32)[None]
    h_fwd = linear_scan(a[0], bterm[0])
    h_bwd = jnp.flip(linear_scan(jnp.flip(a[1], axis=1), jnp.flip(bterm[1], axis=1)), axis=1)
    return (h_fwd + h_bwd).astype(xr.dtype)

def first_inputs(seed: int = 0) -> dict:
    key = jax.random.key(seed)
    ks = jax.random.split(key, 32)
    f32 = jnp.float32

    def nrm(k, shape, scale):
        return jax.random.normal(k, shape, f32) * scale

    def gain(k, n):
        return 1.0 + 0.02 * jax.random.normal(k, (DEPTH, n), f32)

    u = jax.random.uniform(ks[10], (DEPTH, 2, D_REC), f32, minval=0.9, maxval=0.999)
    a0 = u ** (1.0 / C_RG)
    lam = jnp.log(a0) - jnp.log1p(-a0)
    return {
        "x": nrm(ks[0], (BATCH, SEQ, D_MODEL), 1.0),
        "p": nrm(ks[1], (DEPTH, BATCH, SEQ, D_PLE), 1.0),
        "g_mix_pre": gain(ks[2], D_MODEL),
        "w_in": nrm(ks[3], (DEPTH, D_MODEL, D_IN_PROJ), D_MODEL ** -0.5),
        "rpb": nrm(ks[4], (DEPTH, N_ATTN_HEADS, 2 * WIN_R - 1, 2 * WIN_C - 1), 0.02),
        "conv_w": nrm(ks[5], (DEPTH, CONV_W, D_REC), CONV_W ** -0.5),
        "conv_b": nrm(ks[6], (DEPTH, D_REC), 0.01),
        "w_rg_a": nrm(ks[7], (DEPTH, 2, REC_BLOCKS, REC_BLOCK_W, REC_BLOCK_W), REC_BLOCK_W ** -0.5),
        "b_rg_a": nrm(ks[8], (DEPTH, 2, D_REC), 0.01),
        "w_rg_i": nrm(ks[9], (DEPTH, 2, REC_BLOCKS, REC_BLOCK_W, REC_BLOCK_W), REC_BLOCK_W ** -0.5),
        "b_rg_i": nrm(ks[11], (DEPTH, 2, D_REC), 0.01),
        "lam": lam,
        "g_attn_out": gain(ks[12], D_ATTN),
        "g_rec_out": gain(ks[13], D_REC),
        "w_out": nrm(ks[14], (DEPTH, D_ATTN + D_REC, D_MODEL), (D_ATTN + D_REC) ** -0.5),
        "g_mix_post": gain(ks[15], D_MODEL),
        "g_ffn_pre": gain(ks[16], D_MODEL),
        "w_ffn_gate": nrm(ks[17], (DEPTH, D_MODEL, D_FF), D_MODEL ** -0.5),
        "w_ffn_up": nrm(ks[18], (DEPTH, D_MODEL, D_FF), D_MODEL ** -0.5),
        "w_ffn_down": nrm(ks[19], (DEPTH, D_FF, D_MODEL), D_FF ** -0.5),
        "g_ffn_post": gain(ks[20], D_MODEL),
        "g_ple_pre": gain(ks[21], D_MODEL),
        "w_ple_gate": nrm(ks[22], (DEPTH, D_MODEL, D_MODEL), D_MODEL ** -0.5),
        "w_ple_proj": nrm(ks[23], (DEPTH, D_PLE, D_MODEL), D_PLE ** -0.5),
        "g_ple_post": gain(ks[24], D_MODEL),
    }

def first_block(x, p, g_mix_pre, w_in, rpb, conv_w, conv_b, w_rg_a, b_rg_a, w_rg_i, b_rg_i,
              lam, g_attn_out, g_rec_out, w_out, g_mix_post, g_ffn_pre, w_ffn_gate,
              w_ffn_up, w_ffn_down, g_ffn_post, g_ple_pre, w_ple_gate, w_ple_proj, g_ple_post):
    B, S, _ = x.shape
    h = x
    for i in range(DEPTH):
        hn = rms_norm(h, g_mix_pre[i])
        u = hn @ w_in[i]
        q, k, v, xr, yg = jnp.split(
            u, [D_ATTN, 2 * D_ATTN, 3 * D_ATTN, 3 * D_ATTN + D_REC], axis=-1)
        attn = neighborhood_attention(
            q.reshape(B, S, N_ATTN_HEADS, HEAD_DIM),
            k.reshape(B, S, N_ATTN_HEADS, HEAD_DIM),
            v.reshape(B, S, N_ATTN_HEADS, HEAD_DIM), rpb[i])
        rec = rglru_bidirectional(xr, conv_w[i], conv_b[i], w_rg_a[i], b_rg_a[i],
                                  w_rg_i[i], b_rg_i[i], lam[i]) * jax.nn.gelu(yg)
        mixed = jnp.concatenate(
            [rms_norm(attn, g_attn_out[i]), rms_norm(rec, g_rec_out[i])], axis=-1) @ w_out[i]
        h = h + rms_norm(mixed, g_mix_post[i])
        fn = rms_norm(h, g_ffn_pre[i])
        ff = (jax.nn.silu(fn @ w_ffn_gate[i]) * (fn @ w_ffn_up[i])) @ w_ffn_down[i]
        h = h + rms_norm(ff, g_ffn_post[i])
        gate = jax.nn.sigmoid(rms_norm(h, g_ple_pre[i]) @ w_ple_gate[i])
        ple = p[i] @ w_ple_proj[i]
        h = h + rms_norm(gate * ple, g_ple_post[i])
    return h


A_HEADS = D_MODEL // (2 * HEAD_DIM)
A_WIDTH = A_HEADS * HEAD_DIM
DILATED_PAIRS = ((128, 1), (512, 4), (2048, 16))
BLK = 128
ROPE_THETA = 500000.0
A_ROT_DIM = HEAD_DIM // 4

B_HEADS = D_MODEL // (2 * HEAD_DIM)
MLA_Q_RANK = D_MODEL // 4
MLA_KV_RANK = D_MODEL // 4
MLA_NOPE = 128
MLA_ROPE = 64
MLA_V = 128
B_WIDTH = B_HEADS * MLA_V

MIX_WIDTH = A_WIDTH + B_WIDTH
IN_SPLITS = [A_WIDTH, 2 * A_WIDTH, 3 * A_WIDTH, 3 * A_WIDTH + MLA_Q_RANK,
             3 * A_WIDTH + MLA_Q_RANK + MLA_KV_RANK]
IN_COLS = 3 * A_WIDTH + MLA_Q_RANK + MLA_KV_RANK + MLA_ROPE

PEER_HEADS = 8
PEER_N_KEYS = 128
PEER_N_EXPERTS = PEER_N_KEYS ** 2
PEER_TOPK = 16
PEER_KEY_DIM = 256
PEER_CHUNK = 128

DN_ALPHA = (2 * DEPTH) ** 0.25
DN_BETA = (8 * DEPTH) ** -0.25


def layer_norm(x, g=None, b=None, eps=1e-5):
    xf = x.astype(jnp.float32)
    mu = xf.mean(-1, keepdims=True)
    var = jnp.square(xf - mu).mean(-1, keepdims=True)
    y = (xf - mu) * lax.rsqrt(var + eps)
    if g is not None:
        y = y * g.astype(jnp.float32) + b.astype(jnp.float32)
    return y.astype(x.dtype)

def rms_norm_2(x, g, eps=1e-6):
    xf = x.astype(jnp.float32)
    y = xf * lax.rsqrt(jnp.mean(xf * xf, -1, keepdims=True) + eps) * g.astype(jnp.float32)
    return y.astype(x.dtype)

def rope(x, pos, rot_dim):
    half = rot_dim // 2
    inv = ROPE_THETA ** (-jnp.arange(half, dtype=jnp.float32) * 2.0 / rot_dim)
    ang = pos[:, None] * inv[None, :]
    cos = jnp.cos(ang)[:, None, :]
    sin = jnp.sin(ang)[:, None, :]
    xf = x.astype(jnp.float32)
    x1 = xf[..., :half]
    x2 = xf[..., half:rot_dim]
    out = jnp.concatenate([x1 * cos - x2 * sin, x2 * cos + x1 * sin, xf[..., rot_dim:]], -1)
    return out.astype(x.dtype)

def dilated_window_attn(q, k, v, n_back, dil):
    B, S, H, E = q.shape
    L = S // dil
    nb = -(-L // BLK)
    Lp = nb * BLK

    def blocks(t):
        t = t.reshape(B, L, dil, H, E)
        t = jnp.pad(t, ((0, 0), (0, Lp - L), (0, 0), (0, 0), (0, 0)))
        return t.reshape(B, nb, BLK, dil, H, E)

    def with_prev(t):
        prev = jnp.pad(t, ((0, 0), (1, 0), (0, 0), (0, 0), (0, 0), (0, 0)))[:, :-1]
        return jnp.concatenate([prev, t], axis=2)

    qb = blocks(q)
    kk = with_prev(blocks(k))
    vv = with_prev(blocks(v))
    s = jnp.einsum('bnqrhe,bnkrhe->bnrhqk', qb, kk).astype(jnp.float32) * (E ** -0.5)
    qpos = jnp.arange(nb)[:, None] * BLK + jnp.arange(BLK)[None, :]
    kpos = jnp.arange(nb)[:, None] * BLK - BLK + jnp.arange(2 * BLK)[None, :]
    dist = qpos[:, :, None] - kpos[:, None, :]
    valid = (dist >= 0) & (dist <= n_back) & (kpos[:, None, :] >= 0)
    s = jnp.where(valid[None, :, None, None], s, -jnp.inf)
    m = s.max(-1, keepdims=True)
    p = jnp.exp(s - m)
    l = p.sum(-1, keepdims=True)
    o = jnp.einsum('bnrhqk,bnkrhe->bnqrhe', p.astype(vv.dtype), vv).astype(jnp.float32)
    l_t = jnp.moveaxis(l[..., 0], -1, 2)
    lse = jnp.moveaxis((m + jnp.log(l))[..., 0], -1, 2)
    o = o / l_t[..., None]
    o = o.reshape(B, Lp, dil, H, E)[:, :L].reshape(B, S, H, E)
    lse = lse.reshape(B, Lp, dil, H)[:, :L].reshape(B, S, H)
    return o, lse

def dilated_mixture(q, k, v):
    outs, lses = [], []
    for window, dil in DILATED_PAIRS:
        o, lse = dilated_window_attn(q, k, v, window // dil, dil)
        outs.append(o)
        lses.append(lse)
    wts = jax.nn.softmax(jnp.stack(lses, 0), axis=0)
    o = jnp.sum(wts[..., None] * jnp.stack(outs, 0), axis=0)
    return o.astype(q.dtype)

def mla_attention(q_nope, q_rope, k_nope, k_rope, v):
    B, S, H, _ = q_nope.shape
    nq = S // BLK
    scale = (MLA_NOPE + MLA_ROPE) ** -0.5
    kpos = jnp.arange(S)

    def to_blocks(t):
        return jnp.moveaxis(t.reshape(B, nq, BLK, *t.shape[2:]), 1, 0)

    def one_block(args):
        qn, qr, start = args
        s = (jnp.einsum('bqhe,bkhe->bhqk', qn, k_nope).astype(jnp.float32)
             + jnp.einsum('bqhr,bkr->bhqk', qr, k_rope).astype(jnp.float32)) * scale
        qpos = start + jnp.arange(BLK)
        s = jnp.where(kpos[None, :] <= qpos[:, None], s, -jnp.inf)
        p = jax.nn.softmax(s, axis=-1).astype(v.dtype)
        return jnp.einsum('bhqk,bkhe->bqhe', p, v)

    out = lax.map(one_block, (to_blocks(q_nope), to_blocks(q_rope), jnp.arange(nq) * BLK))
    return jnp.moveaxis(out, 0, 1).reshape(B, S, H, MLA_V)

def token_mix(h, pos, w_in, g_q_lat, g_kv_lat, w_uq, w_uk, w_uv, g_out_a, g_out_b, w_o):
    B, S, _ = h.shape
    proj = jnp.dot(h, w_in)
    qa, ka, va, cq, ckv, kr = jnp.split(proj, IN_SPLITS, axis=-1)
    qa = rope(qa.reshape(B, S, A_HEADS, HEAD_DIM), pos, A_ROT_DIM)
    ka = rope(ka.reshape(B, S, A_HEADS, HEAD_DIM), pos, A_ROT_DIM)
    va = va.reshape(B, S, A_HEADS, HEAD_DIM)
    o_a = dilated_mixture(qa, ka, va)
    cq = rms_norm_2(cq, g_q_lat)
    ckv = rms_norm_2(ckv, g_kv_lat)
    qb = jnp.dot(cq, w_uq).reshape(B, S, B_HEADS, MLA_NOPE + MLA_ROPE)
    q_nope = qb[..., :MLA_NOPE]
    q_rope = rope(qb[..., MLA_NOPE:], pos, MLA_ROPE)
    k_nope = jnp.dot(ckv, w_uk).reshape(B, S, B_HEADS, MLA_NOPE)
    v_b = jnp.dot(ckv, w_uv).reshape(B, S, B_HEADS, MLA_V)
    k_rope = rope(kr[:, :, None, :], pos, MLA_ROPE)[:, :, 0, :]
    o_b = mla_attention(q_nope, q_rope, k_nope, k_rope, v_b)
    o = jnp.concatenate([rms_norm_2(o_a.reshape(B, S, A_WIDTH), g_out_a),
                         rms_norm_2(o_b.reshape(B, S, B_WIDTH), g_out_b)], axis=-1)
    return jnp.dot(o, w_o)

def peer(h, w_pq, sub_key_1, sub_key_2, u_table, v_table):
    B, S, D = h.shape
    q = jnp.dot(h, w_pq).reshape(B, S, PEER_HEADS, 2, PEER_KEY_DIM // 2)
    s1 = jnp.einsum('bshe,ke->bshk', q[..., 0, :], sub_key_1).astype(jnp.float32)
    s2 = jnp.einsum('bshe,ke->bshk', q[..., 1, :], sub_key_2).astype(jnp.float32)
    v1, i1 = lax.top_k(s1, PEER_TOPK)
    v2, i2 = lax.top_k(s2, PEER_TOPK)
    cand = (v1[..., :, None] + v2[..., None, :]).reshape(B, S, PEER_HEADS, PEER_TOPK * PEER_TOPK)
    vals, ci = lax.top_k(cand, PEER_TOPK)
    idx = (jnp.take_along_axis(i1, ci // PEER_TOPK, -1) * PEER_N_KEYS
           + jnp.take_along_axis(i2, ci % PEER_TOPK, -1))
    g = jax.nn.softmax(vals, axis=-1)
    nc = (B * S) // PEER_CHUNK
    kk = PEER_HEADS * PEER_TOPK
    hc = h.reshape(nc, PEER_CHUNK, D)
    idc = idx.reshape(nc, PEER_CHUNK, kk)
    gc = g.reshape(nc, PEER_CHUNK, kk).astype(h.dtype)

    def chunk(args):
        ht, it, gt = args
        u = u_table[it]
        a = jnp.einsum('td,tkd->tk', ht, u)
        w = jax.nn.gelu(a.astype(jnp.float32), approximate=False).astype(ht.dtype) * gt
        return jnp.einsum('tk,tkd->td', w, v_table[it])

    return lax.map(chunk, (hc, idc, gc)).reshape(B, S, D)

def second_inputs(seed: int = 0) -> dict:
    key = jax.random.key(seed)
    ks = jax.random.split(key, 24)

    def nrm(k, shape, s):
        return jax.random.normal(k, shape, jnp.float32) * s

    col_scale = jnp.ones((IN_COLS,), jnp.float32).at[2 * A_WIDTH:3 * A_WIDTH].set(DN_BETA)
    return {
        'x': nrm(ks[0], (BATCH, SEQ, D_MODEL), 1.0),
        'c': nrm(ks[1], (BATCH, D_MODEL), 1.0),
        'w_ada': nrm(ks[2], (DEPTH, D_MODEL, 6 * D_MODEL), 0.5 * D_MODEL ** -0.5),
        'b_ada': nrm(ks[3], (DEPTH, 6 * D_MODEL), 0.02),
        'w_in': nrm(ks[4], (DEPTH, D_MODEL, IN_COLS), D_MODEL ** -0.5) * col_scale,
        'g_q_lat': 1.0 + nrm(ks[5], (DEPTH, MLA_Q_RANK), 0.02),
        'g_kv_lat': 1.0 + nrm(ks[6], (DEPTH, MLA_KV_RANK), 0.02),
        'w_uq': nrm(ks[7], (DEPTH, MLA_Q_RANK, B_HEADS * (MLA_NOPE + MLA_ROPE)), MLA_Q_RANK ** -0.5),
        'w_uk': nrm(ks[8], (DEPTH, MLA_KV_RANK, B_HEADS * MLA_NOPE), MLA_KV_RANK ** -0.5),
        'w_uv': nrm(ks[9], (DEPTH, MLA_KV_RANK, B_HEADS * MLA_V), MLA_KV_RANK ** -0.5 * DN_BETA),
        'g_out_a': 1.0 + nrm(ks[10], (DEPTH, A_WIDTH), 0.02),
        'g_out_b': 1.0 + nrm(ks[11], (DEPTH, B_WIDTH), 0.02),
        'w_o': nrm(ks[12], (DEPTH, MIX_WIDTH, D_MODEL), MIX_WIDTH ** -0.5 * DN_BETA),
        'ln1_g': 1.0 + nrm(ks[13], (DEPTH, D_MODEL), 0.02),
        'ln1_b': nrm(ks[14], (DEPTH, D_MODEL), 0.02),
        'w_pq': nrm(ks[15], (DEPTH, D_MODEL, PEER_HEADS * PEER_KEY_DIM), D_MODEL ** -0.5),
        'sub_key_1': nrm(ks[16], (DEPTH, PEER_N_KEYS, PEER_KEY_DIM // 2), (PEER_KEY_DIM // 2) ** -0.5),
        'sub_key_2': nrm(ks[17], (DEPTH, PEER_N_KEYS, PEER_KEY_DIM // 2), (PEER_KEY_DIM // 2) ** -0.5),
        'u_table': nrm(ks[18], (DEPTH, PEER_N_EXPERTS, D_MODEL), D_MODEL ** -0.5),
        'v_table': nrm(ks[19], (DEPTH, PEER_N_EXPERTS, D_MODEL), DN_BETA),
        'ln2_g': 1.0 + nrm(ks[20], (DEPTH, D_MODEL), 0.02),
        'ln2_b': nrm(ks[21], (DEPTH, D_MODEL), 0.02),
    }

def second_block(x, c, w_ada, b_ada, w_in, g_q_lat, g_kv_lat, w_uq, w_uk, w_uv, g_out_a, g_out_b,
              w_o, ln1_g, ln1_b, w_pq, sub_key_1, sub_key_2, u_table, v_table, ln2_g, ln2_b):
    S = x.shape[1]
    pos = jnp.arange(S, dtype=jnp.float32)
    c_act = jax.nn.silu(c)
    for l in range(DEPTH):
        mod = jnp.dot(c_act, w_ada[l]) + b_ada[l]
        sh1, sc1, g1, sh2, sc2, g2 = [m[:, None, :] for m in jnp.split(mod, 6, axis=-1)]
        h = layer_norm(x) * (1.0 + sc1) + sh1
        mix = token_mix(h, pos, w_in[l], g_q_lat[l], g_kv_lat[l], w_uq[l], w_uk[l], w_uv[l],
                        g_out_a[l], g_out_b[l], w_o[l])
        x = layer_norm(DN_ALPHA * x + g1 * mix, ln1_g[l], ln1_b[l])
        h = layer_norm(x) * (1.0 + sc2) + sh2
        ffn = peer(h, w_pq[l], sub_key_1[l], sub_key_2[l], u_table[l], v_table[l])
        x = layer_norm(DN_ALPHA * x + g2 * ffn, ln2_g[l], ln2_b[l])
    return x


_first_inputs = second_inputs


def second_inputs(seed=0):
    import zlib

    import numpy as np

    out = dict(_first_inputs(seed))
    spreads = {}
    factors = {'b_ada': 2.668,
     'g_q_lat': 8.0,
     'g_kv_lat': 8.0,
     'g_out_a': 8.0,
     'g_out_b': 8.0,
     'ln2_g': 2.874,
     'ln2_b': 2.765}
    for name, (base, spread) in spreads.items():
        noise = np.random.default_rng([zlib.crc32(name.encode()), seed]).standard_normal(out[name].shape)
        drawn = base * np.exp(spread * noise) if base else spread * noise
        out[name] = __import__('jax').numpy.asarray(drawn.astype(out[name].dtype))
    for name, factor in factors.items():
        out[name] = (out[name] * factor).astype(out[name].dtype)
    return out


_narrow_inputs = second_inputs


def second_inputs(seed=0):

    out = dict(_narrow_inputs(seed))
    wider = {'g_out_a': 4.46, 'g_out_b': 4.49, 'ln2_g': 3.2, 'ln2_b': 3.23}
    for name, times in wider.items():
        mean = out[name].mean()
        out[name] = (mean + times * (out[name] - mean)).astype(out[name].dtype)
    return out


def setup_inputs(seed=0):
    out = dict(first_inputs(seed))
    for name, value in second_inputs(seed + 1).items():
        if name != "x":
            out[name + "_2"] = value
    return out


def reference(
    x, p, g_mix_pre, w_in, rpb, conv_w, conv_b, w_rg_a, b_rg_a, w_rg_i, b_rg_i, lam, g_attn_out,
    g_rec_out, w_out, g_mix_post, g_ffn_pre, w_ffn_gate, w_ffn_up, w_ffn_down, g_ffn_post,
    g_ple_pre, w_ple_gate, w_ple_proj, g_ple_post, c_2, w_ada_2, b_ada_2, w_in_2, g_q_lat_2,
    g_kv_lat_2, w_uq_2, w_uk_2, w_uv_2, g_out_a_2, g_out_b_2, w_o_2, ln1_g_2, ln1_b_2, w_pq_2,
    sub_key_1_2, sub_key_2_2, u_table_2, v_table_2, ln2_g_2, ln2_b_2,
):
    x = first_block(
        x, p, g_mix_pre, w_in, rpb, conv_w, conv_b, w_rg_a, b_rg_a, w_rg_i, b_rg_i, lam,
        g_attn_out, g_rec_out, w_out, g_mix_post, g_ffn_pre, w_ffn_gate, w_ffn_up, w_ffn_down,
        g_ffn_post, g_ple_pre, w_ple_gate, w_ple_proj, g_ple_post,
    )
    return second_block(
        x, c_2, w_ada_2, b_ada_2, w_in_2, g_q_lat_2, g_kv_lat_2, w_uq_2, w_uk_2, w_uv_2,
        g_out_a_2, g_out_b_2, w_o_2, ln1_g_2, ln1_b_2, w_pq_2, sub_key_1_2, sub_key_2_2,
        u_table_2, v_table_2, ln2_g_2, ln2_b_2,
    )


_drawn_inputs = setup_inputs


def setup_inputs(seed=0):
    import zlib

    import numpy as np

    out = dict(_drawn_inputs(seed))
    spreads = {}
    factors = {'b_rg_a': 8.0, 'b_rg_i': 6.383, 'g_ple_pre': 3.607}
    for name, (base, spread) in spreads.items():
        noise = np.random.default_rng([zlib.crc32(name.encode()), seed]).standard_normal(out[name].shape)
        drawn = base * np.exp(spread * noise) if base else spread * noise
        out[name] = __import__('jax').numpy.asarray(drawn.astype(out[name].dtype))
    for name, factor in factors.items():
        out[name] = (out[name] * factor).astype(out[name].dtype)
    return out
```

```python
from contextlib import ExitStack, contextmanager

import numpy as np

import concourse.bass as bass
from concourse import mybir

ALU = mybir.AluOpType
ACT = mybir.ActivationFunctionType
AXX = mybir.AxisListType.X
F32 = mybir.dt.float32
I32 = mybir.dt.int32
U32 = mybir.dt.uint32

P = 128
S = 256
T = S // P
D = 2048
KD = D // P
HD = 128
NH = 8
DA = NH * HD
GRID_W, ROWS = 64, S // 64
WIN_R, WIN_C = 8, 16
RB = 8
CONV = 4
FF = 5632
KF = FF // P
EPS, EPS_LN = 1e-6, 1e-5
ALPHA = 2.0 ** 0.25
ROT_A, ROT_B = 16, 32
LAT = 512
KL = LAT // P
NKEY = 128
TOPK = 16
NSEL = NH * TOPK
NEG = -1e30
BAND = 512

CH = 2048
SLOTS = 8
BCH = 11 * BAND
BSLOTS = 2
ADA_W = 1024
ADA_G = 6 * D // ADA_W
ADA_SLOTS = 4

PHASES = [("xr", 8), ("yg", 8), ("q", 8), ("k", 8), ("v", 8), ("wout", 16), ("gateup", 2 * KF), ("down", 16),
          ("pproj", 2), ("pgate", 16), ("lat", 8), ("kr", 1), ("qk2", 16), ("v2", 8), ("mla", 7), ("wo", 16),
          ("pq", 16)]
OUTPUTS = {"xr": 8, "yg": 8, "q": 8, "k": 8, "v": 4, "wout": 8, "gateup": 88, "down": 8, "pproj": 8, "pgate": 8, "lat": 4,
           "kr": 2, "qk2": 8, "v2": 4, "mla": 8 + 2 + 8 + 4, "wo": 8, "pq": 16}

COLS = {}
_at = 0
for _n, _w in [("g_mix_pre", KD), ("g_attn_out", 8), ("g_rec_out", 8), ("g_ffn_pre", KD), ("g_ple_pre", KD),
               ("g_q_lat", KL), ("g_kv_lat", KL), ("g_out_a", 8), ("g_out_b", 8), ("conv_w", CONV * RB),
               ("conv_b", RB), ("b_rg_a", 2 * RB), ("b_rg_i", 2 * RB), ("lam", 2 * RB), ("c", KD)]:
    COLS[_n] = _at
    _at += _w
NCOLS = _at
ROW_NAMES = ["g_mix_post", "g_ffn_post", "g_ple_post", "ln1_g", "ln1_b", "ln2_g", "ln2_b"]
SH1, SC1, G1, SH2, SC2, G2 = range(6)


def stream_plan():
    plan, chunk, small, out = {}, 0, 0, 0
    for name, n in PHASES:
        plan[name] = dict(chunk=chunk, small=small, out=out, n=n)
        chunk += n
        out += OUTPUTS[name]
        if name != "down":
            small += n
    return plan, chunk


def build_program(nc, io):
    PLAN, N_CHUNKS = stream_plan()
    assert all(PLAN[p]["small"] % SLOTS == 0 for p in ("gateup", "down"))

    with ExitStack() as ctx:
        def sb(name, shape, dt=F32):
            return ctx.enter_context(nc.sbuf_tensor(name, shape, dt))

        sems = {}

        def sem(name):
            if name not in sems:
                sems[name] = ctx.enter_context(nc.semaphore(name))
            return sems[name]

        ring = sb("ring", [P, SLOTS * CH])
        resid = sb("resid", [P, T, D])
        nat = sb("nat", [P, T, D])
        xT = sb("xT", [P, KD, S])
        aux = sb("aux", [P, 2, D])
        big = sb("big", [P, KF * S])
        misc = sb("misc", [P, 7168])
        cols = sb("cols", [P, NCOLS])
        ident = sb("ident", [P, P])
        ones = sb("ones", [P, P])
        rope_t = sb("rope_t", [P, T, 2 * (ROT_A + ROT_B)])
        pT = sb("pT", [P, 2, S])
        conv_tmp = sb("conv_tmp", [P, 2, S])
        modc = sb("modc", [P, 2, KD])
        ssq = sb("ssq", [P, T, 4])
        st = sb("st", [P, 32])
        stats = sb("stats", [P, T, 4, 6])
        mv = sb("mv", [P, T, 2])
        sp = sb("sp", [P, 4, 2 * RB])
        mxs = sb("mxs", [P, 2, 2 * T])
        den = sb("den", [P, 2, 2 * T])
        cact = sb("cact", [P, KD])
        bank = [ctx.enter_context(nc.psum_tensor(f"bank{i}", [P, BAND], F32)) for i in range(8)]

        ygT = big[:, 0:2048].rearrange("p (b s) -> p b s", b=RB)
        qkT = big[:, 2048:6144].rearrange("p (b s) -> p b s", b=16)
        v1n = big[:, 6144:8192].rearrange("p (t c) -> p t c", t=T)
        xcT = big[:, 8192:10240].rearrange("p (b s) -> p b s", b=RB)
        XP = S + CONV
        xrT = big[:, 8448:8448 + RB * XP].rearrange("p (b s) -> p b s", b=RB)
        attn1 = big[:, 8192:10240].rearrange("p (t c) -> p t c", t=T)
        hidT = big[:, :].rearrange("p (f s) -> p f s", f=KF)
        ple = big[:, 0:T * D].rearrange("p (t c) -> p t c", t=T)
        qkv2 = big[:, 0:6144].rearrange("p (t c) -> p t c", t=T)
        lat = big[:, 6144:6144 + T * 2 * LAT].rearrange("p (t c) -> p t c", t=T)
        scratch2 = big[:, 6144:8192]
        rot = big[:, 8320:8320 + T * 9 * 64].rearrange("p (t c) -> p t c", t=T)
        masks = big[:, 9600:9600 + 2 * T * S].rearrange("p (m t k) -> p m t k", m=2, t=T)
        rows = big[:, 0:5 * D].rearrange("p (r c) -> p r c", r=5)
        bias1 = misc[:, 0:NH * 6 * GRID_W].rearrange("p (h r c) -> p h r c", h=NH, r=6)
        rg_w = misc[:, 3072:3072 + 32 * P].rearrange("p (z g b c) -> p z g b c", z=2, g=2, b=RB)
        scratch1 = misc[:, 3072:5120]
        ada_ring = misc[:, 0:ADA_SLOTS * ADA_W].rearrange("p (s c) -> p s c", s=ADA_SLOTS)
        ada_acc = misc[:, 4096:5120]
        mod_row = misc[:, 5120:6144]
        silu_g = misc[:, 6144:6656].rearrange("p (b s) -> p b s", b=2)
        latT = misc[:, 0:2 * KL * S].rearrange("p (k s) -> p k s", k=2 * KL)
        rotT = misc[:, 2048:2048 + 9 * S].rearrange("p (h s) -> p h s", h=9)
        v2n = misc[:, 4352:4352 + T * DA].rearrange("p (t c) -> p t c", t=T)
        subk = misc[:, 6400:6656].rearrange("p (a k) -> p a k", a=2)
        qb = misc[:, 0:2 * S].rearrange("p (b s) -> p b s", b=2)
        gidx = misc[:, 512:768].bitcast(I32).rearrange("p (t k) -> p t k", t=T)
        gwt = misc[:, 768:1024].rearrange("p (t k) -> p t k", t=T)
        dots = misc[:, 1024:1280].rearrange("p (t k) -> p t k", t=T)
        gstage = misc[:, 1280:1296].bitcast(I32)
        dstage = misc[:, 1296:1312]
        iota16 = misc[:, 1312:1328]

        o2 = xT[:, :, :].rearrange("p k s -> p (k s)").rearrange("p (t c) -> p t c", t=T)

        auxf = aux[:, :, :].rearrange("p a c -> p (a c)")
        tk_v12 = auxf[:, 0:256].rearrange("p (t h a k) -> p t h a k", t=T, h=4, a=2)
        tk_i12 = auxf[:, 256:512].bitcast(U32).rearrange("p (t h a k) -> p t h a k", t=T, h=4, a=2)
        tk_f12 = auxf[:, 512:768].rearrange("p (t h a k) -> p t h a k", t=T, h=4, a=2)
        tk_tmp = auxf[:, 768:1024]
        tk_cand = auxf[:, 1024:2048].rearrange("p (h i j) -> p h i j", h=4, i=16)
        tk_val = auxf[:, 2048:2176].rearrange("p (t h k) -> p t h k", t=T, h=4)
        tk_ci = auxf[:, 2176:2304].bitcast(U32).rearrange("p (t h k) -> p t h k", t=T, h=4)
        tk_ab = auxf[:, 2304:2560].bitcast(U32).rearrange("p (a c) -> p a c", a=2)
        tk_abf = auxf[:, 2560:2816].rearrange("p (a t h k) -> p a t h k", a=2, t=T, h=4)
        tk_hot = auxf[:, 2816:3840].rearrange("p (n k) -> p n k", k=16)
        tk_sum = auxf[:, 3840:3904]
        tk_pick = auxf[:, 3904:4032].rearrange("p (a n) -> p a n", a=2)

        mod_dram = nc.dram_tensor("mod_dram", [6, D], F32).ap()

        slot_loaded = [sem(f"slot_loaded{i}") for i in range(SLOTS)]
        big_loaded = [sem(f"big_loaded{i}") for i in range(BSLOTS)]
        ada_loaded = [sem(f"ada_loaded{i}") for i in range(ADA_SLOTS)]
        multiplied = sem("multiplied")
        taken = sem("taken")
        for n in ("x_in", "cols_in", "consts_in", "bias_in", "rg_in", "bias_masked", "dve_step", "act_step", "pool_step",
                  "ones_set", "rms_in", "root_out", "hn_ready", "xr_padded", "conv_done", "gates",
                  "gates_taken", "gates_ready", "rec_b2", "rec_root", "rec_scan", "rec_sum", "rec_sq",
                  "rec_norm", "rec_normed", "aux_free", "row_in", "ssq_in", "resid_piece", "silu_done",
                  "ada_used", "ada_sum", "ada_rowsum", "mod_ready", "mod_b_in", "mod_out", "cact_ready",
                  "modc_in", "pgate_sig", "misc_in", "lat_ready", "rope_done", "rotq_ready", "rows_in",
                  "rows2_in", "h2_ready", "scores", "scores_taken", "idx_staged", "w_in", "w_out_", "v_done",
                  "out_ready", "out_done", "sk_in", "iota_done", "topk_exp_in", "topk_exp_out", "o_ready",
                  "modc_ready", "row2_in", "row3_in", "ple_ready", "attn1_ready", "softplus_in", "softplus_exp",
                  "chosen"):
            sem(n)
        gath = [sem(f"gathered{i}") for i in range(8)]
        row_used = sem("row_used")

        block = ctx.enter_context(nc.Block())

        def slot_of(phase, j):
            return (PLAN[phase]["small"] + j) % SLOTS

        def loads_before(phase, j):
            return (PLAN[phase]["small"] + j) // SLOTS

        def wait_loaded(eng, phase, j, it=0):
            eng.wait_ge(slot_loaded[slot_of(phase, j)], 16 * (loads_before(phase, j) + 1) + 16 * it)

        def slot_ap(phase, j):
            s = slot_of(phase, j)
            return ring[:, s * CH:(s + 1) * CH]

        def wait_multiplied(eng, phase, j, it=0, per=0):
            eng.wait_ge(multiplied, PLAN[phase]["chunk"] + j + 1 + per * it)

        def out_no(phase, o):
            return PLAN[phase]["out"] + o

        def out_bank(phase, o):
            return bank[out_no(phase, o) % 4]

        def wait_bank(pe, phase, o, it=0, per=0):
            n = out_no(phase, o) - 3
            if n > 0:
                pe.wait_ge(taken, n + per * it)

        def loop(eng, n):
            return eng.Fori(0, n)

        class Steps:

            def __init__(self, eng, name):
                self.eng, self.sem, self.n, self.off = eng, sem(name), 0, 0

            def link(self, ins):
                ins.then_inc(self.sem, 1)
                self.n += 1
                self.eng.wait_ge(self.sem, self.n + self.off)

            def mark(self, ins):
                ins.then_inc(self.sem, 1)
                self.n += 1

            def wait(self):
                self.eng.wait_ge(self.sem, self.n + self.off)

            @contextmanager
            def loop(self, n, per):
                with self.eng.Fori(0, n) as it:
                    start, self.off = self.n, it * per
                    yield it
                    assert self.n == start + per, (self.n - start, per)
                self.off = 0
                self.n = start + n * per

        TURNS = {}

        def turn_sems(name):
            if name not in TURNS:
                TURNS[name] = (sem(f"{name}_turned"), sem(f"{name}_taken_v"), sem(f"{name}_taken_a"))
            return TURNS[name]

        for n in ("n1", "n2", "n3", "n4", "n5", "n6", "n7", "n8", "tq", "tr"):
            turn_sems(n)

        def turn_pe(pe, name, n, src, width=P):
            turned, tv, ta = turn_sems(name)
            for k in range(n):
                if k >= 4:
                    pe.wait_ge(ta if k % 2 else tv, (k - 4) // 2 + 1)
                for t in range(T):
                    m = pe.transpose(bank[4 + k % 4][0:width, t * P:(t + 1) * P], src(k, t), ident[:, :])
                m.then_inc(turned, 1)

        def turn_out(eng, name, n, dst, scale=None, shift=None, width=P):
            turned, tv, ta = turn_sems(name)
            odd = eng is nc.scalar
            for k in range(1 if odd else 0, n, 2):
                eng.wait_ge(turned, k + 1)
                ps = bank[4 + k % 4][0:width, 0:S]
                if odd:
                    if shift is not None:
                        i = eng.activation(dst(k), ps, ACT.Identity, scale=scale(k), bias=shift(k))
                    elif scale is not None:
                        i = eng.activation(dst(k), ps, ACT.Copy, scale=scale(k))
                    else:
                        i = eng.activation(dst(k), ps, ACT.Copy)
                    i.then_inc(ta, 1)
                else:
                    if shift is not None:
                        i = eng.tensor_scalar(dst(k), ps, scale(k), shift(k), ALU.mult, ALU.add)
                    elif scale is not None:
                        i = eng.tensor_scalar(dst(k), ps, scale(k), None, ALU.mult)
                    else:
                        i = eng.tensor_copy(dst(k), ps)
                    i.then_inc(tv, 1)

        def wait_turned_out(eng, name, n):
            _, tv, ta = turn_sems(name)
            eng.wait_ge(tv, (n + 1) // 2)
            if n > 1:
                eng.wait_ge(ta, n // 2)

        def gain(name, first=0):
            return lambda k: cols[:, COLS[name] + first + k:COLS[name] + first + k + 1]

        def product_t(pe, phase, j, o, kk=KD, x=None, it=0, per_out=0, sub=0, last=True, wait=True):
            if wait:
                wait_loaded(pe, phase, j, it)
            wait_bank(pe, phase, o, it, per_out)
            w = slot_ap(phase, j)
            for k in range(kk):
                m = pe.matmul(out_bank(phase, o)[:, 0:S], w[:, (sub * kk + k) * P:(sub * kk + k + 1) * P],
                              (x or (lambda k: xT[:, k, :]))(k), start=(k == 0), stop=(k == kk - 1))
            if last:
                m.then_inc(multiplied, 1)

        def product_n(pe, phase, j0, o, nch, kk, lhs, it=0, per_out=0, width=BAND, sub=0, last=True, wait=True):
            for c in range(nch):
                if wait:
                    wait_loaded(pe, phase, j0 + c, it)
                if c == 0:
                    wait_bank(pe, phase, o + T - 1, it, per_out)
                w = slot_ap(phase, j0 + c)
                for k in range(kk):
                    for t in range(T):
                        m = pe.matmul(out_bank(phase, o + t)[:, 0:width], lhs(c * kk + k, t),
                                      w[:, sub * kk * BAND + k * width:sub * kk * BAND + (k + 1) * width],
                                      start=(c == 0 and k == 0), stop=(c == nch - 1 and k == kk - 1))
                if last:
                    m.then_inc(multiplied, 1)

        def x_lhs(k, t):
            return xT[:, k, t * P:(t + 1) * P]

        def n_lhs(k, t):
            return natT[:, k, t * P:(t + 1) * P]

        natT = nat[:, :, :].rearrange("p t c -> p (t c)").rearrange("p (k s) -> p k s", k=KD)

        KINDS = ("at1", "at2", "at3")
        for n in KINDS:
            for m in ("scored", "biased", "exped", "turned", "pt_out", "valued", "out"):
                sem(f"{n}_{m}")

        def attention_pe(pe, kind, score, value, scratch):
            prob, prT = attention_scratch(scratch)

            def scores(h):
                if h >= 2:
                    pe.wait_ge(sem(f"{kind}_biased"), h - 1)
                for t in range(T):
                    m = score(pe, h, t, bank[h % 2][:, t * S:(t + 1) * S])
                m.then_inc(sem(f"{kind}_scored"), 1)

            def turn(h):
                pe.wait_ge(sem(f"{kind}_exped"), h + 1)
                if h >= 2:
                    pe.wait_ge(sem(f"{kind}_pt_out"), h - 1)
                for kc in range(T):
                    for t in range(T):
                        m = pe.transpose(bank[2 + h % 2][:, kc * S + t * P:kc * S + (t + 1) * P],
                                         prob[:, h % 2, t, kc * P:(kc + 1) * P], ident[:, :])
                m.then_inc(sem(f"{kind}_turned"), 1)

            def values(h):
                pe.wait_ge(sem(f"{kind}_pt_out"), h + 1)
                if h >= 2:
                    pe.wait_ge(sem(f"{kind}_out"), h - 1)
                for t in range(T):
                    for kc in range(T):
                        m = pe.matmul(bank[4 + h % 2][:, t * P:(t + 1) * P], prT[:, h % 2, kc, t * P:(t + 1) * P],
                                      value(kc, h), start=(kc == 0), stop=(kc == T - 1))
                m.then_inc(sem(f"{kind}_valued"), 1)

            scores(0)
            for h in range(NH):
                if h + 1 < NH:
                    scores(h + 1)
                turn(h)
                if h:
                    values(h - 1)
            values(NH - 1)

        def attention_scratch(scratch):
            prob = scratch[:, 0:1024].rearrange("p (b t k) -> p b t k", b=2, t=T)
            prT = scratch[:, 1024:2048].rearrange("p (b c q) -> p b c q", b=2, c=T)
            return prob, prT

        def by_row(ap):
            return ap.rearrange("p (r c) -> p r c", c=GRID_W)

        def attention_dve(v, steps, kind, bias, scale, out, scratch):
            prob, prT = attention_scratch(scratch)

            def biased(h):
                v.wait_ge(sem(f"{kind}_scored"), h + 1)
                if h >= 2:
                    v.wait_ge(sem(f"{kind}_turned"), h - 1)
                for t in range(T):
                    i = v.scalar_tensor_tensor(out=by_row(prob[:, h % 2, t, :]),
                                               in0=by_row(bank[h % 2][:, t * S:(t + 1) * S]),
                                               scalar=scale, in1=bias(h, t), op0=ALU.mult, op1=ALU.add)
                    if t == T - 1:
                        i.then_inc(sem(f"{kind}_biased"), 1)
                    else:
                        steps.mark(i)
                steps.wait()
                v.wait_ge(sem(f"{kind}_biased"), h + 1)
                steps.link(v.tensor_reduce(mxs[:, h % 2, 0:T], prob[:, h % 2, :, :], AXX, ALU.max))
                v.tensor_scalar(mxs[:, h % 2, T:2 * T], mxs[:, h % 2, 0:T], -1.0, None, ALU.mult).then_inc(
                    sem(f"{kind}_negmax"), 1)

            def result(h):
                v.wait_ge(sem(f"{kind}_exped"), h + 1)
                steps.link(v.reciprocal(den[:, h % 2, T:2 * T], den[:, h % 2, 0:T]))
                v.wait_ge(sem(f"{kind}_valued"), h + 1)
                for t in range(T):
                    i = v.tensor_scalar(out(h, t), bank[4 + h % 2][:, t * P:(t + 1) * P],
                                        den[:, h % 2, T + t:T + t + 1], None, ALU.mult)
                    if t == T - 1:
                        i.then_inc(sem(f"{kind}_out"), 1)
                    else:
                        steps.mark(i)
                steps.wait()

            for h in range(NH):
                biased(h)
                if h >= 2:
                    result(h - 2)
            result(NH - 2)
            result(NH - 1)
            v.wait_ge(sem(f"{kind}_out"), NH)

        def attention_act(a, kind, scratch):
            prob, prT = attention_scratch(scratch)

            def exps(h):
                a.wait_ge(sem(f"{kind}_negmax"), h + 1)
                if h >= 2:
                    a.wait_ge(sem(f"{kind}_out"), h - 1)
                for t in range(T):
                    i = a.activation(prob[:, h % 2, t, :], prob[:, h % 2, t, :], ACT.Exp,
                                     bias=mxs[:, h % 2, T + t:T + t + 1], accum_out=den[:, h % 2, t:t + 1])
                i.then_inc(sem(f"{kind}_exped"), 1)

            def turned(h):
                a.wait_ge(sem(f"{kind}_turned"), h + 1)
                if h >= 2:
                    a.wait_ge(sem(f"{kind}_valued"), h - 1)
                a.activation(prT[:, h % 2, :, :].rearrange("p c q -> p (c q)"), bank[2 + h % 2][:, :], ACT.Copy)\
                    .then_inc(sem(f"{kind}_pt_out"), 1)

            exps(0)
            for h in range(NH):
                if h + 1 < NH:
                    exps(h + 1)
                turned(h)

        for n in KINDS:
            sem(f"{n}_negmax")

        wst = io["stream"]

        @block.sync
        def _(sp_):
            for t in range(T):
                sp_.dma_start(resid[:, t, :], io["x"][0, t * P:(t + 1) * P, :]).then_inc(sem("x_in"), 16)

            def load(phase, j, it=None, gate=True):
                s = slot_of(phase, j)
                small = PLAN[phase]["small"] + j
                chunk = PLAN[phase]["chunk"] + j
                if it is None or isinstance(it, int):
                    sp_.dma_start(ring[:, s * CH:(s + 1) * CH], wst[small]).then_inc(slot_loaded[s], 16)
                else:
                    sp_.dma_start(ring[:, s * CH:(s + 1) * CH],
                                  wst[bass.ds(small + it * SLOTS, 1)].rearrange("n p c -> (n p) c"))\
                        .then_inc(slot_loaded[s], 16)

            def stream(phase, n, j0=0):
                rounds = n // SLOTS
                assert n % SLOTS == 0
                if rounds == 1:
                    for j in range(SLOTS):
                        sp_.wait_ge(multiplied, PLAN[phase]["chunk"] + j0 + j - SLOTS + 1)
                        load(phase, j0 + j)
                    return
                with loop(sp_, rounds) as it:
                    for j in range(SLOTS):
                        sp_.wait_ge(multiplied, PLAN[phase]["chunk"] + j0 + j - SLOTS + 1 + it * SLOTS)
                        load(phase, j0 + j, it)

            for j in range(SLOTS):
                load("xr", j)
            stream("yg", 8)
            stream("q", 8)
            stream("k", 8)
            stream("v", 8)
            stream("wout", 16)

            def ada_load(j, g):
                for k in (2 * j, 2 * j + 1):
                    s = k % ADA_SLOTS
                    sp_.wait_ge(sem("ada_used"), KD * g + k + 1)
                    sp_.dma_start(ada_ring[:, s, :], io["w_ada"][k * P:(k + 1) * P, bass.ds(g * ADA_W, ADA_W)])\
                        .then_inc(ada_loaded[s], 16)

            stream("gateup", SLOTS)
            with loop(sp_, KF // 4 - 1) as it:
                for j in range(SLOTS):
                    sp_.wait_ge(multiplied, PLAN["gateup"]["chunk"] + j + 1 + it * SLOTS)
                    load("gateup", SLOTS + j, it)
                    ada_load(j, it)

            gu_end = PLAN["down"]["chunk"]

            def load_big(c, it=0):
                s = c % BSLOTS
                src = io["down"][c] if isinstance(it, int) else \
                    io["down"][bass.ds(c + it * 8, 1)].rearrange("n p c -> (n p) c")
                sp_.dma_start(ring[:, s * BCH:(s + 1) * BCH], src).then_inc(big_loaded[s], 16)

            for j in range(4):
                ada_load(j, ADA_G - 2)
            sp_.wait_ge(multiplied, gu_end - SLOTS + 3)
            load_big(0)
            for j in range(4, 8):
                ada_load(j, ADA_G - 2)
            sp_.wait_ge(multiplied, gu_end - SLOTS + 6)
            load_big(1)
            for j in range(8):
                ada_load(j, ADA_G - 1)
            for c in range(2, 16):
                sp_.wait_ge(multiplied, gu_end + c - BSLOTS + 1)
                load_big(c)
            down_end = PLAN["pproj"]["chunk"]
            assert PLAN["pproj"]["small"] % SLOTS == 0
            first = [("pproj", 0), ("pproj", 1)] + [("pgate", j) for j in range(6)]
            for n, (ph, j) in enumerate(first):
                if n == 0:
                    sp_.wait_ge(multiplied, down_end - 1)
                if n == 2:
                    sp_.wait_ge(multiplied, down_end)
                load(ph, j)

            def rest(phase, j0, n):
                for j in range(j0, j0 + n):
                    sp_.wait_ge(multiplied, PLAN[phase]["chunk"] + j - SLOTS + 1)
                    load(phase, j)

            rest("pgate", 6, 10)
            rest("lat", 0, 8)
            rest("kr", 0, 1)
            stream("qk2", 16)
            stream("v2", 8)
            rest("mla", 0, 7)
            stream("wo", 16)
            stream("pq", 16)

            for t in range(T):
                sp_.wait_ge(sem("out_ready"), t + 1)
                sp_.dma_start(io["out"][0, t * P:(t + 1) * P, :], resid[:, t, :]).then_inc(sem("out_done"), 16)
            sp_.wait_ge(sem("out_done"), 16 * T)

        @block.tensor
        def _(pe):
            pe.wait_ge(sem("consts_in"), 16 * 3)
            pe.wait_ge(sem("ones_set"), 1)
            pe.wait_ge(sem("hn_ready"), 1)
            turn_pe(pe, "n1", KD, lambda k, t: nat[:, t, k * P:(k + 1) * P])
            wait_turned_out(pe, "n1", KD)
            for j in range(RB):
                product_t(pe, "xr", j, j)
            for j in range(RB):
                product_t(pe, "yg", j, j)

            def gates(z):
                if z == 0:
                    pe.wait_ge(sem("rg_in"), 16)
                for b in range(RB):
                    pe.wait_ge(sem("conv_done"), b + 1)
                    n = z * RB + b
                    if n >= 4:
                        pe.wait_ge(sem("gates_taken"), n - 3)
                    for g in range(2):
                        m = pe.matmul(bank[4 + n % 4][:, g * S:(g + 1) * S], rg_w[:, z, g, b, :], xcT[:, b, :],
                                      start=True, stop=True)
                    m.then_inc(sem("gates"), 1)

            gates(0)
            for j in range(RB):
                product_t(pe, "q", j, j)
            gates(1)
            for j in range(RB):
                product_t(pe, "k", j, j)
            for c in range(2):
                product_n(pe, "v", 4 * c, 2 * c, 4, 4, x_lhs)
            pe.wait_ge(sem("bias_masked"), 4)
            pe.wait_ge(taken, out_no("wout", 0))
            pe.wait_ge(sem("gates_taken"), 2 * RB)

            def score1(pe, h, t, ps):
                return pe.matmul(ps, qkT[:, h, t * P:(t + 1) * P], qkT[:, NH + h, :], start=True, stop=True)

            attention_pe(pe, "at1", score1, lambda kc, h: v1n[:, kc, h * HD:(h + 1) * HD], scratch1)
            pe.wait_ge(sem("attn1_ready"), 1)
            pe.wait_ge(sem("at1_out"), NH)
            turn_pe(pe, "n2", 8, lambda k, t: attn1[:, t, k * P:(k + 1) * P])
            wait_turned_out(pe, "n2", 8)
            pe.wait_ge(sem("rec_sq"), 1)
            for b in range(RB):
                m = pe.matmul(bank[4][:, 0:S], ones[:, :], nat[:, 0, b * S:(b + 1) * S], start=(b == 0),
                              stop=(b == RB - 1))
            m.then_inc(sem("rec_norm"), 1)
            pe.wait_ge(sem("rec_normed"), RB)
            with loop(pe, 2) as it:
                for c in range(2):
                    product_n(pe, "wout", 4 * c, 2 * c, 4, 4, x_lhs, it=it, per_out=4)
            pe.wait_ge(sem("hn_ready"), 2)
            turn_pe(pe, "n3", KD, lambda k, t: nat[:, t, k * P:(k + 1) * P])
            wait_turned_out(pe, "n3", KD)

            def ada_sum(g):
                pe.wait_ge(sem("ada_sum"), g + 1)
                for c in range(2):
                    m = pe.matmul(bank[4 + c][0:1, :], ones[:, 0:1], ada_acc[:, c * BAND:(c + 1) * BAND],
                                  start=True, stop=True)
                m.then_inc(sem("ada_rowsum"), 1)

            with loop(pe, KF // 4) as it:
                for j in range(8):
                    product_t(pe, "gateup", j, j, it=it, per_out=8)
                ada_sum(it)
            pe.wait_ge(taken, out_no("down", 0))
            for c in range(4):
                for q in range(4):
                    n = 4 * c + q
                    pe.wait_ge(big_loaded[n % BSLOTS], 16 * (n // BSLOTS + 1))
                    if q == 0:
                        wait_bank(pe, "down", 2 * c + 1)
                    for k in range(11):
                        for t in range(T):
                            m = pe.matmul(out_bank("down", 2 * c + t)[:, :],
                                          hidT[:, 11 * q + k, t * P:(t + 1) * P],
                                          ring[:, (n % BSLOTS) * BCH + k * BAND:(n % BSLOTS) * BCH + (k + 1) * BAND],
                                          start=(q == 0 and k == 0), stop=(q == 3 and k == 10))
                    m.then_inc(multiplied, 1)
                if c == 0:
                    ada_sum(ADA_G - 1)
            for c in range(4):
                product_n(pe, "pproj", c // 2, 2 * c, 1, 2, lambda k, t: pT[:, k, t * P:(t + 1) * P], sub=c % 2,
                          last=(c % 2 == 1))
            pe.wait_ge(sem("hn_ready"), 3)
            turn_pe(pe, "n4", KD, lambda k, t: nat[:, t, k * P:(k + 1) * P])
            wait_turned_out(pe, "n4", KD)
            with loop(pe, 2) as it:
                for c in range(2):
                    product_n(pe, "pgate", 4 * c, 2 * c, 4, 4, x_lhs, it=it, per_out=4)

            pe.wait_ge(sem("hn_ready"), 4)
            turn_pe(pe, "n5", KD, lambda k, t: nat[:, t, k * P:(k + 1) * P])
            wait_turned_out(pe, "n5", KD)
            for c in range(2):
                product_n(pe, "lat", 4 * c, 2 * c, 4, 4, x_lhs)
            product_n(pe, "kr", 0, 0, 1, KD, x_lhs, width=64)
            with loop(pe, 2) as it:
                for c in range(2):
                    product_n(pe, "qk2", 4 * c, 2 * c, 4, 4, x_lhs, it=it, per_out=4)
            pe.wait_ge(sem("lat_ready"), 1)
            turn_pe(pe, "n6", 2 * KL, lambda k, t: lat[:, t, k * P:(k + 1) * P])
            for c in range(2):
                product_n(pe, "v2", 4 * c, 2 * c, 4, 4, x_lhs)
            pe.wait_ge(sem("rope_done"), 1)
            wait_turned_out(pe, "n6", 2 * KL)
            turn_pe(pe, "tq", 2 * NH, lambda k, t: qkv2[:, t, k * P:(k + 1) * P])
            for c in range(2):
                for s in range(4):
                    product_t(pe, "mla", c, 4 * c + s, kk=KL, x=lambda k: latT[:, k, :], sub=s, last=(s == 3))
            product_n(pe, "mla", 2, 8, 1, KL, lambda k, t: latT[:, k, t * P:(t + 1) * P])
            for c in range(2):
                for s in range(4):
                    product_t(pe, "mla", 3 + c, 10 + 4 * c + s, kk=KL, x=lambda k: latT[:, KL + k, :], sub=s,
                              last=(s == 3))
            for c in range(2):
                product_n(pe, "mla", 5 + c, 18 + 2 * c, 1, KL, lambda k, t: latT[:, KL + k, t * P:(t + 1) * P])
            wait_turned_out(pe, "tq", 2 * NH)
            pe.wait_ge(sem("rotq_ready"), 1)
            turn_pe(pe, "tr", 9, lambda k, t: rot[:, t, k * 64:(k + 1) * 64], width=64)
            wait_turned_out(pe, "tr", 9)
            pe.wait_ge(taken, out_no("wo", 0))

            def score2(pe, h, t, ps):
                return pe.matmul(ps, natT[:, h, t * P:(t + 1) * P], natT[:, NH + h, :], start=True, stop=True)

            def score3(pe, h, t, ps):
                pe.matmul(ps, aux[:, 0, h * S + t * P:h * S + (t + 1) * P], aux[:, 1, h * S:(h + 1) * S],
                          start=True, stop=False)
                return pe.matmul(ps, rotT[0:64, h, t * P:(t + 1) * P], rotT[0:64, 8, :], start=False, stop=True)

            pe.wait_ge(sem("misc_in"), 16)
            attention_pe(pe, "at2", score2, lambda kc, h: qkv2[:, kc, 2 * DA + h * HD:2 * DA + (h + 1) * HD], scratch2)
            pe.wait_ge(sem("at2_out"), NH)
            attention_pe(pe, "at3", score3, lambda kc, h: v2n[:, kc, h * HD:(h + 1) * HD], scratch2)
            pe.wait_ge(sem("at3_out"), NH)
            pe.wait_ge(sem("o_ready"), 1)
            turn_pe(pe, "n7", KD, lambda k, t: o2[:, t, k * P:(k + 1) * P])
            wait_turned_out(pe, "n7", KD)
            with loop(pe, 2) as it:
                for c in range(2):
                    product_n(pe, "wo", 4 * c, 2 * c, 4, 4, n_lhs, it=it, per_out=4)
            pe.wait_ge(sem("h2_ready"), 1)
            turn_pe(pe, "n8", KD, lambda k, t: nat[:, t, k * P:(k + 1) * P])
            wait_turned_out(pe, "n8", KD)
            pe.wait_ge(sem("sk_in"), 16)

            with loop(pe, 2) as it:
                def key_scores(j):
                    pe.wait_ge(taken, out_no("pq", j) + 1 + it * 8)
                    if j >= 2:
                        pe.wait_ge(sem("scores_taken"), it * 8 + j - 1)
                    else:
                        pe.wait_ge(sem("scores_taken"), it * 8)
                    for t in range(T):
                        m = pe.matmul(bank[4 + j % 2][:, t * P:(t + 1) * P], qb[:, j % 2, t * P:(t + 1) * P],
                                      subk[:, j % 2, :], start=True, stop=True)
                    m.then_inc(sem("scores"), 1)

                for j in range(8):
                    product_t(pe, "pq", j, j, it=it, per_out=8)
                    if j:
                        key_scores(j - 1)
                key_scores(7)

        @block.scalar
        def _(a):
            steps = Steps(a, "act_step")
            a.wait_ge(sem("cols_in"), 16)
            a.wait_ge(sem("softplus_in"), 1)
            a.activation(sp[:, 1, :], sp[:, 0, :], ACT.Exp, scale=-1.0).then_inc(sem("softplus_exp"), 1)

            def root(n):
                a.wait_ge(sem("rms_in"), n)
                a.activation(st[:, 2:4], st[:, 0:2], ACT.Sqrt).then_inc(sem("root_out"), 1)

            def copy_out(phase, o, dst, it=0, per_chunks=0, chunk=0, func=ACT.Copy, width=BAND, signal=True):
                wait_multiplied(a, phase, chunk, it, per_chunks)
                i = a.activation(dst, out_bank(phase, o)[:, 0:width], func)
                if signal:
                    i.then_inc(taken, 1)
                return i

            root(1)
            turn_out(nc.scalar, "n1", KD, lambda k: xT[:, k, :], gain("g_mix_pre"))
            a.wait_ge(sem("xr_padded"), 1)
            for j in range(RB):
                copy_out("xr", j, xrT[:, j, 2:2 + S], chunk=j, width=S)
            for j in range(RB):
                copy_out("yg", j, ygT[:, j, :], chunk=j, width=S, func=ACT.Gelu_apprx_tanh)

            recA, recB = nat[:, 0, :], nat[:, 1, :]
            recU, recH = aux[:, 0, :], aux[:, 1, :]
            a.wait_ge(sem("n1_turned"), KD)

            def gate_out(z):
                if z:
                    a.wait_ge(sem("rec_scan"), 1)
                for b in range(RB):
                    n = z * RB + b
                    a.wait_ge(sem("gates"), n + 1)
                    steps.mark(a.activation(recA[:, b * S:(b + 1) * S], bank[4 + n % 4][:, 0:S], ACT.Sigmoid,
                                            bias=cols[:, COLS["b_rg_a"] + n:COLS["b_rg_a"] + n + 1]))
                    a.activation(recU[:, b * S:(b + 1) * S], bank[4 + n % 4][:, S:2 * S], ACT.Sigmoid,
                                 bias=cols[:, COLS["b_rg_i"] + n:COLS["b_rg_i"] + n + 1]).then_inc(
                        sem("gates_taken"), 1)
                steps.wait()
                if z == 0:
                    a.wait_ge(sem("softplus_in"), 2)
                for b in range(RB):
                    n = z * RB + b
                    i = a.activation(recA[:, b * S:(b + 1) * S], recA[:, b * S:(b + 1) * S], ACT.Tanh,
                                     scale=sp[:, 3, n:n + 1])
                    if b == RB - 1:
                        i.then_inc(sem("gates_ready"), 1)
                    else:
                        steps.mark(i)

            def rec_root(z):
                a.wait_ge(sem("rec_b2"), z + 1)
                a.activation(recB, recB, ACT.Sqrt, scale=-1.0).then_inc(sem("rec_root"), 1)

            gate_out(0)
            for j in range(RB):
                copy_out("q", j, qkT[:, j, :], chunk=j, width=S)
            rec_root(0)
            gate_out(1)
            for j in range(RB):
                copy_out("k", j, qkT[:, NH + j, :], chunk=j, width=S)
            rec_root(1)
            for c in range(2):
                for t in range(T):
                    copy_out("v", 2 * c + t, v1n[:, t, c * BAND:(c + 1) * BAND], chunk=4 * c + 3)
            attention_act(a, "at1", scratch1)
            root(2)
            turn_out(nc.scalar, "n2", 8, lambda k: xT[:, k, :], gain("g_attn_out"))
            a.wait_ge(sem("rec_sum"), 1)
            a.activation(recA, recH, ACT.Square).then_inc(sem("rec_sq"), 1)
            a.wait_ge(sem("rec_norm"), 2)
            a.activation(conv_tmp[:, 0, :], conv_tmp[:, 0, :], ACT.Sqrt).then_inc(sem("rec_norm"), 1)

            def panels(phase, n, squares=True, func=ACT.Copy, dst=None):
                dst = nat if dst is None else dst
                with loop(a, 2) as it:
                    for c in range(2):
                        for t in range(T):
                            wait_multiplied(a, phase, 4 * c + 3, it, 8)
                            ps = out_bank(phase, 2 * c + t)
                            i = a.activation(dst[:, t, bass.ds(c * BAND + it * 2 * BAND, BAND)], ps[:, :], func)
                            if squares:
                                a.wait_ge(taken, out_no(phase, 2 * c + t) + 4 * it)
                                a.activation(silu_junk, ps[:, :], ACT.Square,
                                             accum_out=ssq[:, t, bass.ds(c + it * 2, 1)]).then_inc(taken, 1)
                            else:
                                i.then_inc(taken, 1)

            silu_junk = bank[6][:, :]

            def resid_squares(n0):
                for t in range(T):
                    for c in range(4):
                        a.wait_ge(sem("resid_piece"), n0 + t * 4 + c + 1)
                        if n0 + t + c:
                            a.wait_ge(sem("ssq_in"), n0 + t * 4 + c)
                        i = a.activation(bank[6][:, :], resid[:, t, c * BAND:(c + 1) * BAND], ACT.Square,
                                         accum_out=ssq[:, t, c:c + 1])
                        i.then_inc(sem("ssq_in"), 1)

            a.activation(cact[:, :], cols[:, COLS["c"]:COLS["c"] + KD], ACT.Silu).then_inc(sem("cact_ready"), 1)
            panels("wout", 0)
            root(3)
            resid_squares(0)
            root(4)
            turn_out(nc.scalar, "n3", KD, lambda k: xT[:, k, :], gain("g_ffn_pre"))
            with loop(a, KF // 4) as it:
                for j in range(4):
                    wait_multiplied(a, "gateup", 2 * j, it, 8)
                    a.wait_ge(taken, out_no("gateup", 0) + 2 * (j - 1) + it * 8)
                    a.activation(silu_g[:, j % 2, :], out_bank("gateup", 2 * j)[:, 0:S], ACT.Silu).then_inc(
                        sem("silu_done"), 1)

            for c in range(4):
                for t in range(T):
                    wait_multiplied(a, "down", 4 * c + 3)
                    ps = out_bank("down", 2 * c + t)
                    a.activation(nat[:, t, c * BAND:(c + 1) * BAND], ps[:, :], ACT.Copy)
                    a.wait_ge(taken, out_no("down", 2 * c + t))
                    a.activation(silu_junk, ps[:, :], ACT.Square, accum_out=ssq[:, t, c:c + 1]).then_inc(taken, 1)
            for c in range(4):
                for t in range(T):
                    i = copy_out("pproj", 2 * c + t, ple[:, t, c * BAND:(c + 1) * BAND], chunk=c // 2)
            root(5)
            resid_squares(8)
            root(6)
            turn_out(nc.scalar, "n4", KD, lambda k: xT[:, k, :], gain("g_ple_pre"))
            with loop(a, 2) as it:
                for c in range(2):
                    for t in range(T):
                        wait_multiplied(a, "pgate", 4 * c + 3, it, 8)
                        a.activation(nat[:, t, bass.ds(c * BAND + it * 2 * BAND, BAND)],
                                     out_bank("pgate", 2 * c + t)[:, :], ACT.Sigmoid).then_inc(taken, 1)
            for t in range(T):
                a.wait_ge(sem("pgate_sig"), t + 1)
                for c in range(4):
                    if t + c:
                        a.wait_ge(sem("ple_ready"), 4 * t + c)
                    a.activation(bank[6][:, :], nat[:, t, c * BAND:(c + 1) * BAND], ACT.Square,
                                 accum_out=ssq[:, t, c:c + 1]).then_inc(sem("ple_ready"), 1)
            root(7)

            root(8)
            a.wait_ge(sem("modc_ready"), 1)
            turn_out(nc.scalar, "n5", KD, lambda k: xT[:, k, :], lambda k: modc[:, 0, k:k + 1],
                     lambda k: modc[:, 1, k:k + 1])
            for c in range(2):
                for t in range(T):
                    wait_multiplied(a, "lat", 4 * c + 3)
                    ps = out_bank("lat", 2 * c + t)
                    a.activation(lat[:, t, c * LAT:(c + 1) * LAT], ps[:, :], ACT.Copy)
                    a.wait_ge(taken, out_no("lat", 2 * c + t))
                    a.activation(silu_junk, ps[:, :], ACT.Square, accum_out=ssq[:, t, c:c + 1]).then_inc(taken, 1)
            for t in range(T):
                copy_out("kr", t, rot[:, t, 8 * 64:9 * 64], chunk=0, width=64)
            a.wait_ge(sem("rms_in"), 9)
            a.activation(st[:, 8:12], st[:, 4:8], ACT.Sqrt).then_inc(sem("root_out"), 1)
            with loop(a, 2) as it:
                for c in range(2):
                    for t in range(T):
                        wait_multiplied(a, "qk2", 4 * c + 3, it, 8)
                        a.activation(qkv2[:, t, bass.ds(c * BAND + it * 2 * BAND, BAND)],
                                     out_bank("qk2", 2 * c + t)[:, :], ACT.Copy).then_inc(taken, 1)
            turn_out(nc.scalar, "n6", 2 * KL, lambda k: latT[:, k, :], gain("g_q_lat"))
            for c in range(2):
                for t in range(T):
                    copy_out("v2", 2 * c + t, qkv2[:, t, 2 * DA + c * BAND:2 * DA + (c + 1) * BAND], chunk=4 * c + 3)
            turn_out(nc.scalar, "tq", 2 * NH, lambda k: natT[:, k, :])
            a.wait_ge(sem("rope_done"), 1)
            for h in range(NH):
                copy_out("mla", h, aux[:, 0, h * S:(h + 1) * S], chunk=h // 4, width=S)
            for t in range(T):
                copy_out("mla", 8 + t, rot[:, t, 0:512], chunk=2)
            for h in range(NH):
                copy_out("mla", 10 + h, aux[:, 1, h * S:(h + 1) * S], chunk=3 + h // 4, width=S)
            for c in range(2):
                for t in range(T):
                    copy_out("mla", 18 + 2 * c + t, v2n[:, t, c * BAND:(c + 1) * BAND], chunk=5 + c)
            turn_out(nc.scalar, "tr", 9, lambda k: rotT[0:64, k, :], width=64)
            attention_act(a, "at2", scratch2)
            a.wait_ge(sem("at2_out"), NH)
            attention_act(a, "at3", scratch2)
            a.wait_ge(sem("rms_in"), 10)
            a.activation(st[:, 8:12], st[:, 4:8], ACT.Sqrt).then_inc(sem("root_out"), 1)
            turn_out(nc.scalar, "n7", KD, lambda k: natT[:, k, :], gain("g_out_a"))
            wait_turned_out(a, "n7", KD)
            with loop(a, 2) as it:
                for c in range(2):
                    for t in range(T):
                        wait_multiplied(a, "wo", 4 * c + 3, it, 8)
                        a.activation(o2[:, t, bass.ds(c * BAND + it * 2 * BAND, BAND)],
                                     out_bank("wo", 2 * c + t)[:, :], ACT.Copy).then_inc(taken, 1)
            root(11)
            root(12)
            turn_out(nc.scalar, "n8", KD, lambda k: xT[:, k, :])
            with loop(a, 2) as it:
                for j in range(8):
                    wait_multiplied(a, "pq", j, it, 8)
                    if j >= 2:
                        a.wait_ge(sem("scores"), it * 8 + j - 1)
                    else:
                        a.wait_ge(sem("scores"), it * 8)
                    a.activation(qb[:, j % 2, :], out_bank("pq", j)[:, 0:S], ACT.Copy).then_inc(taken, 1)
                a.wait_ge(sem("topk_exp_in"), it + 1)
                a.activation(tk_val.rearrange("p t h k -> p (t h k)"),
                             tk_abf[:, 0].rearrange("p t h k -> p (t h k)"), ACT.Exp).then_inc(sem("topk_exp_out"), 1)
            for t in range(T):
                a.wait_ge(sem("w_in"), t + 1)
                a.activation(dots[:, t, :], dots[:, t, :], ACT.Gelu).then_inc(sem("w_out_"), 1)
            for t in range(T):
                root(13 + t)

        @block.vector
        def _(v):
            steps = Steps(v, "dve_step")
            link, mark, wait = steps.link, steps.mark, steps.wait
            rms_n = [0]

            def roots(count, eps, n=2, src=0, dst=16, parts=None):
                rms_n[0] += 1
                v.tensor_scalar(st[:, src:src + n], st[:, src:src + n], 1.0 / count, eps, ALU.mult, ALU.add)\
                    .then_inc(sem("rms_in"), 1)
                v.wait_ge(sem("root_out"), rms_n[0])
                got = st[:, 2:4] if n == 2 else st[:, 8:12]
                link(v.reciprocal(st[:, dst:dst + n], got))

            v.memset(ones[:, :], 1.0).then_inc(sem("ones_set"), 1)
            mark(v.memset(xrT[:, :, 0:2], 0.0))
            v.memset(xrT[:, :, 2 + S:XP], 0.0).then_inc(sem("xr_padded"), 1)
            v.wait_ge(sem("cols_in"), 16)
            lam = cols[:, COLS["lam"]:COLS["lam"] + 2 * RB]
            link(v.tensor_scalar(sp[:, 0, :], lam, -1.0, None, ALU.mult))
            v.tensor_tensor(sp[:, 0, :], sp[:, 0, :], lam, ALU.max).then_inc(sem("softplus_in"), 1)
            v.wait_ge(sem("x_in"), 16 * T)
            for t in range(T):
                mark(v.tensor_tensor_reduce(nat[:, t, :], resid[:, t, :], resid[:, t, :], 1.0, 0.0, ALU.mult, ALU.add,
                                            st[:, t:t + 1]))
            wait()
            roots(D, EPS)
            mark(v.tensor_scalar(nat[:, 0, :], resid[:, 0, :], st[:, 16:17], None, ALU.mult))
            wait()
            v.tensor_scalar(nat[:, 1, :], resid[:, 1, :], st[:, 17:18], None, ALU.mult).then_inc(sem("hn_ready"), 1)
            v.wait_ge(sem("softplus_exp"), 1)
            link(v.tensor_scalar(sp[:, 2, :], sp[:, 1, :], 2.0, None, ALU.add))
            link(v.reciprocal(sp[:, 2, :], sp[:, 2, :]))
            link(v.tensor_tensor(sp[:, 1, :], sp[:, 1, :], sp[:, 2, :], ALU.mult))
            link(v.tensor_tensor(sp[:, 2, :], sp[:, 1, :], sp[:, 1, :], ALU.mult))
            link(v.tensor_scalar(sp[:, 3, :], sp[:, 2, :], 1.0 / 17, 1.0 / 15, ALU.mult, ALU.add))
            for m in (13, 11, 9, 7, 5, 3, 1):
                link(v.tensor_tensor(sp[:, 3, :], sp[:, 3, :], sp[:, 2, :], ALU.mult))
                link(v.tensor_scalar(sp[:, 3, :], sp[:, 3, :], 1.0 / m, None, ALU.add))
            link(v.tensor_tensor(sp[:, 3, :], sp[:, 3, :], sp[:, 1, :], ALU.mult))
            link(v.tensor_scalar(sp[:, 3, :], sp[:, 3, :], 8.0, None, ALU.mult))
            link(v.tensor_scalar(sp[:, 0, :], lam, -4.0, 0.0, ALU.mult, ALU.max))
            v.tensor_tensor(sp[:, 3, :], sp[:, 3, :], sp[:, 0, :], ALU.add).then_inc(sem("softplus_in"), 1)
            turn_out(nc.vector, "n1", KD, lambda k: xT[:, k, :], gain("g_mix_pre"))

            cw = lambda j, b: cols[:, COLS["conv_w"] + j * RB + b:COLS["conv_w"] + j * RB + b + 1]
            v.wait_ge(sem("xr_padded"), 1)
            for b in range(RB):
                v.wait_ge(taken, out_no("xr", b) + 1)
                tmp = conv_tmp[:, b % 2, :]
                link(v.tensor_scalar(tmp, xrT[:, b, 0:S], cw(0, b), cols[:, COLS["conv_b"] + b:COLS["conv_b"] + b + 1],
                                     ALU.mult, ALU.add))
                for j in (1, 2):
                    link(v.scalar_tensor_tensor(out=tmp, in0=xrT[:, b, j:j + S], scalar=cw(j, b), in1=tmp,
                                                op0=ALU.mult, op1=ALU.add))
                v.scalar_tensor_tensor(out=xcT[:, b, :], in0=xrT[:, b, 3:3 + S], scalar=cw(3, b), in1=tmp,
                                       op0=ALU.mult, op1=ALU.add).then_inc(sem("conv_done"), 1)
                v.wait_ge(sem("conv_done"), b + 1)

            recA, recB = nat[:, 0, :], nat[:, 1, :]
            recU, recH = aux[:, 0, :], aux[:, 1, :]
            xc2 = xcT.rearrange("p b s -> p (b s)")

            def rec_gates(z):
                v.wait_ge(sem("gates_ready"), z + 1)
                link(v.tensor_scalar(recB, recA, 1.0, None, ALU.add))
                link(v.reciprocal(recB, recB))
                link(v.scalar_tensor_tensor(out=recA, in0=recA, scalar=2.0, in1=recB, op0=ALU.mult, op1=ALU.mult))
                v.scalar_tensor_tensor(out=recB, in0=recA, scalar=-2.0, in1=recA, op0=ALU.add, op1=ALU.mult)\
                    .then_inc(sem("rec_b2"), 1)
                v.wait_ge(sem("rec_b2"), z + 1)
                link(v.tensor_scalar(recA, recA, -1.0, 1.0, ALU.mult, ALU.add))
                link(v.tensor_tensor(recU, recU, xc2, ALU.mult))
                first = 0 if z == 0 else S - 1
                link(v.memset(recA.rearrange("p (b s) -> p b s", b=RB)[:, :, first:first + 1], 0.0))

            def rec_scan(z):
                v.wait_ge(sem("rec_root"), z + 1)
                link(v.tensor_tensor(recB, recB, recU, ALU.mult))
                if z == 0:
                    v.tensor_tensor_scan(recH, recA, recB, 0.0, ALU.mult, ALU.add).then_inc(sem("rec_scan"), 1)
                else:
                    v.tensor_tensor_scan(recU[:, ::-1], recA[:, ::-1], recB[:, ::-1], 0.0, ALU.mult, ALU.add)\
                        .then_inc(sem("rec_scan"), 1)
                v.wait_ge(sem("rec_scan"), z + 1)

            rec_gates(0)
            rec_scan(0)
            rec_gates(1)
            rec_scan(1)
            link(v.tensor_tensor(recH, recH, recU, ALU.add))
            v.wait_ge(taken, out_no("q", 0))
            v.tensor_tensor(recH, recH, ygT.rearrange("p b s -> p (b s)"), ALU.mult).then_inc(sem("rec_sum"), 1)
            v.wait_ge(sem("rec_sum"), 1)

            v.wait_ge(sem("bias_masked"), 4)

            def bias_1(h, t):
                at = 2 - 2 * t
                return bias1[:, h, at:at + 4, ::-1]

            attention_dve(v, steps, "at1", bias_1, float(HD) ** -0.5,
                          lambda h, t: attn1[:, t, h * HD:(h + 1) * HD], scratch1)
            for t in range(T):
                link(v.tensor_tensor_reduce(recB.rearrange("p (a c) -> p a c", a=2)[:, 0, :], attn1[:, t, :],
                                            attn1[:, t, :], 1.0, 0.0, ALU.mult, ALU.add, st[:, t:t + 1]))
            roots(DA, EPS)
            for t in range(T):
                i = v.tensor_scalar(attn1[:, t, :], attn1[:, t, :], st[:, 16 + t:17 + t], None, ALU.mult)
                if t == 0:
                    link(i)
            i.then_inc(sem("attn1_ready"), 1)
            turn_out(nc.vector, "n2", 8, lambda k: xT[:, k, :], gain("g_attn_out"))
            v.wait_ge(sem("rec_norm"), 1)
            v.tensor_scalar(conv_tmp[:, 0, :], bank[4][:, 0:S], 1.0 / DA, EPS, ALU.mult, ALU.add).then_inc(
                sem("rec_norm"), 1)
            v.wait_ge(sem("rec_norm"), 3)
            link(v.reciprocal(conv_tmp[:, 1, :], conv_tmp[:, 0, :]))
            for b in range(RB):
                v.scalar_tensor_tensor(out=xT[:, 8 + b, :], in0=recH[:, b * S:(b + 1) * S], scalar=gain("g_rec_out")(b),
                                       in1=conv_tmp[:, 1, :], op0=ALU.mult, op1=ALU.mult).then_inc(
                    sem("rec_normed"), 1)
            v.wait_ge(sem("rec_normed"), RB)
            v.memset(mxs[:, 0, 0:1], 0.0).then_inc(sem("ada_used"), ADA_SLOTS)
            v.wait_ge(sem("ada_used"), ADA_SLOTS)
            v.memset(mxs[:, 0, 0:1], 0.0).then_inc(sem("aux_free"), 1)

            def sum_ssq():
                link(v.tensor_reduce(st[:, 0:2], ssq[:, :, :], AXX, ALU.add))

            def add_normed(row, n0):
                for t in range(T):
                    for c in range(4):
                        s = slice(c * BAND, (c + 1) * BAND)
                        link(v.scalar_tensor_tensor(out=nat[:, t, s], in0=nat[:, t, s], scalar=st[:, 16 + t:17 + t],
                                                    in1=row[:, s], op0=ALU.mult, op1=ALU.mult))
                        v.tensor_tensor(resid[:, t, s], resid[:, t, s], nat[:, t, s], ALU.add).then_inc(
                            sem("resid_piece"), 1)
                v.wait_ge(sem("resid_piece"), n0 + 8)

            def normed(n, name, g):
                v.wait_ge(sem("ssq_in"), n)
                sum_ssq()
                roots(D, EPS)
                link(v.tensor_scalar(nat[:, 0, :], resid[:, 0, :], st[:, 16:17], None, ALU.mult))
                v.tensor_scalar(nat[:, 1, :], resid[:, 1, :], st[:, 17:18], None, ALU.mult).then_inc(sem("hn_ready"), 1)
                turn_out(nc.vector, name, KD, lambda k: xT[:, k, :], gain(g))

            v.wait_ge(taken, out_no("gateup", 0))
            sum_ssq()
            roots(D, EPS)
            v.wait_ge(sem("row_in"), 16)
            add_normed(aux[:, 0, :], 0)
            normed(8, "n3", "g_ffn_pre")
            wait()

            v.wait_ge(sem("cact_ready"), 1)

            def hidden(j, it):
                v.wait_ge(sem("silu_done"), it * 4 + j + 1)
                wait_multiplied(v, "gateup", 2 * j + 1, it, 8)
                v.tensor_tensor(big[:, bass.ds(j * S + it * 4 * S, S)], out_bank("gateup", 2 * j + 1)[:, 0:S],
                                silu_g[:, j % 2, :], ALU.mult).then_inc(taken, 2)

            def ada(k, g):
                s = k % ADA_SLOTS
                v.wait_ge(ada_loaded[s], 16 * (KD // ADA_SLOTS) * g + 16 * (k // ADA_SLOTS + 1))
                if k == 0:
                    i = v.tensor_scalar(ada_acc, ada_ring[:, s, :], cact[:, k:k + 1], None, ALU.mult)
                else:
                    v.wait_ge(sem("ada_used"), ADA_SLOTS + KD * g + k)
                    i = v.scalar_tensor_tensor(out=ada_acc, in0=ada_ring[:, s, :], scalar=cact[:, k:k + 1],
                                               in1=ada_acc, op0=ALU.mult, op1=ALU.add)
                i.then_inc(sem("ada_used"), 1)

            def ada_end(g):
                v.wait_ge(sem("ada_used"), ADA_SLOTS + KD * g + KD)
                v.memset(mxs[:, 0, 1:2], 0.0).then_inc(sem("ada_sum"), 1)

            def ada_row(g):
                v.wait_ge(sem("ada_rowsum"), g + 1)
                v.wait_ge(sem("mod_b_in"), 16 * g + 16)
                for c in range(2):
                    i = v.tensor_tensor(mod_row[0:1, c * BAND:(c + 1) * BAND], bank[4 + c][0:1, :],
                                        mod_row[0:1, c * BAND:(c + 1) * BAND], ALU.add)
                    if c == 0:
                        mark(i)
                    else:
                        i.then_inc(sem("mod_ready"), 1)
                wait()

            wait_turned_out(v, "n3", KD)
            with steps.loop(KF // 4, 1) as it:
                for j in range(4):
                    hidden(j, it)
                    for k in range(4 * j, 4 * j + 4):
                        ada(k, it)
                ada_end(it)
                ada_row(it)
            for k in range(KD):
                ada(k, ADA_G - 1)
            ada_end(ADA_G - 1)
            ada_row(ADA_G - 1)

            v.wait_ge(taken, out_no("pproj", 0))
            sum_ssq()
            roots(D, EPS)
            v.wait_ge(sem("row2_in"), 16)
            add_normed(aux[:, 1, :], 8)
            v.memset(mxs[:, 0, 0:1], 0.0).then_inc(row_used, 1)
            normed(16, "n4", "g_ple_pre")
            v.wait_ge(taken, out_no("lat", 0))
            for t in range(T):
                v.tensor_tensor(nat[:, t, :], nat[:, t, :], ple[:, t, :], ALU.mult).then_inc(sem("pgate_sig"), 1)
            v.wait_ge(sem("ple_ready"), 4 * T)
            sum_ssq()
            roots(D, EPS)
            v.wait_ge(sem("row3_in"), 16)
            add_normed(aux[:, 0, :], 16)

            def layer_stats(n, t0=0, tn=T):
                for t in range(t0, tn):
                    for c in range(4):
                        mark(v.bn_stats(stats[:, t, c, :], resid[:, t, c * BAND:(c + 1) * BAND]))
                wait()
                for t in range(t0, tn):
                    mark(v.bn_aggr(mv[:, t, :], stats[:, t, :, :].rearrange("p c s -> p (c s)")))
                wait()
                rms_n[0] += 1
                if tn - t0 == T:
                    v.tensor_scalar(st[:, 0:2], mv[:, :, 1:2].rearrange("p t o -> p (t o)"), EPS_LN, None, ALU.add)\
                        .then_inc(sem("rms_in"), 1)
                else:
                    v.tensor_scalar(st[:, 0:2], mv[:, :, 1:2].rearrange("p t o -> p (t o)"), EPS_LN, None, ALU.add)\
                        .then_inc(sem("rms_in"), 1)
                v.wait_ge(sem("root_out"), rms_n[0])
                link(v.reciprocal(st[:, 16:18], st[:, 2:4]))

            def layer_normed(dst, t):
                return v.tensor_scalar(dst[:, t, :], resid[:, t, :], mv[:, t, 0:1], st[:, 16 + t:17 + t],
                                       ALU.subtract, ALU.mult)

            v.wait_ge(sem("modc_in"), 32)
            v.tensor_scalar(modc[:, 0, :], modc[:, 0, :], 1.0, None, ALU.add).then_inc(sem("modc_ready"), 1)
            layer_stats(0)
            link(layer_normed(nat, 0))
            layer_normed(nat, 1).then_inc(sem("hn_ready"), 1)
            v.wait_ge(sem("modc_ready"), 1)
            turn_out(nc.vector, "n5", KD, lambda k: xT[:, k, :], lambda k: modc[:, 0, k:k + 1],
                     lambda k: modc[:, 1, k:k + 1])
            v.wait_ge(taken, out_no("kr", 0))
            link(v.tensor_copy(st[:, 4:8].rearrange("p (t c) -> p t c", t=T), ssq[:, :, 0:2]))
            rms_n[0] += 1
            v.tensor_scalar(st[:, 4:8], st[:, 4:8], 1.0 / LAT, EPS, ALU.mult, ALU.add).then_inc(sem("rms_in"), 1)
            v.wait_ge(sem("root_out"), rms_n[0])
            link(v.reciprocal(st[:, 20:24], st[:, 8:12]))
            for t in range(T):
                for c in range(2):
                    i = v.tensor_scalar(lat[:, t, c * LAT:(c + 1) * LAT], lat[:, t, c * LAT:(c + 1) * LAT],
                                        st[:, 20 + 2 * t + c:21 + 2 * t + c], None, ALU.mult)
                    if t == T - 1 and c == 1:
                        i.then_inc(sem("lat_ready"), 1)
                    else:
                        link(i)

            def rope(view, heads, half, tab, scr):
                n = heads * half
                for t in range(T):
                    x = view(t)
                    x1, x2 = x[:, :, 0:half], x[:, :, half:2 * half]
                    cos = rope_t[:, t, tab:tab + half].unsqueeze(1).to_broadcast([P, heads, half])
                    sin = rope_t[:, t, tab + half:tab + 2 * half].unsqueeze(1).to_broadcast([P, heads, half])
                    w = [scr[:, i * 288:i * 288 + n].rearrange("p (h c) -> p h c", h=heads) for i in range(4)]
                    for dst, p, q in ((w[0], x1, cos), (w[1], x2, sin), (w[2], x2, cos), (w[3], x1, sin)):
                        mark(v.tensor_tensor(dst, p, q, ALU.mult))
                    wait()
                    mark(v.tensor_tensor(x1, w[0], w[1], ALU.subtract))
                    mark(v.tensor_tensor(x2, w[2], w[3], ALU.add))
                    wait()

            turn_out(nc.vector, "n6", 2 * KL, lambda k: latT[:, k, :], gain("g_q_lat"))
            v.wait_ge(taken, out_no("v2", 0))
            rope(lambda t: qkv2[:, t, 0:2 * DA].rearrange("p (h c) -> p h c", h=2 * NH), 2 * NH, ROT_A, 0, auxf)
            v.memset(mxs[:, 0, 0:1], 0.0).then_inc(sem("rope_done"), 1)
            turn_out(nc.vector, "tq", 2 * NH, lambda k: natT[:, k, :])
            v.wait_ge(taken, out_no("mla", 10))
            rope(lambda t: rot[:, t, :].rearrange("p (h c) -> p h c", h=9), 9, ROT_B, 2 * ROT_A,
                 xT[:, :, :].rearrange("p k s -> p (k s)"))
            v.memset(mxs[:, 0, 0:1], 0.0).then_inc(sem("rotq_ready"), 1)
            turn_out(nc.vector, "tr", 9, lambda k: rotT[0:64, k, :], width=64)
            v.wait_ge(sem("misc_in"), 16)
            attention_dve(v, steps, "at2", lambda h, t: by_row(masks[:, 0, t, :]), float(HD) ** -0.5,
                          lambda h, t: o2[:, t, h * HD:(h + 1) * HD], scratch2)
            attention_dve(v, steps, "at3", lambda h, t: by_row(masks[:, 1, t, :]), float(HD + 64) ** -0.5,
                          lambda h, t: o2[:, t, DA + h * HD:DA + (h + 1) * HD], scratch2)
            for t in range(T):
                for c in range(2):
                    link(v.tensor_tensor_reduce(auxf[:, 0:DA], o2[:, t, c * DA:(c + 1) * DA],
                                                o2[:, t, c * DA:(c + 1) * DA], 1.0, 0.0, ALU.mult, ALU.add,
                                                st[:, 4 + 2 * t + c:5 + 2 * t + c]))
            rms_n[0] += 1
            v.tensor_scalar(st[:, 4:8], st[:, 4:8], 1.0 / DA, EPS, ALU.mult, ALU.add).then_inc(sem("rms_in"), 1)
            v.wait_ge(sem("root_out"), rms_n[0])
            link(v.reciprocal(st[:, 20:24], st[:, 8:12]))
            for t in range(T):
                for c in range(2):
                    link(v.tensor_scalar(o2[:, t, c * DA:(c + 1) * DA], o2[:, t, c * DA:(c + 1) * DA],
                                         st[:, 20 + 2 * t + c:21 + 2 * t + c], None, ALU.mult))
            v.memset(mxs[:, 0, 0:1], 0.0).then_inc(sem("o_ready"), 1)
            turn_out(nc.vector, "n7", KD, lambda k: natT[:, k, :], gain("g_out_a"))

            v.wait_ge(taken, out_no("pq", 0))
            v.wait_ge(sem("rows_in"), 16 * 5)

            def deep_norm(t, mix, r):
                link(v.tensor_tensor(mix, mix, r[:, 0, :], ALU.mult))
                link(v.scalar_tensor_tensor(out=resid[:, t, :], in0=resid[:, t, :], scalar=ALPHA, in1=mix,
                                            op0=ALU.mult, op1=ALU.add))

            def scaled(t, r):
                link(layer_normed(resid, t))
                link(v.tensor_tensor(resid[:, t, :], resid[:, t, :], r[:, 1, :], ALU.mult))
                return v.tensor_tensor(resid[:, t, :], resid[:, t, :], r[:, 2, :], ALU.add)

            for t in range(T):
                deep_norm(t, o2[:, t, :], rows)
            layer_stats(1)
            for t in range(T):
                link(scaled(t, rows))
            layer_stats(2)
            for t in range(T):
                link(layer_normed(nat, t))
                link(v.scalar_tensor_tensor(out=nat[:, t, :], in0=rows[:, 3, :], scalar=1.0, in1=nat[:, t, :],
                                            op0=ALU.add, op1=ALU.mult))
                link(v.tensor_tensor(nat[:, t, :], nat[:, t, :], rows[:, 4, :], ALU.add))
            v.memset(mxs[:, 0, 0:1], 0.0).then_inc(sem("h2_ready"), 1)
            turn_out(nc.vector, "n8", KD, lambda k: xT[:, k, :])

            def top16(vals, idxs, src, tmp):
                link(v.max(vals[:, 0:8], src))
                link(v.max_index(idxs[:, 0:8], vals[:, 0:8], src))
                link(v.match_replace(out=tmp, in_to_replace=vals[:, 0:8], in_values=src, imm_value=-3.0e38))
                link(v.max(vals[:, 8:16], tmp))
                return v.max_index(idxs[:, 8:16], vals[:, 8:16], tmp)

            v.wait_ge(sem("iota_done"), 1)
            for it in range(2):
                for j in range(8):
                    v.wait_ge(sem("scores"), it * 8 + j + 1)
                    for t in range(T):
                        i = top16(tk_v12[:, t, j // 2, j % 2, :], tk_i12[:, t, j // 2, j % 2, :],
                                  bank[4 + j % 2][:, t * P:(t + 1) * P], tk_tmp[:, 0:P])
                        if t == T - 1:
                            i.then_inc(sem("scores_taken"), 1)
                            v.wait_ge(sem("scores_taken"), it * 8 + j + 1)
                        else:
                            link(i)
                link(v.tensor_copy(auxf[:, 512:768], auxf[:, 256:512].bitcast(U32)))
                for t in range(T):
                    link(v.tensor_tensor(tk_cand, tk_v12[:, t, :, 0, :].unsqueeze(3).to_broadcast([P, 4, 16, 16]),
                                         tk_v12[:, t, :, 1, :].unsqueeze(2).to_broadcast([P, 4, 16, 16]), ALU.add))
                    for h in range(4):
                        link(top16(tk_val[:, t, h, :], tk_ci[:, t, h, :],
                                   tk_cand[:, h].rearrange("p i j -> p (i j)"), tk_tmp))
                ci = tk_ci.rearrange("p t h k -> p (t h k)")
                link(v.tensor_scalar(tk_ab[:, 0, :], ci, 4, None, ALU.logical_shift_right))
                link(v.tensor_scalar(tk_ab[:, 1, :], ci, 15, None, ALU.bitwise_and))
                link(v.tensor_copy(auxf[:, 2560:2816], auxf[:, 2304:2560].bitcast(U32)))
                for t in range(T):
                    for a_ in range(2):
                        link(v.tensor_tensor(tk_hot, tk_abf[:, a_, t].rearrange("p h k -> p (h k)").unsqueeze(2)
                                             .to_broadcast([P, 64, 16]),
                                             iota16.unsqueeze(1).to_broadcast([P, 64, 16]), ALU.is_equal))
                        hot4 = tk_hot.rearrange("p (h o) k -> p h o k", h=4)
                        link(v.tensor_tensor(hot4, hot4, tk_f12[:, t, :, a_, :].unsqueeze(2)
                                             .to_broadcast([P, 4, 16, 16]), ALU.mult))
                        link(v.tensor_reduce(tk_pick[:, a_, :], tk_hot, AXX, ALU.add))
                    link(v.scalar_tensor_tensor(out=tk_pick[:, 0, :], in0=tk_pick[:, 0, :], scalar=float(NKEY),
                                                in1=tk_pick[:, 1, :], op0=ALU.mult, op1=ALU.add))
                    link(v.tensor_copy(gidx[:, t, it * 64:it * 64 + 64], tk_pick[:, 0, :]))
                val8 = tk_val.rearrange("p t h k -> p (t h) k")
                v.tensor_tensor(tk_abf[:, 0].rearrange("p t h k -> p (t h) k"), val8,
                                val8[:, :, 0:1].to_broadcast([P, T * 4, 16]), ALU.subtract).then_inc(
                    sem("topk_exp_in"), 1)
                v.wait_ge(sem("topk_exp_out"), it + 1)
                link(v.tensor_reduce(tk_sum[:, 0:8], val8, AXX, ALU.add))
                link(v.reciprocal(tk_sum[:, 8:16], tk_sum[:, 0:8]))
                link(v.tensor_tensor(val8, val8, tk_sum[:, 8:16].unsqueeze(2).to_broadcast([P, 8, 16]), ALU.mult))
                link(v.tensor_copy(gwt[:, :, it * 64:it * 64 + 64], tk_val.rearrange("p t h k -> p t (h k)")))
            v.memset(mxs[:, 0, 0:1], 0.0).then_inc(sem("chosen"), 1)

            v.wait_ge(sem("chosen"), 1)
            v.memset(mxs[:, 0, 0:1], 0.0).then_inc(sem("v_done"), SLOTS)
            v.wait_ge(sem("v_done"), SLOTS)
            PASS = NSEL // 16
            for t in range(T):
                with steps.loop(PASS, 1) as it:
                    for hf in range(2):
                        for g in range(8):
                            n = (t * PASS) * 2 + hf
                            v.wait_ge(gath[g], 16 * (n + 1) + 32 * it)
                            v.tensor_tensor_reduce(ring[:, g * CH:(g + 1) * CH], ring[:, g * CH:(g + 1) * CH],
                                                   nat[:, t, :], 1.0, 0.0, ALU.mult, ALU.add,
                                                   dstage[:, 8 * hf + g:8 * hf + g + 1]).then_inc(sem("v_done"), 1)
                    v.wait_ge(sem("v_done"), SLOTS + (t * PASS + 1) * 16 + 16 * it)
                    link(v.tensor_copy(dots[:, t, bass.ds(it * 16, 16)], dstage))
                v.memset(mxs[:, 0, 0:1], 0.0).then_inc(sem("w_in"), 1)
            for t in range(T):
                v.wait_ge(sem("w_out_"), t + 1)
                link(v.tensor_tensor(dots[:, t, :], dots[:, t, :], gwt[:, t, :], ALU.mult))
            acc = o2
            for t in range(T):
                link(v.memset(acc[:, t, :], 0.0))
                with steps.loop(PASS, 0) as it:
                    for hf in range(2):
                        for g in range(8):
                            n = (T + t) * PASS * 2 + hf
                            v.wait_ge(gath[g], 16 * (n + 1) + 32 * it)
                            v.wait_ge(sem("v_done"), SLOTS + ((T + t) * PASS) * 16 + 8 * hf + g + 16 * it)
                            v.scalar_tensor_tensor(out=acc[:, t, :], in0=ring[:, g * CH:(g + 1) * CH],
                                                   scalar=dots[:, t, bass.ds(8 * hf + g + it * 16, 1)],
                                                   in1=acc[:, t, :], op0=ALU.mult, op1=ALU.add).then_inc(
                                sem("v_done"), 1)
                v.wait_ge(sem("v_done"), SLOTS + ((T + t + 1) * PASS) * 16)
                if t == 0:
                    v.wait_ge(sem("rows2_in"), 48)
                deep_norm(t, acc[:, t, :], rows)
                layer_stats(3 + t, t, t + 1)
                scaled(t, rows).then_inc(sem("out_ready"), 1)
                v.wait_ge(sem("out_ready"), t + 1)

        @block.gpsimd
        def _(g_):
            steps = Steps(g_, "pool_step")
            g_.dma_start(cols[:, :], io["cols"]).then_inc(sem("cols_in"), 16)
            g_.dma_start(ident[:, :], io["ident"]).then_inc(sem("consts_in"), 16)
            g_.dma_start(rope_t[:, :, :], io["rope"]).then_inc(sem("consts_in"), 16)
            g_.dma_start(pT[:, :, :], io["pT"]).then_inc(sem("consts_in"), 16)
            g_.dma_start(rg_w.rearrange("p z g b c -> p (z g b c)"), io["rg"]).then_inc(sem("rg_in"), 16)
            rp = io["rpb"]
            NR, NCC = 2 * WIN_R - 1, 2 * WIN_C - 1
            for half in range(2):
                for h in range(NH):
                    src = bass.AP(tensor=rp.tensor,
                                  offset=h * NR * NCC + (WIN_R - ROWS + 1 - half) * NCC + WIN_C - GRID_W,
                                  ap=[[1, GRID_W], [NCC, 6], [1, GRID_W]])
                    g_.dma_start(bias1[GRID_W * half:GRID_W * (half + 1), h], src).then_inc(sem("bias_in"), 16)
            g_.wait_ge(sem("bias_in"), 16 * 2 * NH)
            for half in range(2):
                q = slice(GRID_W * half, GRID_W * (half + 1))
                rest = GRID_W - WIN_C
                lo = bias1[q, :, :, WIN_C:GRID_W].rearrange("p h r c -> p (h r) c")
                hi = bias1[q, :, :, 0:rest].rearrange("p h r c -> p (h r) c")
                g_.affine_select(out=lo, in_=lo, compare_op=ALU.is_ge, fill=-1e9,
                                 base=rest - 1 + WIN_C // 2, pattern=[[0, NH * 6], [-1, rest]], channel_multiplier=-1).then_inc(
                    sem("bias_masked"), 1)
                g_.wait_ge(sem("bias_masked"), 2 * half + 1)
                g_.affine_select(out=hi, in_=hi, compare_op=ALU.is_ge, fill=-1e9,
                                 base=WIN_C // 2 - GRID_W, pattern=[[0, NH * 6], [1, rest]], channel_multiplier=1).then_inc(
                    sem("bias_masked"), 1)
                g_.wait_ge(sem("bias_masked"), 2 * half + 2)

            def row_in(dst, name, s, dram=None):
                src = io["rows"][ROW_NAMES.index(name):ROW_NAMES.index(name) + 1, :] if dram is None else dram
                g_.dma_start(dst, src.to_broadcast([P, D])).then_inc(s, 16)

            g_.wait_ge(sem("aux_free"), 1)
            row_in(aux[:, 0, :], "g_mix_post", sem("row_in"))
            row_in(aux[:, 1, :], "g_ffn_post", sem("row2_in"))

            def mod_piece(g):
                at = bass.ds(g * ADA_W, ADA_W) if not isinstance(g, int) else slice(g * ADA_W, (g + 1) * ADA_W)
                flat = mod_dram.rearrange("(o m) d -> o (m d)", o=1)
                if not isinstance(g, int):
                    g_.wait_ge(sem("mod_out"), 16 * g)
                    g_.nop(nofuse=True)
                g_.dma_start(mod_row[0:1, :], io["b_ada"][:, at]).then_inc(sem("mod_b_in"), 16)
                g_.wait_ge(sem("mod_ready"), g + 1)
                g_.nop(nofuse=True)
                g_.dma_start(flat[:, at], mod_row[0:1, :]).then_inc(sem("mod_out"), 16)

            mod_piece(0)
            with loop(g_, ADA_G - 1) as it:
                mod_piece(it + 1)
            g_.wait_ge(sem("mod_out"), 16 * ADA_G)
            with nc.allow_non_contiguous_dma(reason="two short vectors by channel"):
                for n, m in enumerate((SC1, SH1)):
                    g_.dma_start(modc[:, n, :], mod_dram[m].rearrange("(k p) -> p k", p=P)).then_inc(
                        sem("modc_in"), 16)
            g_.wait_ge(row_used, 1)
            row_in(aux[:, 0, :], "g_ple_post", sem("row3_in"))
            g_.wait_ge(sem("lat_ready"), 1)
            g_.dma_start(masks.rearrange("p m t k -> p (m t k)"), io["masks"]).then_inc(sem("misc_in"), 16)
            g_.wait_ge(sem("at3_out"), NH)
            g_.dma_start(subk.rearrange("p a k -> p (a k)"), io["subk"]).then_inc(sem("sk_in"), 16)
            g_.iota(iota16, [[1, 16]], base=0, channel_multiplier=0, allow_small_or_imprecise_dtypes=True).then_inc(
                sem("iota_done"), 1)
            for n, (name, m) in enumerate(((None, G1), ("ln1_g", 0), ("ln1_b", 0), (None, SC2), (None, SH2))):
                row_in(rows[:, n, :], name, sem("rows_in"), mod_dram[m:m + 1, :] if name is None else None)
            g_.wait_ge(sem("h2_ready"), 1)
            for n, (name, m) in enumerate(((None, G2), ("ln2_g", 0), ("ln2_b", 0))):
                row_in(rows[:, n, :], name, sem("rows2_in"), mod_dram[m:m + 1, :] if name is None else None)

            g_.wait_ge(sem("chosen"), 1)
            g_.wait_ge(multiplied, N_CHUNKS)
            PASS = NSEL // 16
            for table, base in (("u_table", 0), ("v_table", T)):
                for t in range(T):
                    with loop(g_, PASS) as it:
                        first = (base + t) * PASS
                        for hf in range(2):
                            at = bass.ds(it * 16 + 8 * hf, 8)
                            g_.tensor_copy(gstage[:, 8 * hf:8 * hf + 8], gidx[:, t, at]).then_inc(
                                sem("idx_staged"), 1)
                            g_.wait_ge(sem("idx_staged"), 2 * first + hf + 1 + 2 * it)
                            for g in range(8):
                                g_.wait_ge(sem("v_done"), first * 16 + 8 * hf + g + 1 + 16 * it)
                                g_.nop(nofuse=True)
                                g_.indirect_dma_start(
                                    out=ring[:, g * CH:(g + 1) * CH], out_offset=None, in_=io[table],
                                    in_offset=bass.IndirectOffsetOnAxis(
                                        ap=gstage[:, 8 * hf + g:8 * hf + g + 1], axis=0)).then_inc(gath[g], 16)


def arrange(inputs):
    f = {k: np.asarray(v) for k, v in inputs.items()}

    def stationary(w):
        n = w.shape[1] // P
        return w.reshape(KD, P, n, P).transpose(2, 1, 0, 3).reshape(n, P, CH)

    def moving(w, kq=4):
        n = w.shape[1] // BAND
        q = w.shape[0] // (kq * P)
        return w.reshape(q, kq, P, n, BAND).transpose(3, 0, 2, 1, 4).reshape(n * q, P, kq * BAND)

    def stationary_lat(w):
        return w.reshape(KL, P, 2, 4, P).transpose(2, 1, 3, 0, 4).reshape(2, P, CH)

    w_in = f["w_in"][0]
    q, k, v, xr, yg = (w_in[:, i * DA:(i + 1) * DA] for i in range(5))
    gate_up = np.stack([stationary(f["w_ffn_gate"][0]), stationary(f["w_ffn_up"][0])], 1).reshape(-1, P, CH)
    pproj = f["w_ple_proj"][0].reshape(2, P, 2, 2, BAND).transpose(2, 1, 3, 0, 4).reshape(2, P, CH)
    w2 = f["w_in_2"][0]
    qkv2, lat, kr = w2[:, :3 * DA], w2[:, 3 * DA:3 * DA + 2 * LAT], w2[:, 3 * DA + 2 * LAT:]
    kr_chunk = np.zeros((1, P, CH), w2.dtype)
    kr_chunk[0, :, :KD * 64] = kr.reshape(KD, P, 64).transpose(1, 0, 2).reshape(P, KD * 64)
    uq = f["w_uq_2"][0].reshape(LAT, NH, HD + 64)
    parts = [stationary(xr), stationary(yg), stationary(q), stationary(k), moving(v), moving(f["w_out"][0]), gate_up,
             pproj, moving(f["w_ple_gate"][0]), moving(lat), kr_chunk, moving(qkv2[:, :2 * DA]),
             moving(qkv2[:, 2 * DA:]), stationary_lat(uq[:, :, :HD].reshape(LAT, DA)),
             moving(uq[:, :, HD:].reshape(LAT, 512)), stationary_lat(f["w_uk_2"][0]), moving(f["w_uv_2"][0]),
             moving(f["w_o_2"][0]), stationary(f["w_pq_2"][0])]
    a = {"stream": np.concatenate(parts), "down": moving(f["w_ffn_down"][0], 11)}
    vec = {"g_mix_pre": "g_mix_pre", "g_attn_out": "g_attn_out", "g_rec_out": "g_rec_out", "g_ffn_pre": "g_ffn_pre",
           "g_ple_pre": "g_ple_pre", "g_q_lat": "g_q_lat_2", "g_kv_lat": "g_kv_lat_2", "g_out_a": "g_out_a_2",
           "g_out_b": "g_out_b_2", "conv_w": "conv_w", "conv_b": "conv_b", "b_rg_a": "b_rg_a", "b_rg_i": "b_rg_i",
           "lam": "lam", "c": "c_2"}
    a["cols"] = np.ascontiguousarray(np.concatenate([f[vec[n]].reshape(-1, P) for n in COLS], 0).T)
    a["rows"] = np.concatenate([f[n if n in f else n + "_2"].reshape(1, D) for n in ROW_NAMES], 0)
    a["rg"] = np.ascontiguousarray(np.stack([f["w_rg_a"][0], f["w_rg_i"][0]], 1).transpose(3, 0, 1, 2, 4)).reshape(P, -1)
    a["rpb"] = f["rpb"][0][:, :, ::-1]
    a["pT"] = np.ascontiguousarray(f["p"][0, 0].T.reshape(2, P, S).transpose(1, 0, 2))
    a["x"] = f["x"]
    a["w_ada"] = f["w_ada_2"][0]
    a["b_ada"] = f["b_ada_2"]
    a["subk"] = np.ascontiguousarray(np.stack([f["sub_key_1_2"][0].T, f["sub_key_2_2"][0].T], 1)).reshape(P, -1)
    a["u_table"] = f["u_table_2"][0]
    a["v_table"] = f["v_table_2"][0]
    a.update(shape_tables())
    return {k: np.ascontiguousarray(v) for k, v in a.items()}


def shape_tables():
    pos = np.arange(S, dtype=np.float32)
    rope = []
    for half in (ROT_A, ROT_B):
        inv = np.float32(500000.0) ** (-np.arange(half, dtype=np.float32) * np.float32(2.0) / np.float32(2 * half))
        ang = (pos[:, None] * inv[None, :].astype(np.float32)).astype(np.float32)
        rope += [np.cos(ang), np.sin(ang)]
    rope = np.concatenate(rope, 1).astype(np.float32).reshape(T, P, -1).transpose(1, 0, 2)
    dist = np.arange(S)[:, None] - np.arange(S)[None, :]
    count = sum(((dist >= 0) & (dist % dil == 0) & (dist <= window)).astype(np.int64)
                for window, dil in ((128, 1), (512, 4), (2048, 16)))
    log_count = np.where(count > 0, np.log(np.maximum(count, 1)), NEG)
    causal = np.where(dist >= 0, 0.0, NEG)
    masks = np.stack([log_count, causal]).astype(np.float32).reshape(2, T, P, S).transpose(2, 0, 1, 3)
    return {"ident": np.eye(P, dtype=np.float32), "rope": np.ascontiguousarray(rope),
            "masks": np.ascontiguousarray(masks).reshape(P, -1)}


def kernel(**inputs):
    import concourse.bacc as bacc
    from concourse.bass_utils import run_bass_kernel_spmd

    nc = bacc.Bacc("TRN2", target_bir_lowering=False, num_devices=1)
    arrays = {f"in_{n}": a for n, a in arrange(inputs).items()}
    io = {n[3:]: nc.dram_tensor(n, a.shape, mybir.dt.from_np(a.dtype), kind="ExternalInput").ap()
          for n, a in arrays.items()}
    io["out"] = nc.dram_tensor("out", (1, S, D), F32, kind="ExternalOutput").ap()
    build_program(nc, io)
    r = run_bass_kernel_spmd(nc, [arrays], core_ids=[0])
    return r.results[0]["out"]
```

```python
from contextlib import ExitStack, contextmanager

import numpy as np

import concourse.bass as bass
from concourse import mybir

ALU = mybir.AluOpType
ACT = mybir.ActivationFunctionType
AXX = mybir.AxisListType.X
F32 = mybir.dt.float32
F32R = mybir.dt.float32r
I32 = mybir.dt.int32
U32 = mybir.dt.uint32

P = 128
S = 256
T = S // P
D = 2048
KD = D // P
HD = 128
NH = 8
DA = NH * HD
GRID_W, ROWS = 64, S // 64
WIN_R, WIN_C = 8, 16
RB = 8
CONV = 4
FF = 5632
KF = FF // P
EPS, EPS_LN = 1e-6, 1e-5
ALPHA = 2.0 ** 0.25
ROT_A, ROT_B = 16, 32
LAT = 512
KL = LAT // P
NKEY = 128
TOPK = 16
NSEL = NH * TOPK
NEXP = NKEY * NKEY
NEB = NEXP // P
RAW = 4
PARTS = 4
POOL_LOW = 24
NEG = -1e30
BAND = 512

CH = 2048
SLOTS = 8
BCH = 11 * BAND
BSLOTS = 2
ADA_W = 1024
ADA_G = 6 * D // ADA_W
ADA_SLOTS = 4

PHASES = [("xr", 8), ("yg", 8), ("q", 8), ("k", 8), ("v", 8), ("wout", 16), ("gateup", 2 * KF), ("down", 16),
          ("pproj", 2), ("pgate", 16), ("lat", 8), ("kr", 1), ("qk2", 16), ("v2", 8), ("mla", 7), ("wo", 16),
          ("pq", 16)]
OUTPUTS = {"xr": 8, "yg": 8, "q": 8, "k": 8, "v": 4, "wout": 8, "gateup": 88, "down": 8, "pproj": 8, "pgate": 8, "lat": 4,
           "kr": 2, "qk2": 8, "v2": 4, "mla": 8 + 2 + 8 + 4, "wo": 8, "pq": 16}

COLS = {}
_at = 0
for _n, _w in [("g_mix_pre", KD), ("g_attn_out", 8), ("g_rec_out", 8), ("g_ffn_pre", KD), ("g_ple_pre", KD),
               ("g_q_lat", KL), ("g_kv_lat", KL), ("g_out_a", 8), ("g_out_b", 8), ("conv_w", CONV * RB),
               ("conv_b", RB), ("b_rg_a", 2 * RB), ("b_rg_i", 2 * RB), ("lam", 2 * RB), ("c", KD)]:
    COLS[_n] = _at
    _at += _w
NCOLS = _at
ROW_NAMES = ["g_mix_post", "g_ffn_post", "g_ple_post", "ln1_g", "ln1_b", "ln2_g", "ln2_b"]
SH1, SC1, G1, SH2, SC2, G2 = range(6)


def stream_plan():
    plan, chunk, small, out = {}, 0, 0, 0
    for name, n in PHASES:
        plan[name] = dict(chunk=chunk, small=small, out=out, n=n)
        chunk += n
        out += OUTPUTS[name]
        if name != "down":
            small += n
    return plan, chunk


def build_program(nc, io):
    PLAN, N_CHUNKS = stream_plan()
    assert all(PLAN[p]["small"] % SLOTS == 0 for p in ("gateup", "down"))

    with ExitStack() as ctx:
        place = {}

        def sb(name, shape, dt=F32):
            place[name] = -(-nc.sbuf_base // 32) * 32
            return ctx.enter_context(nc.sbuf_tensor(name, shape, dt))

        def rounded(name, over, first, words):
            return nc.alloc_sbuf_tensor_at(name, [P, words], F32R, offset=place[over] + 4 * first)

        sems = {}

        def sem(name):
            if name not in sems:
                sems[name] = ctx.enter_context(nc.semaphore(name))
            return sems[name]

        ring = sb("ring", [P, SLOTS * CH])
        resid = sb("resid", [P, T, D])
        nat = sb("nat", [P, T, D])
        xT = sb("xT", [P, KD, S])
        aux = sb("aux", [P, 2, D])
        big = sb("big", [P, KF * S])
        misc = sb("misc", [P, 7168])
        cols = sb("cols", [P, NCOLS])
        ident = sb("ident", [P, P])
        ones = sb("ones", [P, P])
        rope_t = sb("rope_t", [P, T, 2 * (ROT_A + ROT_B)])
        pT = sb("pT", [P, 2, S])
        conv_tmp = sb("conv_tmp", [P, 2, S])
        modc = sb("modc", [P, 2, KD])
        ssq = sb("ssq", [P, T, 4])
        st = sb("st", [P, 32])
        stats = sb("stats", [P, T, 4, 6])
        mv = sb("mv", [P, T, 2])
        sp = sb("sp", [P, 4, 2 * RB])
        mxs = sb("mxs", [P, 2, 2 * T])
        den = sb("den", [P, 2, 2 * T])
        cact = sb("cact", [P, KD])
        bank = [ctx.enter_context(nc.psum_tensor(f"bank{i}", [P, BAND], F32)) for i in range(8)]

        ygT = big[:, 0:2048].rearrange("p (b s) -> p b s", b=RB)
        qkT = big[:, 2048:6144].rearrange("p (b s) -> p b s", b=16)
        v1n = big[:, 6144:8192].rearrange("p (t c) -> p t c", t=T)
        xcT = big[:, 8192:10240].rearrange("p (b s) -> p b s", b=RB)
        XP = S + CONV
        xrT = big[:, 8448:8448 + RB * XP].rearrange("p (b s) -> p b s", b=RB)
        attn1 = big[:, 8192:10240].rearrange("p (t c) -> p t c", t=T)
        hidT = big[:, :].rearrange("p (f s) -> p f s", f=KF)
        ple = big[:, 0:T * D].rearrange("p (t c) -> p t c", t=T)
        qkv2 = big[:, 0:6144].rearrange("p (t c) -> p t c", t=T)
        lat = big[:, 6144:6144 + T * 2 * LAT].rearrange("p (t c) -> p t c", t=T)
        scratch2 = big[:, 6144:8192]
        rot = big[:, 8320:8320 + T * 9 * 64].rearrange("p (t c) -> p t c", t=T)
        masks = big[:, 9600:9600 + 2 * T * S].rearrange("p (m t k) -> p m t k", m=2, t=T)
        rows = big[:, 0:5 * D].rearrange("p (r c) -> p r c", r=5)
        bias1 = misc[:, 0:NH * 6 * GRID_W].rearrange("p (h r c) -> p h r c", h=NH, r=6)
        rg_w = misc[:, 3072:3072 + 32 * P].rearrange("p (z g b c) -> p z g b c", z=2, g=2, b=RB)
        scratch1 = misc[:, 3072:5120]
        ada_ring = misc[:, 0:ADA_SLOTS * ADA_W].rearrange("p (s c) -> p s c", s=ADA_SLOTS)
        ada_acc = misc[:, 4096:5120]
        mod_row = misc[:, 5120:6144]
        silu_g = misc[:, 6144:6656].rearrange("p (b s) -> p b s", b=2)
        latT = misc[:, 0:2 * KL * S].rearrange("p (k s) -> p k s", k=2 * KL)
        rotT = misc[:, 2048:2048 + 9 * S].rearrange("p (h s) -> p h s", h=9)
        v2n = misc[:, 4352:4352 + T * DA].rearrange("p (t c) -> p t c", t=T)
        subk = misc[:, 6400:6656].rearrange("p (a k) -> p a k", a=2)
        qb = misc[:, 0:2 * S].rearrange("p (b s) -> p b s", b=2)
        gidx = misc[:, 512:768].bitcast(I32).rearrange("p (t k) -> p t k", t=T)
        gwt = misc[:, 768:1024].rearrange("p (t k) -> p t k", t=T)
        score = misc[:, 2048:2048 + 16 * S].rearrange("p (j c) -> p j c", j=16)
        gstage = misc[:, 1024:1024 + T * TOPK].bitcast(I32).rearrange("p (t k) -> p t k", t=T)
        wstage = misc[:, 1088:1088 + T * TOPK].rearrange("p (t k) -> p t k", t=T)
        token = misc[:, 1152:1152 + T]
        tokbase = misc[:, 1160:1161]
        iota16 = misc[:, 1312:1328]

        o2 = xT[:, :, :].rearrange("p k s -> p (k s)").rearrange("p (t c) -> p t c", t=T)

        auxf = aux[:, :, :].rearrange("p a c -> p (a c)")
        tk_v12 = auxf[:, 0:256].rearrange("p (t h a k) -> p t h a k", t=T, h=4, a=2)
        tk_i12 = auxf[:, 256:512].bitcast(U32).rearrange("p (t h a k) -> p t h a k", t=T, h=4, a=2)
        tk_f12 = auxf[:, 512:768].rearrange("p (t h a k) -> p t h a k", t=T, h=4, a=2)
        tk_tmp = auxf[:, 768:1024]
        tk_cand = auxf[:, 1024:2048].rearrange("p (h i j) -> p h i j", h=4, i=16)
        tk_val = auxf[:, 2048:2176].rearrange("p (t h k) -> p t h k", t=T, h=4)
        tk_ci = auxf[:, 2176:2304].bitcast(U32).rearrange("p (t h k) -> p t h k", t=T, h=4)
        tk_ab = auxf[:, 2304:2560].bitcast(U32).rearrange("p (a c) -> p a c", a=2)
        tk_abf = auxf[:, 2560:2816].rearrange("p (a t h k) -> p a t h k", a=2, t=T, h=4)
        tk_hot = auxf[:, 2816:3840].rearrange("p (n k) -> p n k", k=16)
        tk_sum = auxf[:, 3840:3904]
        tk_pick = auxf[:, 3904:4032].rearrange("p (a n) -> p a n", a=2)

        h2_hi = rounded("h2_hi", "nat", 0, KD * S)[:, :].rearrange("p (k s) -> p k s", k=KD)
        h2_lo = rounded("h2_lo", "big", 6144, KD * S)[:, :].rearrange("p (k s) -> p k s", k=KD)
        slots_left = [(PLAN["pq"]["small"] + i) % SLOTS for i in range(SLOTS)]
        raw = [ring[:, i * CH:(i + 1) * CH] for i in slots_left[:RAW]]
        part_hi = [rounded(f"part_hi{n}", "ring", i * CH, CH)[:, :] for n, i in enumerate(slots_left[RAW:])]
        part_lo = [rounded(f"part_lo{n}", "xT" if n < 2 else "big", (n % 2) * CH, CH)[:, :] for n in range(PARTS)]
        gelu_out = big[:, 10240:11264].rearrange("p (b c) -> p b c", b=2)
        pairs = misc[:, 2048:4096].rearrange("p (n b c) -> p n b c", n=2, b=2)
        weight_in, gelu_in = pairs[:, 0], pairs[:, 1]
        coef_hi, coef_lo = (rounded(n, "misc", first, 4 * S)[:, :].rearrange("p (b c) -> p b c", b=2)
                            for n, first in (("coef_hi", 4096), ("coef_lo", 5120)))
        last_rows = [raw[0], raw[1], raw[2]]
        result = big[:, 0:T * D].rearrange("p (t c) -> p t c", t=T)

        weight_dram = nc.dram_tensor("weight_dram", [P, NEB * S], F32).ap()
        gelu_dram = nc.dram_tensor("gelu_dram", [P, NEB * S], F32).ap()
        mod_dram = nc.dram_tensor("mod_dram", [6, D], F32).ap()

        slot_loaded = [sem(f"slot_loaded{i}") for i in range(SLOTS)]
        big_loaded = [sem(f"big_loaded{i}") for i in range(BSLOTS)]
        ada_loaded = [sem(f"ada_loaded{i}") for i in range(ADA_SLOTS)]
        multiplied = sem("multiplied")
        taken = sem("taken")
        for n in ("x_in", "cols_in", "consts_in", "bias_in", "rg_in", "bias_masked", "dve_step", "act_step", "pool_step",
                  "ones_set", "rms_in", "root_out", "hn_ready", "xr_padded", "conv_done", "gates",
                  "gates_taken", "gates_ready", "rec_b2", "rec_root", "rec_scan", "rec_sum", "rec_sq",
                  "rec_norm", "rec_normed", "aux_free", "row_in", "ssq_in", "resid_piece", "silu_done",
                  "ada_used", "ada_sum", "ada_rowsum", "mod_ready", "mod_b_in", "mod_out", "cact_ready",
                  "modc_in", "pgate_sig", "misc_in", "lat_ready", "rope_done", "rotq_ready", "rows_in",
                  "rows2_in", "h2_ready", "scores", "scores_taken", "staged", "zeros_set", "scattered", "hi_ready", "lo_ready", "h2_hi_ready",
                  "h2_lo_ready", "expert_used", "gelu_done", "coef_raw", "coef_hi_ready", "coef_ready",
                  "result_out", "score_out",
                  "out_ready", "out_done", "sk_in", "iota_done", "topk_exp_in", "topk_exp_out", "o_ready",
                  "modc_ready", "row2_in", "row3_in", "ple_ready", "attn1_ready", "softplus_in", "softplus_exp",
                  "chosen"):
            sem(n)
        table_loaded = [sem(f"table_loaded{i}") for i in range(RAW)]
        gelu_stored = [sem(f"gelu_stored{i}") for i in range(2)]
        pair_loaded = [sem(f"pair_loaded{i}") for i in range(2)]
        row_used = sem("row_used")

        block = ctx.enter_context(nc.Block())

        def slot_of(phase, j):
            return (PLAN[phase]["small"] + j) % SLOTS

        def loads_before(phase, j):
            return (PLAN[phase]["small"] + j) // SLOTS

        def wait_loaded(eng, phase, j, it=0):
            eng.wait_ge(slot_loaded[slot_of(phase, j)], 16 * (loads_before(phase, j) + 1) + 16 * it)

        def slot_ap(phase, j):
            s = slot_of(phase, j)
            return ring[:, s * CH:(s + 1) * CH]

        def wait_multiplied(eng, phase, j, it=0, per=0):
            eng.wait_ge(multiplied, PLAN[phase]["chunk"] + j + 1 + per * it)

        def out_no(phase, o):
            return PLAN[phase]["out"] + o

        def out_bank(phase, o):
            return bank[out_no(phase, o) % 4]

        def wait_bank(pe, phase, o, it=0, per=0):
            n = out_no(phase, o) - 3
            if n > 0:
                pe.wait_ge(taken, n + per * it)

        def loop(eng, n):
            return eng.Fori(0, n)

        class Steps:

            def __init__(self, eng, name):
                self.eng, self.sem, self.n, self.off = eng, sem(name), 0, 0

            def link(self, ins):
                ins.then_inc(self.sem, 1)
                self.n += 1
                self.eng.wait_ge(self.sem, self.n + self.off)

            def mark(self, ins):
                ins.then_inc(self.sem, 1)
                self.n += 1

            def wait(self):
                self.eng.wait_ge(self.sem, self.n + self.off)

            @contextmanager
            def loop(self, n, per):
                with self.eng.Fori(0, n) as it:
                    start, self.off = self.n, it * per
                    yield it
                    assert self.n == start + per, (self.n - start, per)
                self.off = 0
                self.n = start + n * per

        TURNS = {}

        def turn_sems(name):
            if name not in TURNS:
                TURNS[name] = (sem(f"{name}_turned"), sem(f"{name}_taken_v"), sem(f"{name}_taken_a"))
            return TURNS[name]

        for n in ("n1", "n2", "n3", "n4", "n5", "n6", "n7", "n8", "tq", "tr"):
            turn_sems(n)

        def turn_pe(pe, name, n, src, width=P):
            turned, tv, ta = turn_sems(name)
            for k in range(n):
                if k >= 4:
                    pe.wait_ge(ta if k % 2 else tv, (k - 4) // 2 + 1)
                for t in range(T):
                    m = pe.transpose(bank[4 + k % 4][0:width, t * P:(t + 1) * P], src(k, t), ident[:, :])
                m.then_inc(turned, 1)

        def turn_out(eng, name, n, dst, scale=None, shift=None, width=P):
            turned, tv, ta = turn_sems(name)
            odd = eng is nc.scalar
            for k in range(1 if odd else 0, n, 2):
                eng.wait_ge(turned, k + 1)
                ps = bank[4 + k % 4][0:width, 0:S]
                if odd:
                    if shift is not None:
                        i = eng.activation(dst(k), ps, ACT.Identity, scale=scale(k), bias=shift(k))
                    elif scale is not None:
                        i = eng.activation(dst(k), ps, ACT.Copy, scale=scale(k))
                    else:
                        i = eng.activation(dst(k), ps, ACT.Copy)
                    i.then_inc(ta, 1)
                else:
                    if shift is not None:
                        i = eng.tensor_scalar(dst(k), ps, scale(k), shift(k), ALU.mult, ALU.add)
                    elif scale is not None:
                        i = eng.tensor_scalar(dst(k), ps, scale(k), None, ALU.mult)
                    else:
                        i = eng.tensor_copy(dst(k), ps)
                    i.then_inc(tv, 1)

        def wait_turned_out(eng, name, n):
            _, tv, ta = turn_sems(name)
            eng.wait_ge(tv, (n + 1) // 2)
            if n > 1:
                eng.wait_ge(ta, n // 2)

        def gain(name, first=0):
            return lambda k: cols[:, COLS[name] + first + k:COLS[name] + first + k + 1]

        def product_t(pe, phase, j, o, kk=KD, x=None, it=0, per_out=0, sub=0, last=True, wait=True):
            if wait:
                wait_loaded(pe, phase, j, it)
            wait_bank(pe, phase, o, it, per_out)
            w = slot_ap(phase, j)
            for k in range(kk):
                m = pe.matmul(out_bank(phase, o)[:, 0:S], w[:, (sub * kk + k) * P:(sub * kk + k + 1) * P],
                              (x or (lambda k: xT[:, k, :]))(k), start=(k == 0), stop=(k == kk - 1))
            if last:
                m.then_inc(multiplied, 1)

        def product_n(pe, phase, j0, o, nch, kk, lhs, it=0, per_out=0, width=BAND, sub=0, last=True, wait=True):
            for c in range(nch):
                if wait:
                    wait_loaded(pe, phase, j0 + c, it)
                if c == 0:
                    wait_bank(pe, phase, o + T - 1, it, per_out)
                w = slot_ap(phase, j0 + c)
                for k in range(kk):
                    for t in range(T):
                        m = pe.matmul(out_bank(phase, o + t)[:, 0:width], lhs(c * kk + k, t),
                                      w[:, sub * kk * BAND + k * width:sub * kk * BAND + (k + 1) * width],
                                      start=(c == 0 and k == 0), stop=(c == nch - 1 and k == kk - 1))
                if last:
                    m.then_inc(multiplied, 1)

        def x_lhs(k, t):
            return xT[:, k, t * P:(t + 1) * P]

        def n_lhs(k, t):
            return natT[:, k, t * P:(t + 1) * P]

        natT = nat[:, :, :].rearrange("p t c -> p (t c)").rearrange("p (k s) -> p k s", k=KD)

        KINDS = ("at1", "at2", "at3")
        for n in KINDS:
            for m in ("scored", "biased", "exped", "turned", "pt_out", "valued", "out"):
                sem(f"{n}_{m}")

        def attention_pe(pe, kind, score, value, scratch):
            prob, prT = attention_scratch(scratch)

            def scores(h):
                if h >= 2:
                    pe.wait_ge(sem(f"{kind}_biased"), h - 1)
                for t in range(T):
                    m = score(pe, h, t, bank[h % 2][:, t * S:(t + 1) * S])
                m.then_inc(sem(f"{kind}_scored"), 1)

            def turn(h):
                pe.wait_ge(sem(f"{kind}_exped"), h + 1)
                if h >= 2:
                    pe.wait_ge(sem(f"{kind}_pt_out"), h - 1)
                for kc in range(T):
                    for t in range(T):
                        m = pe.transpose(bank[2 + h % 2][:, kc * S + t * P:kc * S + (t + 1) * P],
                                         prob[:, h % 2, t, kc * P:(kc + 1) * P], ident[:, :])
                m.then_inc(sem(f"{kind}_turned"), 1)

            def values(h):
                pe.wait_ge(sem(f"{kind}_pt_out"), h + 1)
                if h >= 2:
                    pe.wait_ge(sem(f"{kind}_out"), h - 1)
                for t in range(T):
                    for kc in range(T):
                        m = pe.matmul(bank[4 + h % 2][:, t * P:(t + 1) * P], prT[:, h % 2, kc, t * P:(t + 1) * P],
                                      value(kc, h), start=(kc == 0), stop=(kc == T - 1))
                m.then_inc(sem(f"{kind}_valued"), 1)

            scores(0)
            for h in range(NH):
                if h + 1 < NH:
                    scores(h + 1)
                turn(h)
                if h:
                    values(h - 1)
            values(NH - 1)

        def attention_scratch(scratch):
            prob = scratch[:, 0:1024].rearrange("p (b t k) -> p b t k", b=2, t=T)
            prT = scratch[:, 1024:2048].rearrange("p (b c q) -> p b c q", b=2, c=T)
            return prob, prT

        def by_row(ap):
            return ap.rearrange("p (r c) -> p r c", c=GRID_W)

        def attention_dve(v, steps, kind, bias, scale, out, scratch):
            prob, prT = attention_scratch(scratch)

            def biased(h):
                v.wait_ge(sem(f"{kind}_scored"), h + 1)
                if h >= 2:
                    v.wait_ge(sem(f"{kind}_turned"), h - 1)
                for t in range(T):
                    i = v.scalar_tensor_tensor(out=by_row(prob[:, h % 2, t, :]),
                                               in0=by_row(bank[h % 2][:, t * S:(t + 1) * S]),
                                               scalar=scale, in1=bias(h, t), op0=ALU.mult, op1=ALU.add)
                    if t == T - 1:
                        i.then_inc(sem(f"{kind}_biased"), 1)
                    else:
                        steps.mark(i)
                steps.wait()
                v.wait_ge(sem(f"{kind}_biased"), h + 1)
                steps.link(v.tensor_reduce(mxs[:, h % 2, 0:T], prob[:, h % 2, :, :], AXX, ALU.max))
                v.tensor_scalar(mxs[:, h % 2, T:2 * T], mxs[:, h % 2, 0:T], -1.0, None, ALU.mult).then_inc(
                    sem(f"{kind}_negmax"), 1)

            def result(h):
                v.wait_ge(sem(f"{kind}_exped"), h + 1)
                steps.link(v.reciprocal(den[:, h % 2, T:2 * T], den[:, h % 2, 0:T]))
                v.wait_ge(sem(f"{kind}_valued"), h + 1)
                for t in range(T):
                    i = v.tensor_scalar(out(h, t), bank[4 + h % 2][:, t * P:(t + 1) * P],
                                        den[:, h % 2, T + t:T + t + 1], None, ALU.mult)
                    if t == T - 1:
                        i.then_inc(sem(f"{kind}_out"), 1)
                    else:
                        steps.mark(i)
                steps.wait()

            for h in range(NH):
                biased(h)
                if h >= 2:
                    result(h - 2)
            result(NH - 2)
            result(NH - 1)
            v.wait_ge(sem(f"{kind}_out"), NH)

        def attention_act(a, kind, scratch):
            prob, prT = attention_scratch(scratch)

            def exps(h):
                a.wait_ge(sem(f"{kind}_negmax"), h + 1)
                if h >= 2:
                    a.wait_ge(sem(f"{kind}_out"), h - 1)
                for t in range(T):
                    i = a.activation(prob[:, h % 2, t, :], prob[:, h % 2, t, :], ACT.Exp,
                                     bias=mxs[:, h % 2, T + t:T + t + 1], accum_out=den[:, h % 2, t:t + 1])
                i.then_inc(sem(f"{kind}_exped"), 1)

            def turned(h):
                a.wait_ge(sem(f"{kind}_turned"), h + 1)
                if h >= 2:
                    a.wait_ge(sem(f"{kind}_valued"), h - 1)
                a.activation(prT[:, h % 2, :, :].rearrange("p c q -> p (c q)"), bank[2 + h % 2][:, :], ACT.Copy)\
                    .then_inc(sem(f"{kind}_pt_out"), 1)

            exps(0)
            for h in range(NH):
                if h + 1 < NH:
                    exps(h + 1)
                turned(h)

        for n in KINDS:
            sem(f"{n}_negmax")

        wst = io["stream"]

        @block.sync
        def _(sp_):
            for t in range(T):
                sp_.dma_start(resid[:, t, :], io["x"][0, t * P:(t + 1) * P, :]).then_inc(sem("x_in"), 16)

            def load(phase, j, it=None, gate=True):
                s = slot_of(phase, j)
                small = PLAN[phase]["small"] + j
                chunk = PLAN[phase]["chunk"] + j
                if it is None or isinstance(it, int):
                    sp_.dma_start(ring[:, s * CH:(s + 1) * CH], wst[small]).then_inc(slot_loaded[s], 16)
                else:
                    sp_.dma_start(ring[:, s * CH:(s + 1) * CH],
                                  wst[bass.ds(small + it * SLOTS, 1)].rearrange("n p c -> (n p) c"))\
                        .then_inc(slot_loaded[s], 16)

            def stream(phase, n, j0=0):
                rounds = n // SLOTS
                assert n % SLOTS == 0
                if rounds == 1:
                    for j in range(SLOTS):
                        sp_.wait_ge(multiplied, PLAN[phase]["chunk"] + j0 + j - SLOTS + 1)
                        load(phase, j0 + j)
                    return
                with loop(sp_, rounds) as it:
                    for j in range(SLOTS):
                        sp_.wait_ge(multiplied, PLAN[phase]["chunk"] + j0 + j - SLOTS + 1 + it * SLOTS)
                        load(phase, j0 + j, it)

            for j in range(SLOTS):
                load("xr", j)
            stream("yg", 8)
            stream("q", 8)
            stream("k", 8)
            stream("v", 8)
            stream("wout", 16)

            def ada_load(j, g):
                for k in (2 * j, 2 * j + 1):
                    s = k % ADA_SLOTS
                    sp_.wait_ge(sem("ada_used"), KD * g + k + 1)
                    sp_.dma_start(ada_ring[:, s, :], io["w_ada"][k * P:(k + 1) * P, bass.ds(g * ADA_W, ADA_W)])\
                        .then_inc(ada_loaded[s], 16)

            stream("gateup", SLOTS)
            with loop(sp_, KF // 4 - 1) as it:
                for j in range(SLOTS):
                    sp_.wait_ge(multiplied, PLAN["gateup"]["chunk"] + j + 1 + it * SLOTS)
                    load("gateup", SLOTS + j, it)
                    ada_load(j, it)

            gu_end = PLAN["down"]["chunk"]

            def load_big(c, it=0):
                s = c % BSLOTS
                src = io["down"][c] if isinstance(it, int) else \
                    io["down"][bass.ds(c + it * 8, 1)].rearrange("n p c -> (n p) c")
                sp_.dma_start(ring[:, s * BCH:(s + 1) * BCH], src).then_inc(big_loaded[s], 16)

            for j in range(4):
                ada_load(j, ADA_G - 2)
            sp_.wait_ge(multiplied, gu_end - SLOTS + 3)
            load_big(0)
            for j in range(4, 8):
                ada_load(j, ADA_G - 2)
            sp_.wait_ge(multiplied, gu_end - SLOTS + 6)
            load_big(1)
            for j in range(8):
                ada_load(j, ADA_G - 1)
            for c in range(2, 16):
                sp_.wait_ge(multiplied, gu_end + c - BSLOTS + 1)
                load_big(c)
            down_end = PLAN["pproj"]["chunk"]
            assert PLAN["pproj"]["small"] % SLOTS == 0
            first = [("pproj", 0), ("pproj", 1)] + [("pgate", j) for j in range(6)]
            for n, (ph, j) in enumerate(first):
                if n == 0:
                    sp_.wait_ge(multiplied, down_end - 1)
                if n == 2:
                    sp_.wait_ge(multiplied, down_end)
                load(ph, j)

            def rest(phase, j0, n):
                for j in range(j0, j0 + n):
                    sp_.wait_ge(multiplied, PLAN[phase]["chunk"] + j - SLOTS + 1)
                    load(phase, j)

            rest("pgate", 6, 10)
            rest("lat", 0, 8)
            rest("kr", 0, 1)
            stream("qk2", 16)
            stream("v2", 8)
            rest("mla", 0, 7)
            stream("wo", 16)
            stream("pq", 16)

            for j in range(RAW):
                sp_.wait_ge(multiplied, N_CHUNKS - SLOTS + j + 1)
                sp_.dma_start(raw[j], io["u_table"][j]).then_inc(table_loaded[j], 16)

            def table_chunks(table, base, rounds):
                with loop(sp_, rounds) as it:
                    for j in range(RAW):
                        sp_.wait_ge(sem("lo_ready"), base - RAW + j + 1 + RAW * it)
                        row = bass.ds(base % NEB + j + RAW * it, 1)
                        sp_.dma_start(raw[j], io[table][row].rearrange("n p c -> (n p) c"))\
                            .then_inc(table_loaded[j], 16)

            table_chunks("u_table", RAW, NEB // RAW - 1)
            table_chunks("v_table", NEB, NEB // RAW)

            for t in range(T):
                sp_.wait_ge(sem("out_ready"), t + 1)
                sp_.dma_start(io["out"][0, t * P:(t + 1) * P, :], resid[:, t, :]).then_inc(sem("out_done"), 16)
            sp_.wait_ge(sem("out_done"), 16 * T)

        @block.tensor
        def _(pe):
            pe.wait_ge(sem("consts_in"), 16 * 3)
            pe.wait_ge(sem("ones_set"), 1)
            pe.wait_ge(sem("hn_ready"), 1)
            turn_pe(pe, "n1", KD, lambda k, t: nat[:, t, k * P:(k + 1) * P])
            wait_turned_out(pe, "n1", KD)
            for j in range(RB):
                product_t(pe, "xr", j, j)
            for j in range(RB):
                product_t(pe, "yg", j, j)

            def gates(z):
                if z == 0:
                    pe.wait_ge(sem("rg_in"), 16)
                for b in range(RB):
                    pe.wait_ge(sem("conv_done"), b + 1)
                    n = z * RB + b
                    if n >= 4:
                        pe.wait_ge(sem("gates_taken"), n - 3)
                    for g in range(2):
                        m = pe.matmul(bank[4 + n % 4][:, g * S:(g + 1) * S], rg_w[:, z, g, b, :], xcT[:, b, :],
                                      start=True, stop=True)
                    m.then_inc(sem("gates"), 1)

            gates(0)
            for j in range(RB):
                product_t(pe, "q", j, j)
            gates(1)
            for j in range(RB):
                product_t(pe, "k", j, j)
            for c in range(2):
                product_n(pe, "v", 4 * c, 2 * c, 4, 4, x_lhs)
            pe.wait_ge(sem("bias_masked"), 4)
            pe.wait_ge(taken, out_no("wout", 0))
            pe.wait_ge(sem("gates_taken"), 2 * RB)

            def score1(pe, h, t, ps):
                return pe.matmul(ps, qkT[:, h, t * P:(t + 1) * P], qkT[:, NH + h, :], start=True, stop=True)

            attention_pe(pe, "at1", score1, lambda kc, h: v1n[:, kc, h * HD:(h + 1) * HD], scratch1)
            pe.wait_ge(sem("attn1_ready"), 1)
            pe.wait_ge(sem("at1_out"), NH)
            turn_pe(pe, "n2", 8, lambda k, t: attn1[:, t, k * P:(k + 1) * P])
            wait_turned_out(pe, "n2", 8)
            pe.wait_ge(sem("rec_sq"), 1)
            for b in range(RB):
                m = pe.matmul(bank[4][:, 0:S], ones[:, :], nat[:, 0, b * S:(b + 1) * S], start=(b == 0),
                              stop=(b == RB - 1))
            m.then_inc(sem("rec_norm"), 1)
            pe.wait_ge(sem("rec_normed"), RB)
            with loop(pe, 2) as it:
                for c in range(2):
                    product_n(pe, "wout", 4 * c, 2 * c, 4, 4, x_lhs, it=it, per_out=4)
            pe.wait_ge(sem("hn_ready"), 2)
            turn_pe(pe, "n3", KD, lambda k, t: nat[:, t, k * P:(k + 1) * P])
            wait_turned_out(pe, "n3", KD)

            def ada_sum(g):
                pe.wait_ge(sem("ada_sum"), g + 1)
                for c in range(2):
                    m = pe.matmul(bank[4 + c][0:1, :], ones[:, 0:1], ada_acc[:, c * BAND:(c + 1) * BAND],
                                  start=True, stop=True)
                m.then_inc(sem("ada_rowsum"), 1)

            with loop(pe, KF // 4) as it:
                for j in range(8):
                    product_t(pe, "gateup", j, j, it=it, per_out=8)
                ada_sum(it)
            pe.wait_ge(taken, out_no("down", 0))
            for c in range(4):
                for q in range(4):
                    n = 4 * c + q
                    pe.wait_ge(big_loaded[n % BSLOTS], 16 * (n // BSLOTS + 1))
                    if q == 0:
                        wait_bank(pe, "down", 2 * c + 1)
                    for k in range(11):
                        for t in range(T):
                            m = pe.matmul(out_bank("down", 2 * c + t)[:, :],
                                          hidT[:, 11 * q + k, t * P:(t + 1) * P],
                                          ring[:, (n % BSLOTS) * BCH + k * BAND:(n % BSLOTS) * BCH + (k + 1) * BAND],
                                          start=(q == 0 and k == 0), stop=(q == 3 and k == 10))
                    m.then_inc(multiplied, 1)
                if c == 0:
                    ada_sum(ADA_G - 1)
            for c in range(4):
                product_n(pe, "pproj", c // 2, 2 * c, 1, 2, lambda k, t: pT[:, k, t * P:(t + 1) * P], sub=c % 2,
                          last=(c % 2 == 1))
            pe.wait_ge(sem("hn_ready"), 3)
            turn_pe(pe, "n4", KD, lambda k, t: nat[:, t, k * P:(k + 1) * P])
            wait_turned_out(pe, "n4", KD)
            with loop(pe, 2) as it:
                for c in range(2):
                    product_n(pe, "pgate", 4 * c, 2 * c, 4, 4, x_lhs, it=it, per_out=4)

            pe.wait_ge(sem("hn_ready"), 4)
            turn_pe(pe, "n5", KD, lambda k, t: nat[:, t, k * P:(k + 1) * P])
            wait_turned_out(pe, "n5", KD)
            for c in range(2):
                product_n(pe, "lat", 4 * c, 2 * c, 4, 4, x_lhs)
            product_n(pe, "kr", 0, 0, 1, KD, x_lhs, width=64)
            with loop(pe, 2) as it:
                for c in range(2):
                    product_n(pe, "qk2", 4 * c, 2 * c, 4, 4, x_lhs, it=it, per_out=4)
            pe.wait_ge(sem("lat_ready"), 1)
            turn_pe(pe, "n6", 2 * KL, lambda k, t: lat[:, t, k * P:(k + 1) * P])
            for c in range(2):
                product_n(pe, "v2", 4 * c, 2 * c, 4, 4, x_lhs)
            pe.wait_ge(sem("rope_done"), 1)
            wait_turned_out(pe, "n6", 2 * KL)
            turn_pe(pe, "tq", 2 * NH, lambda k, t: qkv2[:, t, k * P:(k + 1) * P])
            for c in range(2):
                for s in range(4):
                    product_t(pe, "mla", c, 4 * c + s, kk=KL, x=lambda k: latT[:, k, :], sub=s, last=(s == 3))
            product_n(pe, "mla", 2, 8, 1, KL, lambda k, t: latT[:, k, t * P:(t + 1) * P])
            for c in range(2):
                for s in range(4):
                    product_t(pe, "mla", 3 + c, 10 + 4 * c + s, kk=KL, x=lambda k: latT[:, KL + k, :], sub=s,
                              last=(s == 3))
            for c in range(2):
                product_n(pe, "mla", 5 + c, 18 + 2 * c, 1, KL, lambda k, t: latT[:, KL + k, t * P:(t + 1) * P])
            wait_turned_out(pe, "tq", 2 * NH)
            pe.wait_ge(sem("rotq_ready"), 1)
            turn_pe(pe, "tr", 9, lambda k, t: rot[:, t, k * 64:(k + 1) * 64], width=64)
            wait_turned_out(pe, "tr", 9)
            pe.wait_ge(taken, out_no("wo", 0))

            def score2(pe, h, t, ps):
                return pe.matmul(ps, natT[:, h, t * P:(t + 1) * P], natT[:, NH + h, :], start=True, stop=True)

            def score3(pe, h, t, ps):
                pe.matmul(ps, aux[:, 0, h * S + t * P:h * S + (t + 1) * P], aux[:, 1, h * S:(h + 1) * S],
                          start=True, stop=False)
                return pe.matmul(ps, rotT[0:64, h, t * P:(t + 1) * P], rotT[0:64, 8, :], start=False, stop=True)

            pe.wait_ge(sem("misc_in"), 16)
            attention_pe(pe, "at2", score2, lambda kc, h: qkv2[:, kc, 2 * DA + h * HD:2 * DA + (h + 1) * HD], scratch2)
            pe.wait_ge(sem("at2_out"), NH)
            attention_pe(pe, "at3", score3, lambda kc, h: v2n[:, kc, h * HD:(h + 1) * HD], scratch2)
            pe.wait_ge(sem("at3_out"), NH)
            pe.wait_ge(sem("o_ready"), 1)
            turn_pe(pe, "n7", KD, lambda k, t: o2[:, t, k * P:(k + 1) * P])
            wait_turned_out(pe, "n7", KD)
            with loop(pe, 2) as it:
                for c in range(2):
                    product_n(pe, "wo", 4 * c, 2 * c, 4, 4, n_lhs, it=it, per_out=4)
            pe.wait_ge(sem("h2_ready"), 1)
            turn_pe(pe, "n8", KD, lambda k, t: nat[:, t, k * P:(k + 1) * P])
            wait_turned_out(pe, "n8", KD)
            pe.wait_ge(sem("sk_in"), 16)

            with loop(pe, 2) as it:
                def key_scores(j):
                    pe.wait_ge(taken, out_no("pq", j) + 1 + it * 8)
                    pe.wait_ge(sem("score_out"), it * 8 + j + 1)
                    for t in range(T):
                        m = pe.matmul(bank[4 + j % 2][:, t * P:(t + 1) * P], qb[:, j % 2, t * P:(t + 1) * P],
                                      subk[:, j % 2, :], start=True, stop=True)
                    m.then_inc(sem("scores"), 1)

                for j in range(8):
                    product_t(pe, "pq", j, j, it=it, per_out=8)
                    if j:
                        key_scores(j - 1)
                key_scores(7)

            def split_products(out, hi, lo, x_hi, x_lo, start, stop):
                pe.matmul(out, hi, x_hi, start=start, stop=False)
                pe.matmul(out, hi, x_lo, start=False, stop=False)
                return pe.matmul(out, lo, x_hi, start=False, stop=stop)

            pe.wait_ge(sem("h2_lo_ready"), 1)
            pe.wait_ge(taken, out_no("pq", 16))

            def dots_of_block(j, it, first=False):
                pe.wait_ge(sem("lo_ready"), j + 1 + PARTS * it)
                if not first:
                    pe.wait_ge(sem("gelu_done"), j - 3 + PARTS * it)
                for k in range(KD):
                    ks = slice(k * P, (k + 1) * P)
                    m = split_products(bank[j % 4][:, 0:S], part_hi[j % PARTS][:, ks], part_lo[j % PARTS][:, ks],
                                       h2_hi[:, k, :], h2_lo[:, k, :], k == 0, k == KD - 1)
                m.then_inc(sem("expert_used"), 1)

            for j in range(PARTS):
                dots_of_block(j, 0, True)
            with loop(pe, NEB // PARTS - 1) as it:
                for j in range(PARTS):
                    dots_of_block(j + PARTS, it)

            pe.wait_ge(sem("gelu_done"), NEB)
            pe.wait_ge(sem("score_out"), 2 + 16)

            def values_of_block(j, it, start=False, stop=False):
                pe.wait_ge(sem("lo_ready"), NEB + j + 1 + PARTS * it)
                if j % 2 == 0:
                    pe.wait_ge(sem("coef_ready"), j // 2 + 1 + PARTS // 2 * it)
                for t in range(T):
                    for c in range(D // BAND):
                        ts = slice((j % 2) * S + t * P, (j % 2) * S + (t + 1) * P)
                        cs = slice(c * BAND, (c + 1) * BAND)
                        b = j // 2 % 2
                        m = split_products(bank[4 * t + c][:, :], coef_hi[:, b, ts], coef_lo[:, b, ts],
                                           part_hi[j % PARTS][:, cs], part_lo[j % PARTS][:, cs], start, stop)
                m.then_inc(sem("expert_used"), 1)

            for j in range(PARTS):
                values_of_block(j, 0, start=j == 0)
            with loop(pe, NEB // PARTS - 2) as it:
                for j in range(PARTS):
                    values_of_block(PARTS + j, it)
            for j in range(NEB - PARTS, NEB):
                values_of_block(j, 0, stop=j == NEB - 1)

        @block.scalar
        def _(a):
            steps = Steps(a, "act_step")
            a.wait_ge(sem("cols_in"), 16)
            a.wait_ge(sem("softplus_in"), 1)
            a.activation(sp[:, 1, :], sp[:, 0, :], ACT.Exp, scale=-1.0).then_inc(sem("softplus_exp"), 1)

            def root(n):
                a.wait_ge(sem("rms_in"), n)
                a.activation(st[:, 2:4], st[:, 0:2], ACT.Sqrt).then_inc(sem("root_out"), 1)

            def copy_out(phase, o, dst, it=0, per_chunks=0, chunk=0, func=ACT.Copy, width=BAND, signal=True):
                wait_multiplied(a, phase, chunk, it, per_chunks)
                i = a.activation(dst, out_bank(phase, o)[:, 0:width], func)
                if signal:
                    i.then_inc(taken, 1)
                return i

            root(1)
            turn_out(nc.scalar, "n1", KD, lambda k: xT[:, k, :], gain("g_mix_pre"))
            a.wait_ge(sem("xr_padded"), 1)
            for j in range(RB):
                copy_out("xr", j, xrT[:, j, 2:2 + S], chunk=j, width=S)
            for j in range(RB):
                copy_out("yg", j, ygT[:, j, :], chunk=j, width=S, func=ACT.Gelu_apprx_tanh)

            recA, recB = nat[:, 0, :], nat[:, 1, :]
            recU, recH = aux[:, 0, :], aux[:, 1, :]
            a.wait_ge(sem("n1_turned"), KD)

            def gate_out(z):
                if z:
                    a.wait_ge(sem("rec_scan"), 1)
                for b in range(RB):
                    n = z * RB + b
                    a.wait_ge(sem("gates"), n + 1)
                    steps.mark(a.activation(recA[:, b * S:(b + 1) * S], bank[4 + n % 4][:, 0:S], ACT.Sigmoid,
                                            bias=cols[:, COLS["b_rg_a"] + n:COLS["b_rg_a"] + n + 1]))
                    a.activation(recU[:, b * S:(b + 1) * S], bank[4 + n % 4][:, S:2 * S], ACT.Sigmoid,
                                 bias=cols[:, COLS["b_rg_i"] + n:COLS["b_rg_i"] + n + 1]).then_inc(
                        sem("gates_taken"), 1)
                steps.wait()
                if z == 0:
                    a.wait_ge(sem("softplus_in"), 2)
                for b in range(RB):
                    n = z * RB + b
                    i = a.activation(recA[:, b * S:(b + 1) * S], recA[:, b * S:(b + 1) * S], ACT.Tanh,
                                     scale=sp[:, 3, n:n + 1])
                    if b == RB - 1:
                        i.then_inc(sem("gates_ready"), 1)
                    else:
                        steps.mark(i)

            def rec_root(z):
                a.wait_ge(sem("rec_b2"), z + 1)
                a.activation(recB, recB, ACT.Sqrt, scale=-1.0).then_inc(sem("rec_root"), 1)

            gate_out(0)
            for j in range(RB):
                copy_out("q", j, qkT[:, j, :], chunk=j, width=S)
            rec_root(0)
            gate_out(1)
            for j in range(RB):
                copy_out("k", j, qkT[:, NH + j, :], chunk=j, width=S)
            rec_root(1)
            for c in range(2):
                for t in range(T):
                    copy_out("v", 2 * c + t, v1n[:, t, c * BAND:(c + 1) * BAND], chunk=4 * c + 3)
            attention_act(a, "at1", scratch1)
            root(2)
            turn_out(nc.scalar, "n2", 8, lambda k: xT[:, k, :], gain("g_attn_out"))
            a.wait_ge(sem("rec_sum"), 1)
            a.activation(recA, recH, ACT.Square).then_inc(sem("rec_sq"), 1)
            a.wait_ge(sem("rec_norm"), 2)
            a.activation(conv_tmp[:, 0, :], conv_tmp[:, 0, :], ACT.Sqrt).then_inc(sem("rec_norm"), 1)

            def panels(phase, n, squares=True, func=ACT.Copy, dst=None):
                dst = nat if dst is None else dst
                with loop(a, 2) as it:
                    for c in range(2):
                        for t in range(T):
                            wait_multiplied(a, phase, 4 * c + 3, it, 8)
                            ps = out_bank(phase, 2 * c + t)
                            i = a.activation(dst[:, t, bass.ds(c * BAND + it * 2 * BAND, BAND)], ps[:, :], func)
                            if squares:
                                a.wait_ge(taken, out_no(phase, 2 * c + t) + 4 * it)
                                a.activation(silu_junk, ps[:, :], ACT.Square,
                                             accum_out=ssq[:, t, bass.ds(c + it * 2, 1)]).then_inc(taken, 1)
                            else:
                                i.then_inc(taken, 1)

            silu_junk = bank[6][:, :]

            def resid_squares(n0):
                for t in range(T):
                    for c in range(4):
                        a.wait_ge(sem("resid_piece"), n0 + t * 4 + c + 1)
                        if n0 + t + c:
                            a.wait_ge(sem("ssq_in"), n0 + t * 4 + c)
                        i = a.activation(bank[6][:, :], resid[:, t, c * BAND:(c + 1) * BAND], ACT.Square,
                                         accum_out=ssq[:, t, c:c + 1])
                        i.then_inc(sem("ssq_in"), 1)

            a.activation(cact[:, :], cols[:, COLS["c"]:COLS["c"] + KD], ACT.Silu).then_inc(sem("cact_ready"), 1)
            panels("wout", 0)
            root(3)
            resid_squares(0)
            root(4)
            turn_out(nc.scalar, "n3", KD, lambda k: xT[:, k, :], gain("g_ffn_pre"))
            with loop(a, KF // 4) as it:
                for j in range(4):
                    wait_multiplied(a, "gateup", 2 * j, it, 8)
                    a.wait_ge(taken, out_no("gateup", 0) + 2 * (j - 1) + it * 8)
                    a.activation(silu_g[:, j % 2, :], out_bank("gateup", 2 * j)[:, 0:S], ACT.Silu).then_inc(
                        sem("silu_done"), 1)

            for c in range(4):
                for t in range(T):
                    wait_multiplied(a, "down", 4 * c + 3)
                    ps = out_bank("down", 2 * c + t)
                    a.activation(nat[:, t, c * BAND:(c + 1) * BAND], ps[:, :], ACT.Copy)
                    a.wait_ge(taken, out_no("down", 2 * c + t))
                    a.activation(silu_junk, ps[:, :], ACT.Square, accum_out=ssq[:, t, c:c + 1]).then_inc(taken, 1)
            for c in range(4):
                for t in range(T):
                    i = copy_out("pproj", 2 * c + t, ple[:, t, c * BAND:(c + 1) * BAND], chunk=c // 2)
            root(5)
            resid_squares(8)
            root(6)
            turn_out(nc.scalar, "n4", KD, lambda k: xT[:, k, :], gain("g_ple_pre"))
            with loop(a, 2) as it:
                for c in range(2):
                    for t in range(T):
                        wait_multiplied(a, "pgate", 4 * c + 3, it, 8)
                        a.activation(nat[:, t, bass.ds(c * BAND + it * 2 * BAND, BAND)],
                                     out_bank("pgate", 2 * c + t)[:, :], ACT.Sigmoid).then_inc(taken, 1)
            for t in range(T):
                a.wait_ge(sem("pgate_sig"), t + 1)
                for c in range(4):
                    if t + c:
                        a.wait_ge(sem("ple_ready"), 4 * t + c)
                    a.activation(bank[6][:, :], nat[:, t, c * BAND:(c + 1) * BAND], ACT.Square,
                                 accum_out=ssq[:, t, c:c + 1]).then_inc(sem("ple_ready"), 1)
            root(7)

            root(8)
            a.wait_ge(sem("modc_ready"), 1)
            turn_out(nc.scalar, "n5", KD, lambda k: xT[:, k, :], lambda k: modc[:, 0, k:k + 1],
                     lambda k: modc[:, 1, k:k + 1])
            for c in range(2):
                for t in range(T):
                    wait_multiplied(a, "lat", 4 * c + 3)
                    ps = out_bank("lat", 2 * c + t)
                    a.activation(lat[:, t, c * LAT:(c + 1) * LAT], ps[:, :], ACT.Copy)
                    a.wait_ge(taken, out_no("lat", 2 * c + t))
                    a.activation(silu_junk, ps[:, :], ACT.Square, accum_out=ssq[:, t, c:c + 1]).then_inc(taken, 1)
            for t in range(T):
                copy_out("kr", t, rot[:, t, 8 * 64:9 * 64], chunk=0, width=64)
            a.wait_ge(sem("rms_in"), 9)
            a.activation(st[:, 8:12], st[:, 4:8], ACT.Sqrt).then_inc(sem("root_out"), 1)
            with loop(a, 2) as it:
                for c in range(2):
                    for t in range(T):
                        wait_multiplied(a, "qk2", 4 * c + 3, it, 8)
                        a.activation(qkv2[:, t, bass.ds(c * BAND + it * 2 * BAND, BAND)],
                                     out_bank("qk2", 2 * c + t)[:, :], ACT.Copy).then_inc(taken, 1)
            turn_out(nc.scalar, "n6", 2 * KL, lambda k: latT[:, k, :], gain("g_q_lat"))
            for c in range(2):
                for t in range(T):
                    copy_out("v2", 2 * c + t, qkv2[:, t, 2 * DA + c * BAND:2 * DA + (c + 1) * BAND], chunk=4 * c + 3)
            turn_out(nc.scalar, "tq", 2 * NH, lambda k: natT[:, k, :])
            a.wait_ge(sem("rope_done"), 1)
            for h in range(NH):
                copy_out("mla", h, aux[:, 0, h * S:(h + 1) * S], chunk=h // 4, width=S)
            for t in range(T):
                copy_out("mla", 8 + t, rot[:, t, 0:512], chunk=2)
            for h in range(NH):
                copy_out("mla", 10 + h, aux[:, 1, h * S:(h + 1) * S], chunk=3 + h // 4, width=S)
            for c in range(2):
                for t in range(T):
                    copy_out("mla", 18 + 2 * c + t, v2n[:, t, c * BAND:(c + 1) * BAND], chunk=5 + c)
            turn_out(nc.scalar, "tr", 9, lambda k: rotT[0:64, k, :], width=64)
            attention_act(a, "at2", scratch2)
            a.wait_ge(sem("at2_out"), NH)
            attention_act(a, "at3", scratch2)
            a.wait_ge(sem("rms_in"), 10)
            a.activation(st[:, 8:12], st[:, 4:8], ACT.Sqrt).then_inc(sem("root_out"), 1)
            turn_out(nc.scalar, "n7", KD, lambda k: natT[:, k, :], gain("g_out_a"))
            wait_turned_out(a, "n7", KD)
            with loop(a, 2) as it:
                for c in range(2):
                    for t in range(T):
                        wait_multiplied(a, "wo", 4 * c + 3, it, 8)
                        a.activation(o2[:, t, bass.ds(c * BAND + it * 2 * BAND, BAND)],
                                     out_bank("wo", 2 * c + t)[:, :], ACT.Copy).then_inc(taken, 1)
            root(11)
            root(12)
            turn_out(nc.scalar, "n8", KD, lambda k: xT[:, k, :])
            wait_turned_out(a, "n8", KD)
            for n in range(4):
                a.activation(h2_hi[:, 4 * n:4 * n + 4, :], xT[:, 4 * n:4 * n + 4, :], ACT.Copy).then_inc(
                    sem("h2_hi_ready"), 1)
            a.wait_ge(sem("zeros_set"), 1)

            def query(j, it):
                wait_multiplied(a, "pq", j, it, 8)
                if j >= 2:
                    a.wait_ge(sem("scores"), it * 8 + j - 1)
                a.activation(qb[:, j % 2, :], out_bank("pq", j)[:, 0:S], ACT.Copy).then_inc(taken, 1)

            def score_copy(j, it):
                a.wait_ge(sem("scores"), it * 8 + j + 1)
                to = score[:, j, :] if isinstance(it, int) else \
                    score[:, bass.ds(it * 8 + j, 1), :].rearrange("p o c -> p (o c)")
                a.activation(to, bank[4 + j % 2][:, 0:S], ACT.Copy).then_inc(sem("score_out"), 1)

            with loop(a, 2) as it:
                for j in range(8):
                    query(j, it)
                    if j:
                        score_copy(j - 1, it)
                score_copy(7, it)

            def upper(j, it=0, first=False):
                a.wait_ge(table_loaded[j % RAW], 16 * (j // RAW + 1) + 16 * it)
                if not first:
                    a.wait_ge(sem("expert_used"), j - PARTS + 1 + PARTS * it)
                a.activation(part_hi[j % PARTS], raw[j % RAW], ACT.Copy).then_inc(
                    sem("hi_ready"), 1)

            def gelu(j, it=0, first=False):
                a.wait_ge(sem("expert_used"), j + 1 + PARTS * it)
                if j % 2 == 0 and not first:
                    a.wait_ge(gelu_stored[j // 2 % 2], 16 * (j // 4) + 16 * it)
                a.activation(gelu_out[:, j // 2 % 2, (j % 2) * S:(j % 2 + 1) * S], bank[j % 4][:, 0:S], ACT.Gelu)\
                    .then_inc(sem("gelu_done"), 1)
                if j % 2:
                    a.wait_ge(sem("gelu_done"), j + 1 + PARTS * it)
                    if isinstance(it, int):
                        a.dma_start(gelu_dram[:, (j - 1) * S:(j + 1) * S], gelu_out[:, j // 2 % 2, :]).then_inc(
                            gelu_stored[j // 2 % 2], 16)
                    else:
                        a.dma_start(gelu_dram[:, bass.ds(((j - 1) + PARTS * it) * S, 2 * S)],
                                    gelu_out[:, j // 2 % 2, :]).then_inc(gelu_stored[j // 2 % 2], 16)

            def choice_exp(n):
                a.wait_ge(sem("topk_exp_in"), n + 1)
                a.activation(tk_val.rearrange("p t h k -> p (t h k)"),
                             tk_abf[:, 0].rearrange("p t h k -> p (t h k)"), ACT.Exp).then_inc(sem("topk_exp_out"), 1)

            a.wait_ge(multiplied, N_CHUNKS)
            for j in range(PARTS):
                upper(j, first=True)
            choice_exp(0)
            for j in range(PARTS):
                upper(PARTS + j)
                gelu(j, first=True)
            with loop(a, POOL_LOW // PARTS - 2) as it:
                for j in range(PARTS):
                    upper(2 * PARTS + j, it)
                    gelu(PARTS + j, it)
            choice_exp(1)
            done = POOL_LOW // PARTS - 2
            with loop(a, NEB // PARTS - 1 - done) as it:
                for j in range(PARTS):
                    upper((2 + done) * PARTS + j, it)
                    gelu((1 + done) * PARTS + j, it)

            def coefficients_hi(q, it=0, first=False):
                a.wait_ge(sem("coef_raw"), q + 1 + PARTS // 2 * it)
                if not first:
                    a.wait_ge(sem("expert_used"), NEB + 2 * q - 2 + PARTS * it)
                a.activation(coef_hi[:, q % 2, :], weight_in[:, q % 2, :], ACT.Copy).then_inc(sem("coef_hi_ready"), 1)

            coefficients_hi(0, first=True)
            coefficients_hi(1, first=True)
            for j in range(2):
                upper(NEB + PARTS + j)
            with loop(a, NEB // PARTS - 2) as it:
                for q in range(2):
                    coefficients_hi(2 + q, it)
                    for j in (2 * q, 2 * q + 1):
                        upper(NEB + PARTS + 2 + j, it)
            coefficients_hi(NEB // 2 - 2)
            for j in range(2):
                upper(2 * NEB - 2 + j)
            coefficients_hi(NEB // 2 - 1)
            for t in range(T):
                root(13 + t)

        @block.vector
        def _(v):
            steps = Steps(v, "dve_step")
            link, mark, wait = steps.link, steps.mark, steps.wait
            rms_n = [0]

            def roots(count, eps, n=2, src=0, dst=16, parts=None):
                rms_n[0] += 1
                v.tensor_scalar(st[:, src:src + n], st[:, src:src + n], 1.0 / count, eps, ALU.mult, ALU.add)\
                    .then_inc(sem("rms_in"), 1)
                v.wait_ge(sem("root_out"), rms_n[0])
                got = st[:, 2:4] if n == 2 else st[:, 8:12]
                link(v.reciprocal(st[:, dst:dst + n], got))

            v.memset(ones[:, :], 1.0).then_inc(sem("ones_set"), 1)
            mark(v.memset(xrT[:, :, 0:2], 0.0))
            v.memset(xrT[:, :, 2 + S:XP], 0.0).then_inc(sem("xr_padded"), 1)
            v.wait_ge(sem("cols_in"), 16)
            lam = cols[:, COLS["lam"]:COLS["lam"] + 2 * RB]
            link(v.tensor_scalar(sp[:, 0, :], lam, -1.0, None, ALU.mult))
            v.tensor_tensor(sp[:, 0, :], sp[:, 0, :], lam, ALU.max).then_inc(sem("softplus_in"), 1)
            v.wait_ge(sem("x_in"), 16 * T)
            for t in range(T):
                mark(v.tensor_tensor_reduce(nat[:, t, :], resid[:, t, :], resid[:, t, :], 1.0, 0.0, ALU.mult, ALU.add,
                                            st[:, t:t + 1]))
            wait()
            roots(D, EPS)
            mark(v.tensor_scalar(nat[:, 0, :], resid[:, 0, :], st[:, 16:17], None, ALU.mult))
            wait()
            v.tensor_scalar(nat[:, 1, :], resid[:, 1, :], st[:, 17:18], None, ALU.mult).then_inc(sem("hn_ready"), 1)
            v.wait_ge(sem("softplus_exp"), 1)
            link(v.tensor_scalar(sp[:, 2, :], sp[:, 1, :], 2.0, None, ALU.add))
            link(v.reciprocal(sp[:, 2, :], sp[:, 2, :]))
            link(v.tensor_tensor(sp[:, 1, :], sp[:, 1, :], sp[:, 2, :], ALU.mult))
            link(v.tensor_tensor(sp[:, 2, :], sp[:, 1, :], sp[:, 1, :], ALU.mult))
            link(v.tensor_scalar(sp[:, 3, :], sp[:, 2, :], 1.0 / 17, 1.0 / 15, ALU.mult, ALU.add))
            for m in (13, 11, 9, 7, 5, 3, 1):
                link(v.tensor_tensor(sp[:, 3, :], sp[:, 3, :], sp[:, 2, :], ALU.mult))
                link(v.tensor_scalar(sp[:, 3, :], sp[:, 3, :], 1.0 / m, None, ALU.add))
            link(v.tensor_tensor(sp[:, 3, :], sp[:, 3, :], sp[:, 1, :], ALU.mult))
            link(v.tensor_scalar(sp[:, 3, :], sp[:, 3, :], 8.0, None, ALU.mult))
            link(v.tensor_scalar(sp[:, 0, :], lam, -4.0, 0.0, ALU.mult, ALU.max))
            v.tensor_tensor(sp[:, 3, :], sp[:, 3, :], sp[:, 0, :], ALU.add).then_inc(sem("softplus_in"), 1)
            turn_out(nc.vector, "n1", KD, lambda k: xT[:, k, :], gain("g_mix_pre"))

            cw = lambda j, b: cols[:, COLS["conv_w"] + j * RB + b:COLS["conv_w"] + j * RB + b + 1]
            v.wait_ge(sem("xr_padded"), 1)
            for b in range(RB):
                v.wait_ge(taken, out_no("xr", b) + 1)
                tmp = conv_tmp[:, b % 2, :]
                link(v.tensor_scalar(tmp, xrT[:, b, 0:S], cw(0, b), cols[:, COLS["conv_b"] + b:COLS["conv_b"] + b + 1],
                                     ALU.mult, ALU.add))
                for j in (1, 2):
                    link(v.scalar_tensor_tensor(out=tmp, in0=xrT[:, b, j:j + S], scalar=cw(j, b), in1=tmp,
                                                op0=ALU.mult, op1=ALU.add))
                v.scalar_tensor_tensor(out=xcT[:, b, :], in0=xrT[:, b, 3:3 + S], scalar=cw(3, b), in1=tmp,
                                       op0=ALU.mult, op1=ALU.add).then_inc(sem("conv_done"), 1)
                v.wait_ge(sem("conv_done"), b + 1)

            recA, recB = nat[:, 0, :], nat[:, 1, :]
            recU, recH = aux[:, 0, :], aux[:, 1, :]
            xc2 = xcT.rearrange("p b s -> p (b s)")

            def rec_gates(z):
                v.wait_ge(sem("gates_ready"), z + 1)
                link(v.tensor_scalar(recB, recA, 1.0, None, ALU.add))
                link(v.reciprocal(recB, recB))
                link(v.scalar_tensor_tensor(out=recA, in0=recA, scalar=2.0, in1=recB, op0=ALU.mult, op1=ALU.mult))
                v.scalar_tensor_tensor(out=recB, in0=recA, scalar=-2.0, in1=recA, op0=ALU.add, op1=ALU.mult)\
                    .then_inc(sem("rec_b2"), 1)
                v.wait_ge(sem("rec_b2"), z + 1)
                link(v.tensor_scalar(recA, recA, -1.0, 1.0, ALU.mult, ALU.add))
                link(v.tensor_tensor(recU, recU, xc2, ALU.mult))
                first = 0 if z == 0 else S - 1
                link(v.memset(recA.rearrange("p (b s) -> p b s", b=RB)[:, :, first:first + 1], 0.0))

            def rec_scan(z):
                v.wait_ge(sem("rec_root"), z + 1)
                link(v.tensor_tensor(recB, recB, recU, ALU.mult))
                if z == 0:
                    v.tensor_tensor_scan(recH, recA, recB, 0.0, ALU.mult, ALU.add).then_inc(sem("rec_scan"), 1)
                else:
                    v.tensor_tensor_scan(recU[:, ::-1], recA[:, ::-1], recB[:, ::-1], 0.0, ALU.mult, ALU.add)\
                        .then_inc(sem("rec_scan"), 1)
                v.wait_ge(sem("rec_scan"), z + 1)

            rec_gates(0)
            rec_scan(0)
            rec_gates(1)
            rec_scan(1)
            link(v.tensor_tensor(recH, recH, recU, ALU.add))
            v.wait_ge(taken, out_no("q", 0))
            v.tensor_tensor(recH, recH, ygT.rearrange("p b s -> p (b s)"), ALU.mult).then_inc(sem("rec_sum"), 1)
            v.wait_ge(sem("rec_sum"), 1)

            v.wait_ge(sem("bias_masked"), 4)

            def bias_1(h, t):
                at = 2 - 2 * t
                return bias1[:, h, at:at + 4, ::-1]

            attention_dve(v, steps, "at1", bias_1, float(HD) ** -0.5,
                          lambda h, t: attn1[:, t, h * HD:(h + 1) * HD], scratch1)
            for t in range(T):
                link(v.tensor_tensor_reduce(recB.rearrange("p (a c) -> p a c", a=2)[:, 0, :], attn1[:, t, :],
                                            attn1[:, t, :], 1.0, 0.0, ALU.mult, ALU.add, st[:, t:t + 1]))
            roots(DA, EPS)
            for t in range(T):
                i = v.tensor_scalar(attn1[:, t, :], attn1[:, t, :], st[:, 16 + t:17 + t], None, ALU.mult)
                if t == 0:
                    link(i)
            i.then_inc(sem("attn1_ready"), 1)
            turn_out(nc.vector, "n2", 8, lambda k: xT[:, k, :], gain("g_attn_out"))
            v.wait_ge(sem("rec_norm"), 1)
            v.tensor_scalar(conv_tmp[:, 0, :], bank[4][:, 0:S], 1.0 / DA, EPS, ALU.mult, ALU.add).then_inc(
                sem("rec_norm"), 1)
            v.wait_ge(sem("rec_norm"), 3)
            link(v.reciprocal(conv_tmp[:, 1, :], conv_tmp[:, 0, :]))
            for b in range(RB):
                v.scalar_tensor_tensor(out=xT[:, 8 + b, :], in0=recH[:, b * S:(b + 1) * S], scalar=gain("g_rec_out")(b),
                                       in1=conv_tmp[:, 1, :], op0=ALU.mult, op1=ALU.mult).then_inc(
                    sem("rec_normed"), 1)
            v.wait_ge(sem("rec_normed"), RB)
            v.memset(mxs[:, 0, 0:1], 0.0).then_inc(sem("ada_used"), ADA_SLOTS)
            v.wait_ge(sem("ada_used"), ADA_SLOTS)
            v.memset(mxs[:, 0, 0:1], 0.0).then_inc(sem("aux_free"), 1)

            def sum_ssq():
                link(v.tensor_reduce(st[:, 0:2], ssq[:, :, :], AXX, ALU.add))

            def add_normed(row, n0):
                for t in range(T):
                    for c in range(4):
                        s = slice(c * BAND, (c + 1) * BAND)
                        link(v.scalar_tensor_tensor(out=nat[:, t, s], in0=nat[:, t, s], scalar=st[:, 16 + t:17 + t],
                                                    in1=row[:, s], op0=ALU.mult, op1=ALU.mult))
                        v.tensor_tensor(resid[:, t, s], resid[:, t, s], nat[:, t, s], ALU.add).then_inc(
                            sem("resid_piece"), 1)
                v.wait_ge(sem("resid_piece"), n0 + 8)

            def normed(n, name, g):
                v.wait_ge(sem("ssq_in"), n)
                sum_ssq()
                roots(D, EPS)
                link(v.tensor_scalar(nat[:, 0, :], resid[:, 0, :], st[:, 16:17], None, ALU.mult))
                v.tensor_scalar(nat[:, 1, :], resid[:, 1, :], st[:, 17:18], None, ALU.mult).then_inc(sem("hn_ready"), 1)
                turn_out(nc.vector, name, KD, lambda k: xT[:, k, :], gain(g))

            v.wait_ge(taken, out_no("gateup", 0))
            sum_ssq()
            roots(D, EPS)
            v.wait_ge(sem("row_in"), 16)
            add_normed(aux[:, 0, :], 0)
            normed(8, "n3", "g_ffn_pre")
            wait()

            v.wait_ge(sem("cact_ready"), 1)

            def hidden(j, it):
                v.wait_ge(sem("silu_done"), it * 4 + j + 1)
                wait_multiplied(v, "gateup", 2 * j + 1, it, 8)
                v.tensor_tensor(big[:, bass.ds(j * S + it * 4 * S, S)], out_bank("gateup", 2 * j + 1)[:, 0:S],
                                silu_g[:, j % 2, :], ALU.mult).then_inc(taken, 2)

            def ada(k, g):
                s = k % ADA_SLOTS
                v.wait_ge(ada_loaded[s], 16 * (KD // ADA_SLOTS) * g + 16 * (k // ADA_SLOTS + 1))
                if k == 0:
                    i = v.tensor_scalar(ada_acc, ada_ring[:, s, :], cact[:, k:k + 1], None, ALU.mult)
                else:
                    v.wait_ge(sem("ada_used"), ADA_SLOTS + KD * g + k)
                    i = v.scalar_tensor_tensor(out=ada_acc, in0=ada_ring[:, s, :], scalar=cact[:, k:k + 1],
                                               in1=ada_acc, op0=ALU.mult, op1=ALU.add)
                i.then_inc(sem("ada_used"), 1)

            def ada_end(g):
                v.wait_ge(sem("ada_used"), ADA_SLOTS + KD * g + KD)
                v.memset(mxs[:, 0, 1:2], 0.0).then_inc(sem("ada_sum"), 1)

            def ada_row(g):
                v.wait_ge(sem("ada_rowsum"), g + 1)
                v.wait_ge(sem("mod_b_in"), 16 * g + 16)
                for c in range(2):
                    i = v.tensor_tensor(mod_row[0:1, c * BAND:(c + 1) * BAND], bank[4 + c][0:1, :],
                                        mod_row[0:1, c * BAND:(c + 1) * BAND], ALU.add)
                    if c == 0:
                        mark(i)
                    else:
                        i.then_inc(sem("mod_ready"), 1)
                wait()

            wait_turned_out(v, "n3", KD)
            with steps.loop(KF // 4, 1) as it:
                for j in range(4):
                    hidden(j, it)
                    for k in range(4 * j, 4 * j + 4):
                        ada(k, it)
                ada_end(it)
                ada_row(it)
            for k in range(KD):
                ada(k, ADA_G - 1)
            ada_end(ADA_G - 1)
            ada_row(ADA_G - 1)

            v.wait_ge(taken, out_no("pproj", 0))
            sum_ssq()
            roots(D, EPS)
            v.wait_ge(sem("row2_in"), 16)
            add_normed(aux[:, 1, :], 8)
            v.memset(mxs[:, 0, 0:1], 0.0).then_inc(row_used, 1)
            normed(16, "n4", "g_ple_pre")
            v.wait_ge(taken, out_no("lat", 0))
            for t in range(T):
                v.tensor_tensor(nat[:, t, :], nat[:, t, :], ple[:, t, :], ALU.mult).then_inc(sem("pgate_sig"), 1)
            v.wait_ge(sem("ple_ready"), 4 * T)
            sum_ssq()
            roots(D, EPS)
            v.wait_ge(sem("row3_in"), 16)
            add_normed(aux[:, 0, :], 16)

            def layer_stats(n, t0=0, tn=T):
                for t in range(t0, tn):
                    for c in range(4):
                        mark(v.bn_stats(stats[:, t, c, :], resid[:, t, c * BAND:(c + 1) * BAND]))
                wait()
                for t in range(t0, tn):
                    mark(v.bn_aggr(mv[:, t, :], stats[:, t, :, :].rearrange("p c s -> p (c s)")))
                wait()
                rms_n[0] += 1
                if tn - t0 == T:
                    v.tensor_scalar(st[:, 0:2], mv[:, :, 1:2].rearrange("p t o -> p (t o)"), EPS_LN, None, ALU.add)\
                        .then_inc(sem("rms_in"), 1)
                else:
                    v.tensor_scalar(st[:, 0:2], mv[:, :, 1:2].rearrange("p t o -> p (t o)"), EPS_LN, None, ALU.add)\
                        .then_inc(sem("rms_in"), 1)
                v.wait_ge(sem("root_out"), rms_n[0])
                link(v.reciprocal(st[:, 16:18], st[:, 2:4]))

            def layer_normed(dst, t):
                return v.tensor_scalar(dst[:, t, :], resid[:, t, :], mv[:, t, 0:1], st[:, 16 + t:17 + t],
                                       ALU.subtract, ALU.mult)

            v.wait_ge(sem("modc_in"), 32)
            v.tensor_scalar(modc[:, 0, :], modc[:, 0, :], 1.0, None, ALU.add).then_inc(sem("modc_ready"), 1)
            layer_stats(0)
            link(layer_normed(nat, 0))
            layer_normed(nat, 1).then_inc(sem("hn_ready"), 1)
            v.wait_ge(sem("modc_ready"), 1)
            turn_out(nc.vector, "n5", KD, lambda k: xT[:, k, :], lambda k: modc[:, 0, k:k + 1],
                     lambda k: modc[:, 1, k:k + 1])
            v.wait_ge(taken, out_no("kr", 0))
            link(v.tensor_copy(st[:, 4:8].rearrange("p (t c) -> p t c", t=T), ssq[:, :, 0:2]))
            rms_n[0] += 1
            v.tensor_scalar(st[:, 4:8], st[:, 4:8], 1.0 / LAT, EPS, ALU.mult, ALU.add).then_inc(sem("rms_in"), 1)
            v.wait_ge(sem("root_out"), rms_n[0])
            link(v.reciprocal(st[:, 20:24], st[:, 8:12]))
            for t in range(T):
                for c in range(2):
                    i = v.tensor_scalar(lat[:, t, c * LAT:(c + 1) * LAT], lat[:, t, c * LAT:(c + 1) * LAT],
                                        st[:, 20 + 2 * t + c:21 + 2 * t + c], None, ALU.mult)
                    if t == T - 1 and c == 1:
                        i.then_inc(sem("lat_ready"), 1)
                    else:
                        link(i)

            def rope(view, heads, half, tab, scr):
                n = heads * half
                for t in range(T):
                    x = view(t)
                    x1, x2 = x[:, :, 0:half], x[:, :, half:2 * half]
                    cos = rope_t[:, t, tab:tab + half].unsqueeze(1).to_broadcast([P, heads, half])
                    sin = rope_t[:, t, tab + half:tab + 2 * half].unsqueeze(1).to_broadcast([P, heads, half])
                    w = [scr[:, i * 288:i * 288 + n].rearrange("p (h c) -> p h c", h=heads) for i in range(4)]
                    for dst, p, q in ((w[0], x1, cos), (w[1], x2, sin), (w[2], x2, cos), (w[3], x1, sin)):
                        mark(v.tensor_tensor(dst, p, q, ALU.mult))
                    wait()
                    mark(v.tensor_tensor(x1, w[0], w[1], ALU.subtract))
                    mark(v.tensor_tensor(x2, w[2], w[3], ALU.add))
                    wait()

            turn_out(nc.vector, "n6", 2 * KL, lambda k: latT[:, k, :], gain("g_q_lat"))
            v.wait_ge(taken, out_no("v2", 0))
            rope(lambda t: qkv2[:, t, 0:2 * DA].rearrange("p (h c) -> p h c", h=2 * NH), 2 * NH, ROT_A, 0, auxf)
            v.memset(mxs[:, 0, 0:1], 0.0).then_inc(sem("rope_done"), 1)
            turn_out(nc.vector, "tq", 2 * NH, lambda k: natT[:, k, :])
            v.wait_ge(taken, out_no("mla", 10))
            rope(lambda t: rot[:, t, :].rearrange("p (h c) -> p h c", h=9), 9, ROT_B, 2 * ROT_A,
                 xT[:, :, :].rearrange("p k s -> p (k s)"))
            v.memset(mxs[:, 0, 0:1], 0.0).then_inc(sem("rotq_ready"), 1)
            turn_out(nc.vector, "tr", 9, lambda k: rotT[0:64, k, :], width=64)
            v.wait_ge(sem("misc_in"), 16)
            attention_dve(v, steps, "at2", lambda h, t: by_row(masks[:, 0, t, :]), float(HD) ** -0.5,
                          lambda h, t: o2[:, t, h * HD:(h + 1) * HD], scratch2)
            attention_dve(v, steps, "at3", lambda h, t: by_row(masks[:, 1, t, :]), float(HD + 64) ** -0.5,
                          lambda h, t: o2[:, t, DA + h * HD:DA + (h + 1) * HD], scratch2)
            for t in range(T):
                for c in range(2):
                    link(v.tensor_tensor_reduce(auxf[:, 0:DA], o2[:, t, c * DA:(c + 1) * DA],
                                                o2[:, t, c * DA:(c + 1) * DA], 1.0, 0.0, ALU.mult, ALU.add,
                                                st[:, 4 + 2 * t + c:5 + 2 * t + c]))
            rms_n[0] += 1
            v.tensor_scalar(st[:, 4:8], st[:, 4:8], 1.0 / DA, EPS, ALU.mult, ALU.add).then_inc(sem("rms_in"), 1)
            v.wait_ge(sem("root_out"), rms_n[0])
            link(v.reciprocal(st[:, 20:24], st[:, 8:12]))
            for t in range(T):
                for c in range(2):
                    link(v.tensor_scalar(o2[:, t, c * DA:(c + 1) * DA], o2[:, t, c * DA:(c + 1) * DA],
                                         st[:, 20 + 2 * t + c:21 + 2 * t + c], None, ALU.mult))
            v.memset(mxs[:, 0, 0:1], 0.0).then_inc(sem("o_ready"), 1)
            turn_out(nc.vector, "n7", KD, lambda k: natT[:, k, :], gain("g_out_a"))

            v.wait_ge(taken, out_no("pq", 0))
            v.wait_ge(sem("rows_in"), 16 * 5)

            mixer_rows = [rows[:, n, :] for n in range(3)]

            def deep_norm(t, mix, r):
                link(v.tensor_tensor(mix, mix, r[0], ALU.mult))
                link(v.scalar_tensor_tensor(out=resid[:, t, :], in0=resid[:, t, :], scalar=ALPHA, in1=mix,
                                            op0=ALU.mult, op1=ALU.add))

            def scaled(t, r):
                link(layer_normed(resid, t))
                link(v.tensor_tensor(resid[:, t, :], resid[:, t, :], r[1], ALU.mult))
                return v.tensor_tensor(resid[:, t, :], resid[:, t, :], r[2], ALU.add)

            for t in range(T):
                deep_norm(t, o2[:, t, :], mixer_rows)
            layer_stats(1)
            for t in range(T):
                link(scaled(t, mixer_rows))
            layer_stats(2)
            for t in range(T):
                link(layer_normed(nat, t))
                link(v.scalar_tensor_tensor(out=nat[:, t, :], in0=rows[:, 3, :], scalar=1.0, in1=nat[:, t, :],
                                            op0=ALU.add, op1=ALU.mult))
                link(v.tensor_tensor(nat[:, t, :], nat[:, t, :], rows[:, 4, :], ALU.add))
            v.memset(conv_tmp[:, :, :], 0.0).then_inc(sem("zeros_set"), 1)
            v.memset(mxs[:, 0, 0:1], 0.0).then_inc(sem("h2_ready"), 1)
            v.wait_ge(sem("h2_ready"), 1)
            v.memset(mxs[:, 0, 0:1], 0.0).then_inc(sem("score_out"), 2)
            turn_out(nc.vector, "n8", KD, lambda k: xT[:, k, :])

            for n in range(4):
                v.wait_ge(sem("h2_hi_ready"), n + 1)
                link(v.tensor_tensor(h2_lo[:, 4 * n:4 * n + 4, :], xT[:, 4 * n:4 * n + 4, :],
                                     h2_hi[:, 4 * n:4 * n + 4, :].bitcast(F32), ALU.subtract))
            v.memset(mxs[:, 0, 0:1], 0.0).then_inc(sem("h2_lo_ready"), 1)

            def top16(vals, idxs, src, tmp):
                link(v.max(vals[:, 0:8], src))
                link(v.max_index(idxs[:, 0:8], vals[:, 0:8], src))
                link(v.match_replace(out=tmp, in_to_replace=vals[:, 0:8], in_values=src, imm_value=-3.0e38))
                link(v.max(vals[:, 8:16], tmp))
                return v.max_index(idxs[:, 8:16], vals[:, 8:16], tmp)

            v.wait_ge(sem("iota_done"), 2)
            for t in range(T):
                link(v.tensor_scalar(token[:, t:t + 1], tokbase, float(t * P), None, ALU.add))
            for it in range(2):
                for j in range(8):
                    v.wait_ge(sem("score_out"), 2 + it * 8 + j + 1)
                    for t in range(T):
                        link(top16(tk_v12[:, t, j // 2, j % 2, :], tk_i12[:, t, j // 2, j % 2, :],
                                   score[:, it * 8 + j, t * P:(t + 1) * P], tk_tmp[:, 0:P]))
                link(v.tensor_copy(auxf[:, 512:768], auxf[:, 256:512].bitcast(U32)))
                for t in range(T):
                    link(v.tensor_tensor(tk_cand, tk_v12[:, t, :, 0, :].unsqueeze(3).to_broadcast([P, 4, 16, 16]),
                                         tk_v12[:, t, :, 1, :].unsqueeze(2).to_broadcast([P, 4, 16, 16]), ALU.add))
                    for h in range(4):
                        link(top16(tk_val[:, t, h, :], tk_ci[:, t, h, :],
                                   tk_cand[:, h].rearrange("p i j -> p (i j)"), tk_tmp))
                ci = tk_ci.rearrange("p t h k -> p (t h k)")
                link(v.tensor_scalar(tk_ab[:, 0, :], ci, 4, None, ALU.logical_shift_right))
                link(v.tensor_scalar(tk_ab[:, 1, :], ci, 15, None, ALU.bitwise_and))
                link(v.tensor_copy(auxf[:, 2560:2816], auxf[:, 2304:2560].bitcast(U32)))
                for t in range(T):
                    for a_ in range(2):
                        link(v.tensor_tensor(tk_hot, tk_abf[:, a_, t].rearrange("p h k -> p (h k)").unsqueeze(2)
                                             .to_broadcast([P, 64, 16]),
                                             iota16.unsqueeze(1).to_broadcast([P, 64, 16]), ALU.is_equal))
                        hot4 = tk_hot.rearrange("p (h o) k -> p h o k", h=4)
                        link(v.tensor_tensor(hot4, hot4, tk_f12[:, t, :, a_, :].unsqueeze(2)
                                             .to_broadcast([P, 4, 16, 16]), ALU.mult))
                        link(v.tensor_reduce(tk_pick[:, a_, :], tk_hot, AXX, ALU.add))
                    link(v.tensor_scalar(tk_pick[:, 1, :], tk_pick[:, 1, :], float(NEB * S), token[:, t:t + 1],
                                         ALU.mult, ALU.add))
                    link(v.scalar_tensor_tensor(out=tk_pick[:, 0, :], in0=tk_pick[:, 0, :], scalar=float(S),
                                                in1=tk_pick[:, 1, :], op0=ALU.mult, op1=ALU.add))
                    link(v.tensor_copy(gidx[:, t, it * 64:it * 64 + 64], tk_pick[:, 0, :]))
                val8 = tk_val.rearrange("p t h k -> p (t h) k")
                v.tensor_tensor(tk_abf[:, 0].rearrange("p t h k -> p (t h) k"), val8,
                                val8[:, :, 0:1].to_broadcast([P, T * 4, 16]), ALU.subtract).then_inc(
                    sem("topk_exp_in"), 1)
                v.wait_ge(sem("topk_exp_out"), it + 1)
                link(v.tensor_reduce(tk_sum[:, 0:8], val8, AXX, ALU.add))
                link(v.reciprocal(tk_sum[:, 8:16], tk_sum[:, 0:8]))
                link(v.tensor_tensor(val8, val8, tk_sum[:, 8:16].unsqueeze(2).to_broadcast([P, 8, 16]), ALU.mult))
                link(v.tensor_copy(gwt[:, :, it * 64:it * 64 + 64], tk_val.rearrange("p t h k -> p t (h k)")))
            v.memset(mxs[:, 0, 0:1], 0.0).then_inc(sem("chosen"), 1)

            def lower(j, it=0):
                v.wait_ge(sem("hi_ready"), j + 1 + PARTS * it)
                v.tensor_tensor(part_lo[j % PARTS], raw[j % RAW],
                                part_hi[j % PARTS].bitcast(F32), ALU.subtract).then_inc(sem("lo_ready"), 1)

            def coefficients(q, it=0):
                v.wait_ge(pair_loaded[q % 2], 32 * (q // 2 + 1) + 32 * it)
                v.tensor_tensor(weight_in[:, q % 2, :], weight_in[:, q % 2, :], gelu_in[:, q % 2, :], ALU.mult)\
                    .then_inc(sem("coef_raw"), 1)

            def coefficients_lo(q, it=0):
                v.wait_ge(sem("coef_hi_ready"), q + 1 + PARTS // 2 * it)
                v.tensor_tensor(coef_lo[:, q % 2, :], weight_in[:, q % 2, :], coef_hi[:, q % 2, :].bitcast(F32),
                                ALU.subtract).then_inc(sem("coef_ready"), 1)

            v.wait_ge(sem("lo_ready"), POOL_LOW)
            with loop(v, (NEB - POOL_LOW) // PARTS + 1) as it:
                for j in range(PARTS):
                    lower(POOL_LOW + j, it)
            coefficients(0)
            coefficients_lo(0)
            with loop(v, NEB // PARTS - 1) as it:
                for q in range(2):
                    coefficients(q + 1, it)
                    coefficients_lo(q + 1, it)
                    lower(NEB + PARTS + 2 * q, it)
                    lower(NEB + PARTS + 2 * q + 1, it)
            coefficients(NEB // 2 - 1)
            coefficients_lo(NEB // 2 - 1)
            v.wait_ge(sem("expert_used"), 2 * NEB)
            for t in range(T):
                for c in range(D // BAND):
                    v.tensor_copy(result[:, t, c * BAND:(c + 1) * BAND], bank[4 * t + c][:, :]).then_inc(
                        sem("result_out"), 1)
                v.wait_ge(sem("result_out"), 4 * (t + 1))
                if t == 0:
                    v.wait_ge(sem("rows2_in"), 48)
                deep_norm(t, result[:, t, :], last_rows)
                layer_stats(3 + t, t, t + 1)
                scaled(t, last_rows).then_inc(sem("out_ready"), 1)
                v.wait_ge(sem("out_ready"), t + 1)

        @block.gpsimd
        def _(g_):
            steps = Steps(g_, "pool_step")
            g_.dma_start(cols[:, :], io["cols"]).then_inc(sem("cols_in"), 16)
            g_.dma_start(ident[:, :], io["ident"]).then_inc(sem("consts_in"), 16)
            g_.dma_start(rope_t[:, :, :], io["rope"]).then_inc(sem("consts_in"), 16)
            g_.dma_start(pT[:, :, :], io["pT"]).then_inc(sem("consts_in"), 16)
            g_.dma_start(rg_w.rearrange("p z g b c -> p (z g b c)"), io["rg"]).then_inc(sem("rg_in"), 16)
            rp = io["rpb"]
            NR, NCC = 2 * WIN_R - 1, 2 * WIN_C - 1
            for half in range(2):
                for h in range(NH):
                    src = bass.AP(tensor=rp.tensor,
                                  offset=h * NR * NCC + (WIN_R - ROWS + 1 - half) * NCC + WIN_C - GRID_W,
                                  ap=[[1, GRID_W], [NCC, 6], [1, GRID_W]])
                    g_.dma_start(bias1[GRID_W * half:GRID_W * (half + 1), h], src).then_inc(sem("bias_in"), 16)
            g_.wait_ge(sem("bias_in"), 16 * 2 * NH)
            for half in range(2):
                q = slice(GRID_W * half, GRID_W * (half + 1))
                rest = GRID_W - WIN_C
                lo = bias1[q, :, :, WIN_C:GRID_W].rearrange("p h r c -> p (h r) c")
                hi = bias1[q, :, :, 0:rest].rearrange("p h r c -> p (h r) c")
                g_.affine_select(out=lo, in_=lo, compare_op=ALU.is_ge, fill=-1e9,
                                 base=rest - 1 + WIN_C // 2, pattern=[[0, NH * 6], [-1, rest]], channel_multiplier=-1).then_inc(
                    sem("bias_masked"), 1)
                g_.wait_ge(sem("bias_masked"), 2 * half + 1)
                g_.affine_select(out=hi, in_=hi, compare_op=ALU.is_ge, fill=-1e9,
                                 base=WIN_C // 2 - GRID_W, pattern=[[0, NH * 6], [1, rest]], channel_multiplier=1).then_inc(
                    sem("bias_masked"), 1)
                g_.wait_ge(sem("bias_masked"), 2 * half + 2)

            def row_in(dst, name, s, dram=None):
                src = io["rows"][ROW_NAMES.index(name):ROW_NAMES.index(name) + 1, :] if dram is None else dram
                g_.dma_start(dst, src.to_broadcast([P, D])).then_inc(s, 16)

            g_.wait_ge(sem("aux_free"), 1)
            row_in(aux[:, 0, :], "g_mix_post", sem("row_in"))
            row_in(aux[:, 1, :], "g_ffn_post", sem("row2_in"))

            def mod_piece(g):
                at = bass.ds(g * ADA_W, ADA_W) if not isinstance(g, int) else slice(g * ADA_W, (g + 1) * ADA_W)
                flat = mod_dram.rearrange("(o m) d -> o (m d)", o=1)
                if not isinstance(g, int):
                    g_.wait_ge(sem("mod_out"), 16 * g)
                    g_.nop(nofuse=True)
                g_.dma_start(mod_row[0:1, :], io["b_ada"][:, at]).then_inc(sem("mod_b_in"), 16)
                g_.wait_ge(sem("mod_ready"), g + 1)
                g_.nop(nofuse=True)
                g_.dma_start(flat[:, at], mod_row[0:1, :]).then_inc(sem("mod_out"), 16)

            mod_piece(0)
            with loop(g_, ADA_G - 1) as it:
                mod_piece(it + 1)
            g_.wait_ge(sem("mod_out"), 16 * ADA_G)
            with nc.allow_non_contiguous_dma(reason="two short vectors by channel"):
                for n, m in enumerate((SC1, SH1)):
                    g_.dma_start(modc[:, n, :], mod_dram[m].rearrange("(k p) -> p k", p=P)).then_inc(
                        sem("modc_in"), 16)
            g_.wait_ge(row_used, 1)
            row_in(aux[:, 0, :], "g_ple_post", sem("row3_in"))
            g_.wait_ge(sem("lat_ready"), 1)
            g_.dma_start(masks.rearrange("p m t k -> p (m t k)"), io["masks"]).then_inc(sem("misc_in"), 16)
            g_.wait_ge(sem("at3_out"), NH)
            g_.dma_start(subk.rearrange("p a k -> p (a k)"), io["subk"]).then_inc(sem("sk_in"), 16)
            g_.iota(iota16, [[1, 16]], base=0, channel_multiplier=0, allow_small_or_imprecise_dtypes=True).then_inc(
                sem("iota_done"), 1)
            g_.iota(tokbase, [[0, 1]], base=0, channel_multiplier=1, allow_small_or_imprecise_dtypes=True).then_inc(
                sem("iota_done"), 1)
            for n, (name, m) in enumerate(((None, G1), ("ln1_g", 0), ("ln1_b", 0), (None, SC2), (None, SH2))):
                row_in(rows[:, n, :], name, sem("rows_in"), mod_dram[m:m + 1, :] if name is None else None)
            g_.wait_ge(sem("zeros_set"), 1)
            g_.dma_start(weight_dram.rearrange("p (a c) -> p a c", c=2 * S),
                         conv_tmp[:, :, :].rearrange("p a s -> p (a s)").unsqueeze(1)
                         .to_broadcast([P, NEB // 2, 2 * S])).then_inc(sem("scattered"), 16)

            g_.wait_ge(sem("h2_lo_ready"), 1)
            for j in range(POOL_LOW):
                g_.wait_ge(sem("hi_ready"), j + 1)
                g_.tensor_tensor(part_lo[j % PARTS], raw[j % RAW],
                                 part_hi[j % PARTS].bitcast(F32), ALU.subtract).then_inc(sem("lo_ready"), 1)

            g_.wait_ge(sem("chosen"), 1)
            places = weight_dram.rearrange("p (c o) -> (p c) o", o=1)
            with loop(g_, NH) as it:
                g_.wait_ge(sem("scattered"), 16 + 16 * T * TOPK * it)
                g_.nop(nofuse=True)
                for t in range(T):
                    of_head = bass.ds(it * TOPK, TOPK)
                    g_.tensor_copy(gstage[:, t, :], gidx[:, t, of_head]).then_inc(sem("staged"), 1)
                    g_.tensor_copy(wstage[:, t, :], gwt[:, t, of_head]).then_inc(sem("staged"), 1)
                g_.wait_ge(sem("staged"), 2 * T + 2 * T * it)
                g_.nop(nofuse=True)
                for t in range(T):
                    for k in range(TOPK):
                        g_.indirect_dma_start(
                            out=places, out_offset=bass.IndirectOffsetOnAxis(ap=gstage[:, t, k:k + 1], axis=0),
                            in_=wstage[:, t, k:k + 1], in_offset=None, compute_op=ALU.add).then_inc(
                                sem("scattered"), 16)

            g_.wait_ge(sem("scattered"), 16 + 16 * T * NSEL)
            for b in range(2):
                g_.wait_ge(gelu_stored[b], 16 * NEB // 4)

            def load_pair(q, it=0):
                at = slice(2 * q * S, (2 * q + 2) * S) if isinstance(it, int) else \
                    bass.ds((2 * q + PARTS * it) * S, 2 * S)
                g_.dma_start(weight_in[:, q % 2, :], weight_dram[:, at]).then_inc(pair_loaded[q % 2], 16)
                g_.dma_start(gelu_in[:, q % 2, :], gelu_dram[:, at]).then_inc(pair_loaded[q % 2], 16)

            for q in range(2):
                load_pair(q)
            with loop(g_, NEB // PARTS - 1) as it:
                for q in range(2):
                    g_.wait_ge(sem("coef_ready"), q + 1 + PARTS // 2 * it)
                    g_.nop(nofuse=True)
                    load_pair(2 + q, it)

            g_.wait_ge(sem("lo_ready"), 2 * NEB)
            for n, (name, m) in enumerate(((None, G2), ("ln2_g", 0), ("ln2_b", 0))):
                row_in(last_rows[n], name, sem("rows2_in"), mod_dram[m:m + 1, :] if name is None else None)


def arrange(inputs):
    f = {k: np.asarray(v) for k, v in inputs.items()}

    def stationary(w):
        n = w.shape[1] // P
        return w.reshape(KD, P, n, P).transpose(2, 1, 0, 3).reshape(n, P, CH)

    def moving(w, kq=4):
        n = w.shape[1] // BAND
        q = w.shape[0] // (kq * P)
        return w.reshape(q, kq, P, n, BAND).transpose(3, 0, 2, 1, 4).reshape(n * q, P, kq * BAND)

    def stationary_lat(w):
        return w.reshape(KL, P, 2, 4, P).transpose(2, 1, 3, 0, 4).reshape(2, P, CH)

    w_in = f["w_in"][0]
    q, k, v, xr, yg = (w_in[:, i * DA:(i + 1) * DA] for i in range(5))
    gate_up = np.stack([stationary(f["w_ffn_gate"][0]), stationary(f["w_ffn_up"][0])], 1).reshape(-1, P, CH)
    pproj = f["w_ple_proj"][0].reshape(2, P, 2, 2, BAND).transpose(2, 1, 3, 0, 4).reshape(2, P, CH)
    w2 = f["w_in_2"][0]
    qkv2, lat, kr = w2[:, :3 * DA], w2[:, 3 * DA:3 * DA + 2 * LAT], w2[:, 3 * DA + 2 * LAT:]
    kr_chunk = np.zeros((1, P, CH), w2.dtype)
    kr_chunk[0, :, :KD * 64] = kr.reshape(KD, P, 64).transpose(1, 0, 2).reshape(P, KD * 64)
    uq = f["w_uq_2"][0].reshape(LAT, NH, HD + 64)
    parts = [stationary(xr), stationary(yg), stationary(q), stationary(k), moving(v), moving(f["w_out"][0]), gate_up,
             pproj, moving(f["w_ple_gate"][0]), moving(lat), kr_chunk, moving(qkv2[:, :2 * DA]),
             moving(qkv2[:, 2 * DA:]), stationary_lat(uq[:, :, :HD].reshape(LAT, DA)),
             moving(uq[:, :, HD:].reshape(LAT, 512)), stationary_lat(f["w_uk_2"][0]), moving(f["w_uv_2"][0]),
             moving(f["w_o_2"][0]), stationary(f["w_pq_2"][0])]
    a = {"stream": np.concatenate(parts), "down": moving(f["w_ffn_down"][0], 11)}
    vec = {"g_mix_pre": "g_mix_pre", "g_attn_out": "g_attn_out", "g_rec_out": "g_rec_out", "g_ffn_pre": "g_ffn_pre",
           "g_ple_pre": "g_ple_pre", "g_q_lat": "g_q_lat_2", "g_kv_lat": "g_kv_lat_2", "g_out_a": "g_out_a_2",
           "g_out_b": "g_out_b_2", "conv_w": "conv_w", "conv_b": "conv_b", "b_rg_a": "b_rg_a", "b_rg_i": "b_rg_i",
           "lam": "lam", "c": "c_2"}
    a["cols"] = np.ascontiguousarray(np.concatenate([f[vec[n]].reshape(-1, P) for n in COLS], 0).T)
    a["rows"] = np.concatenate([f[n if n in f else n + "_2"].reshape(1, D) for n in ROW_NAMES], 0)
    a["rg"] = np.ascontiguousarray(np.stack([f["w_rg_a"][0], f["w_rg_i"][0]], 1).transpose(3, 0, 1, 2, 4)).reshape(P, -1)
    a["rpb"] = f["rpb"][0][:, :, ::-1]
    a["pT"] = np.ascontiguousarray(f["p"][0, 0].T.reshape(2, P, S).transpose(1, 0, 2))
    a["x"] = f["x"]
    a["w_ada"] = f["w_ada_2"][0]
    a["b_ada"] = f["b_ada_2"]
    a["subk"] = np.ascontiguousarray(np.stack([f["sub_key_1_2"][0].T, f["sub_key_2_2"][0].T], 1)).reshape(P, -1)
    a["u_table"] = stationary(f["u_table_2"][0].T)
    a["v_table"] = f["v_table_2"][0].reshape(NEB, P, D)
    a.update(shape_tables())
    return {k: np.ascontiguousarray(v) for k, v in a.items()}


def shape_tables():
    pos = np.arange(S, dtype=np.float32)
    rope = []
    for half in (ROT_A, ROT_B):
        inv = np.float32(500000.0) ** (-np.arange(half, dtype=np.float32) * np.float32(2.0) / np.float32(2 * half))
        ang = (pos[:, None] * inv[None, :].astype(np.float32)).astype(np.float32)
        rope += [np.cos(ang), np.sin(ang)]
    rope = np.concatenate(rope, 1).astype(np.float32).reshape(T, P, -1).transpose(1, 0, 2)
    dist = np.arange(S)[:, None] - np.arange(S)[None, :]
    count = sum(((dist >= 0) & (dist % dil == 0) & (dist <= window)).astype(np.int64)
                for window, dil in ((128, 1), (512, 4), (2048, 16)))
    log_count = np.where(count > 0, np.log(np.maximum(count, 1)), NEG)
    causal = np.where(dist >= 0, 0.0, NEG)
    masks = np.stack([log_count, causal]).astype(np.float32).reshape(2, T, P, S).transpose(2, 0, 1, 3)
    return {"ident": np.eye(P, dtype=np.float32), "rope": np.ascontiguousarray(rope),
            "masks": np.ascontiguousarray(masks).reshape(P, -1)}


def kernel(**inputs):
    import concourse.bacc as bacc
    from concourse.bass_utils import run_bass_kernel_spmd

    nc = bacc.Bacc("TRN2", target_bir_lowering=False, num_devices=1)
    arrays = {f"in_{n}": a for n, a in arrange(inputs).items()}
    io = {n[3:]: nc.dram_tensor(n, a.shape, mybir.dt.from_np(a.dtype), kind="ExternalInput").ap()
          for n, a in arrays.items()}
    io["out"] = nc.dram_tensor("out", (1, S, D), F32, kind="ExternalOutput").ap()
    build_program(nc, io)
    r = run_bass_kernel_spmd(nc, [arrays], core_ids=[0])
    return r.results[0]["out"]
```

```python
from contextlib import ExitStack, contextmanager

import numpy as np

import concourse.bass as bass
from concourse import mybir

ALU = mybir.AluOpType
ACT = mybir.ActivationFunctionType
AXX = mybir.AxisListType.X
F32 = mybir.dt.float32
F32R = mybir.dt.float32r
I32 = mybir.dt.int32
U32 = mybir.dt.uint32

P = 128
S = 256
T = S // P
D = 2048
KD = D // P
HD = 128
NH = 8
DA = NH * HD
GRID_W, ROWS = 64, S // 64
WIN_R, WIN_C = 8, 16
RB = 8
CONV = 4
FF = 5632
KF = FF // P
EPS, EPS_LN = 1e-6, 1e-5
ALPHA = 2.0 ** 0.25
ROT_A, ROT_B = 16, 32
LAT = 512
KL = LAT // P
NKEY = 128
TOPK = 16
NSEL = NH * TOPK
NEXP = NKEY * NKEY
NEB = NEXP // P
RAW = 4
PARTS = 4
POOL_LOW = 24
NEG = -1e30
BAND = 512

CH = 2048
SLOTS = 8
BCH = 11 * BAND
BSLOTS = 2
ADA_W = 512
ADA_G = 6 * D // ADA_W
ADA_EARLY = 4
ADA_FFN = ADA_EARLY + KF // 4
ADA_SLOTS = 8

PHASES = [("xr", 8), ("yg", 8), ("q", 8), ("k", 8), ("v", 8), ("wout", 16), ("gateup", 2 * KF), ("down", 16),
          ("pproj", 2), ("pgate", 16), ("lat", 8), ("kr", 1), ("qk2", 16), ("v2", 8), ("mla", 7), ("wo", 16),
          ("pq", 16)]
OUTPUTS = {"xr": 8, "yg": 8, "q": 8, "k": 8, "v": 4, "wout": 8, "gateup": 88, "down": 8, "pproj": 8, "pgate": 8, "lat": 4,
           "kr": 2, "qk2": 8, "v2": 4, "mla": 8 + 2 + 8 + 4, "wo": 8, "pq": 16}

COLS = {}
_at = 0
for _n, _w in [("g_mix_pre", KD), ("g_attn_out", 8), ("g_rec_out", 8), ("g_ffn_pre", KD), ("g_ple_pre", KD),
               ("g_q_lat", KL), ("g_kv_lat", KL), ("g_out_a", 8), ("g_out_b", 8), ("conv_w", CONV * RB),
               ("conv_b", RB), ("b_rg_a", 2 * RB), ("b_rg_i", 2 * RB), ("lam", 2 * RB), ("c", KD)]:
    COLS[_n] = _at
    _at += _w
NCOLS = _at
ROW_NAMES = ["g_mix_post", "g_ffn_post", "g_ple_post", "ln1_g", "ln1_b", "ln2_g", "ln2_b"]
SH1, SC1, G1, SH2, SC2, G2 = range(6)


def stream_plan():
    plan, chunk, small, out = {}, 0, 0, 0
    for name, n in PHASES:
        plan[name] = dict(chunk=chunk, small=small, out=out, n=n)
        chunk += n
        out += OUTPUTS[name]
        if name not in ("gateup", "down", "wo", "pq"):
            small += n
    return plan, chunk


def build_program(nc, io):
    PLAN, N_CHUNKS = stream_plan()
    assert all(PLAN[p]["small"] % SLOTS == 0 for p in ("gateup", "down"))

    with ExitStack() as ctx:
        place = {}

        def sb(name, shape, dt=F32):
            place[name] = -(-nc.sbuf_base // 32) * 32
            return ctx.enter_context(nc.sbuf_tensor(name, shape, dt))

        def rounded(name, over, first, words):
            return nc.alloc_sbuf_tensor_at(name, [P, words], F32R, offset=place[over] + 4 * first)

        sems = {}

        def sem(name):
            if name not in sems:
                sems[name] = ctx.enter_context(nc.semaphore(name))
            return sems[name]

        ring = sb("ring", [P, SLOTS * CH])
        resid = sb("resid", [P, T, D])
        nat = sb("nat", [P, T, D])
        xT = sb("xT", [P, KD, S])
        aux = sb("aux", [P, 2, D])
        big = sb("big", [P, KF * S])
        misc = sb("misc", [P, 7168])
        cols = sb("cols", [P, NCOLS])
        ident = sb("ident", [P, P])
        ones = sb("ones", [P, P])
        rope_t = sb("rope_t", [P, T, 2 * (ROT_A + ROT_B)])
        pT = sb("pT", [P, 2, S])
        conv_tmp = sb("conv_tmp", [P, 2, S])
        modc = sb("modc", [P, 2, KD])
        ssq = sb("ssq", [P, T, 4])
        st = sb("st", [P, 32])
        stats = sb("stats", [P, T, 4, 6])
        mv = sb("mv", [P, T, 2])
        sp = sb("sp", [P, 4, 2 * RB])
        mxs = sb("mxs", [P, 2, 2 * T])
        den = sb("den", [P, 2, 2 * T])
        cact = sb("cact", [P, KD])
        bank = [ctx.enter_context(nc.psum_tensor(f"bank{i}", [P, BAND], F32)) for i in range(8)]

        ygT = big[:, 0:2048].rearrange("p (b s) -> p b s", b=RB)
        qkT = big[:, 2048:6144].rearrange("p (b s) -> p b s", b=16)
        v1n = big[:, 6144:8192].rearrange("p (t c) -> p t c", t=T)
        xcT = big[:, 8192:10240].rearrange("p (b s) -> p b s", b=RB)
        XP = S + CONV
        xrT = big[:, 8448:8448 + RB * XP].rearrange("p (b s) -> p b s", b=RB)
        attn1 = big[:, 8192:10240].rearrange("p (t c) -> p t c", t=T)
        hidT = big[:, :].rearrange("p (f s) -> p f s", f=KF)
        ple = big[:, 0:T * D].rearrange("p (t c) -> p t c", t=T)
        qkv2 = big[:, 0:6144].rearrange("p (t c) -> p t c", t=T)
        lat = big[:, 6144:6144 + T * 2 * LAT].rearrange("p (t c) -> p t c", t=T)
        scratch2 = big[:, 6144:8192]
        rot = big[:, 8320:8320 + T * 9 * 64].rearrange("p (t c) -> p t c", t=T)
        masks = big[:, 9600:9600 + 2 * T * S].rearrange("p (m t k) -> p m t k", m=2, t=T)
        rows = big[:, 0:3 * D].rearrange("p (r c) -> p r c", r=3)
        bias1 = misc[:, 0:NH * 6 * GRID_W].rearrange("p (h r c) -> p h r c", h=NH, r=6)
        rg_w = misc[:, 3072:3072 + 32 * P].rearrange("p (z g b c) -> p z g b c", z=2, g=2, b=RB)
        scratch1 = misc[:, 3072:5120]
        ada_ring = misc[:, 0:ADA_SLOTS * ADA_W].rearrange("p (s c) -> p s c", s=ADA_SLOTS)
        ada_acc = misc[:, 4096:4096 + ADA_W]
        mod_row = misc[:, 5120:5120 + ADA_W]
        silu_g = misc[:, 6144:6656].rearrange("p (b s) -> p b s", b=2)
        latT = misc[:, 0:2 * KL * S].rearrange("p (k s) -> p k s", k=2 * KL)
        rotT = misc[:, 2048:2048 + 9 * S].rearrange("p (h s) -> p h s", h=9)
        v2n = misc[:, 4352:4352 + T * DA].rearrange("p (t c) -> p t c", t=T)
        subk = misc[:, 6400:6656].rearrange("p (a k) -> p a k", a=2)
        qb = misc[:, 0:2 * S].rearrange("p (b s) -> p b s", b=2)
        gidx = misc[:, 512:768].bitcast(I32).rearrange("p (t k) -> p t k", t=T)
        gwt = misc[:, 768:1024].rearrange("p (t k) -> p t k", t=T)
        score = misc[:, 2048:2048 + 16 * S].rearrange("p (j c) -> p j c", j=16)
        gstage = misc[:, 1024:1024 + T * TOPK].bitcast(I32).rearrange("p (t k) -> p t k", t=T)
        wstage = misc[:, 1088:1088 + T * TOPK].rearrange("p (t k) -> p t k", t=T)
        token = misc[:, 1152:1152 + T]
        tokbase = misc[:, 1160:1161]
        iota16 = misc[:, 1312:1328]

        o2 = xT[:, :, :].rearrange("p k s -> p (k s)").rearrange("p (t c) -> p t c", t=T)

        auxf = aux[:, :, :].rearrange("p a c -> p (a c)")
        tk_v12 = auxf[:, 0:256].rearrange("p (t h a k) -> p t h a k", t=T, h=4, a=2)
        tk_i12 = auxf[:, 256:512].bitcast(U32).rearrange("p (t h a k) -> p t h a k", t=T, h=4, a=2)
        tk_f12 = auxf[:, 512:768].rearrange("p (t h a k) -> p t h a k", t=T, h=4, a=2)
        tk_tmp = auxf[:, 768:1024]
        tk_cand = auxf[:, 1024:2048].rearrange("p (h i j) -> p h i j", h=4, i=16)
        tk_val = auxf[:, 2048:2176].rearrange("p (t h k) -> p t h k", t=T, h=4)
        tk_ci = auxf[:, 2176:2304].bitcast(U32).rearrange("p (t h k) -> p t h k", t=T, h=4)
        tk_ab = auxf[:, 2304:2560].bitcast(U32).rearrange("p (a c) -> p a c", a=2)
        tk_abf = auxf[:, 2560:2816].rearrange("p (a t h k) -> p a t h k", a=2, t=T, h=4)
        tk_hot = auxf[:, 2816:3840].rearrange("p (n k) -> p n k", k=16)
        tk_sum = auxf[:, 3840:3904]
        tk_pick = auxf[:, 3904:4032].rearrange("p (a n) -> p a n", a=2)

        h3_hi = rounded("h3_hi", "xT", 0, KD * S)[:, :].rearrange("p (k s) -> p k s", k=KD)
        h3_lo = rounded("h3_lo", "aux", 0, KD * S)[:, :].rearrange("p (k s) -> p k s", k=KD)
        ffn_raw = [ring[:, i * CH:(i + 1) * CH] for i in range(RAW)]
        ffn_hi = [rounded(f"ffn_hi{i}", "ring", (RAW + i) * CH, CH)[:, :] for i in range(PARTS)]
        ffn_lo = [rounded(f"ffn_lo{i}", "nat", i * CH, CH)[:, :] for i in range(2)]
        mix_hi = rounded("mix_hi", "nat", 0, KD * S)[:, :].rearrange("p (k s) -> p k s", k=KD)
        mix_lo = rounded("mix_lo", "aux", 0, KD * S)[:, :].rearrange("p (k s) -> p k s", k=KD)
        h2_hi = rounded("h2_hi", "xT", 0, KD * S)[:, :].rearrange("p (k s) -> p k s", k=KD)
        h2_lo = rounded("h2_lo", "big", 6144, KD * S)[:, :].rearrange("p (k s) -> p k s", k=KD)
        slots_left = [(PLAN["wo"]["small"] + i) % SLOTS for i in range(SLOTS)]
        raw = [ring[:, i * CH:(i + 1) * CH] for i in slots_left[:RAW]]
        part_hi = [rounded(f"part_hi{n}", "ring", i * CH, CH)[:, :] for n, i in enumerate(slots_left[RAW:])]
        wo_lo = [rounded(f"wo_lo{n}", "big", 6144 + n * CH, CH)[:, :] for n in range(2)]
        part_lo = [rounded(f"part_lo{n}", "nat" if n < 2 else "big", (n % 2) * CH, CH)[:, :] for n in range(PARTS)]
        normed2 = big[:, 0:T * D].rearrange("p (t c) -> p t c", t=T)
        mod_tmp = auxf[:, 0:2 * S].rearrange("p (b s) -> p b s", b=2)
        gelu_out = big[:, 10240:11264].rearrange("p (b c) -> p b c", b=2)
        pairs = misc[:, 2048:4096].rearrange("p (n b c) -> p n b c", n=2, b=2)
        weight_in, gelu_in = pairs[:, 0], pairs[:, 1]
        coef_hi, coef_lo = (rounded(n, "misc", first, 4 * S)[:, :].rearrange("p (b c) -> p b c", b=2)
                            for n, first in (("coef_hi", 4096), ("coef_lo", 5120)))
        last_rows = [raw[0], raw[1], raw[2]]
        result = big[:, 0:T * D].rearrange("p (t c) -> p t c", t=T)

        weight_dram = nc.dram_tensor("weight_dram", [P, NEB * S], F32).ap()
        gelu_dram = nc.dram_tensor("gelu_dram", [P, NEB * S], F32).ap()
        mod_dram = nc.dram_tensor("mod_dram", [6, D], F32).ap()

        slot_loaded = [sem(f"slot_loaded{i}") for i in range(SLOTS)]
        big_loaded = [sem(f"big_loaded{i}") for i in range(BSLOTS)]
        ada_loaded = [sem(f"ada_loaded{i}") for i in range(ADA_SLOTS // 2)]
        multiplied = sem("multiplied")
        taken = sem("taken")
        for n in ("x_in", "cols_in", "consts_in", "bias_in", "rg_in", "bias_masked", "dve_step", "act_step", "pool_step",
                  "ones_set", "rms_in", "root_out", "hn_ready", "xr_padded", "conv_done", "gates",
                  "gates_taken", "gates_ready", "rec_b2", "rec_root", "rec_scan", "rec_sum", "rec_sq",
                  "rec_norm", "rec_normed", "aux_free", "row_in", "ssq_in", "resid_piece", "silu_done",
                  "ada_used", "ada_sum", "ada_rowsum", "mod_ready", "mod_b_in", "mod_out", "cact_ready",
                  "modc_in", "misc_in", "lat_ready", "rope_done", "rotq_ready", "rows_in", "rows2_in",
                  "h2_ready", "scores", "staged", "zeros_set", "scattered", "hi_ready", "lo_ready",
                  "mix_turned", "mix_hi_out", "mix_lo_out", "h2_turned", "h2_hi_out", "h2_lo_out",
                  "expert_used", "gelu_done", "coef_raw", "coef_hi_ready", "coef_ready", "score_out",
                  "h3_turned", "h3_hi_out", "h3_lo_out", "out_ready", "out_done", "sk_in", "iota_done",
                  "topk_exp_in", "topk_exp_out", "o_ready", "modc_ready", "row2_in", "row3_in", "attn1_ready",
                  "softplus_in", "softplus_exp", "chosen"):
            sem(n)
        raw_loaded = [sem(f"raw_loaded{i}") for i in range(RAW)]
        SPLIT_WO, SPLIT_PQ, SPLIT_EXP = 2 * KF, 2 * KF + 16, 2 * KF + 32
        gelu_stored = [sem(f"gelu_stored{i}") for i in range(2)]
        pair_loaded = [sem(f"pair_loaded{i}") for i in range(2)]
        row_used = sem("row_used")

        block = ctx.enter_context(nc.Block())

        def slot_of(phase, j):
            return (PLAN[phase]["small"] + j) % SLOTS

        def loads_before(phase, j):
            return (PLAN[phase]["small"] + j) // SLOTS

        def wait_loaded(eng, phase, j, it=0):
            eng.wait_ge(slot_loaded[slot_of(phase, j)], 16 * (loads_before(phase, j) + 1) + 16 * it)

        def slot_ap(phase, j):
            s = slot_of(phase, j)
            return ring[:, s * CH:(s + 1) * CH]

        def wait_multiplied(eng, phase, j, it=0, per=0):
            eng.wait_ge(multiplied, PLAN[phase]["chunk"] + j + 1 + per * it)

        def out_no(phase, o):
            return PLAN[phase]["out"] + o

        def out_bank(phase, o):
            return bank[out_no(phase, o) % 4]

        def wait_bank(pe, phase, o, it=0, per=0):
            n = out_no(phase, o) - 3
            if n > 0:
                pe.wait_ge(taken, n + per * it)

        def loop(eng, n):
            return eng.Fori(0, n)

        class Steps:

            def __init__(self, eng, name):
                self.eng, self.sem, self.n, self.off = eng, sem(name), 0, 0

            def link(self, ins):
                ins.then_inc(self.sem, 1)
                self.n += 1
                self.eng.wait_ge(self.sem, self.n + self.off)

            def mark(self, ins):
                ins.then_inc(self.sem, 1)
                self.n += 1

            def wait(self):
                self.eng.wait_ge(self.sem, self.n + self.off)

            @contextmanager
            def loop(self, n, per):
                with self.eng.Fori(0, n) as it:
                    start, self.off = self.n, it * per
                    yield it
                    assert self.n == start + per, (self.n - start, per)
                self.off = 0
                self.n = start + n * per

        TURNS = {}

        def turn_sems(name):
            if name not in TURNS:
                TURNS[name] = (sem(f"{name}_turned"), sem(f"{name}_taken_v"), sem(f"{name}_taken_a"))
            return TURNS[name]

        for n in ("n1", "n2", "n4", "n5", "n6", "tq", "tr"):
            turn_sems(n)

        def turn_pe(pe, name, n, src, width=P):
            turned, tv, ta = turn_sems(name)
            for k in range(n):
                if k >= 4:
                    pe.wait_ge(ta if k % 2 else tv, (k - 4) // 2 + 1)
                for t in range(T):
                    m = pe.transpose(bank[4 + k % 4][0:width, t * P:(t + 1) * P], src(k, t), ident[:, :])
                m.then_inc(turned, 1)

        def turn_out(eng, name, n, dst, scale=None, shift=None, width=P):
            turned, tv, ta = turn_sems(name)
            odd = eng is nc.scalar
            for k in range(1 if odd else 0, n, 2):
                eng.wait_ge(turned, k + 1)
                ps = bank[4 + k % 4][0:width, 0:S]
                if odd:
                    if shift is not None:
                        i = eng.activation(dst(k), ps, ACT.Identity, scale=scale(k), bias=shift(k))
                    elif scale is not None:
                        i = eng.activation(dst(k), ps, ACT.Copy, scale=scale(k))
                    else:
                        i = eng.activation(dst(k), ps, ACT.Copy)
                    i.then_inc(ta, 1)
                else:
                    if shift is not None:
                        i = eng.tensor_scalar(dst(k), ps, scale(k), shift(k), ALU.mult, ALU.add)
                    elif scale is not None:
                        i = eng.tensor_scalar(dst(k), ps, scale(k), None, ALU.mult)
                    else:
                        i = eng.tensor_copy(dst(k), ps)
                    i.then_inc(tv, 1)

        def wait_turned_out(eng, name, n):
            _, tv, ta = turn_sems(name)
            eng.wait_ge(tv, (n + 1) // 2)
            if n > 1:
                eng.wait_ge(ta, n // 2)

        def gain(name, first=0):
            return lambda k: cols[:, COLS[name] + first + k:COLS[name] + first + k + 1]

        def product_t(pe, phase, j, o, kk=KD, x=None, it=0, per_out=0, sub=0, last=True, wait=True):
            if wait:
                wait_loaded(pe, phase, j, it)
            wait_bank(pe, phase, o, it, per_out)
            w = slot_ap(phase, j)
            for k in range(kk):
                m = pe.matmul(out_bank(phase, o)[:, 0:S], w[:, (sub * kk + k) * P:(sub * kk + k + 1) * P],
                              (x or (lambda k: xT[:, k, :]))(k), start=(k == 0), stop=(k == kk - 1))
            if last:
                m.then_inc(multiplied, 1)

        def product_n(pe, phase, j0, o, nch, kk, lhs, it=0, per_out=0, width=BAND, sub=0, last=True, wait=True):
            for c in range(nch):
                if wait:
                    wait_loaded(pe, phase, j0 + c, it)
                if c == 0:
                    wait_bank(pe, phase, o + T - 1, it, per_out)
                w = slot_ap(phase, j0 + c)
                for k in range(kk):
                    for t in range(T):
                        m = pe.matmul(out_bank(phase, o + t)[:, 0:width], lhs(c * kk + k, t),
                                      w[:, sub * kk * BAND + k * width:sub * kk * BAND + (k + 1) * width],
                                      start=(c == 0 and k == 0), stop=(c == nch - 1 and k == kk - 1))
                if last:
                    m.then_inc(multiplied, 1)

        def x_lhs(k, t):
            return xT[:, k, t * P:(t + 1) * P]

        def n_lhs(k, t):
            return natT[:, k, t * P:(t + 1) * P]

        natT = nat[:, :, :].rearrange("p t c -> p (t c)").rearrange("p (k s) -> p k s", k=KD)

        KINDS = ("at1", "at2", "at3")
        for n in KINDS:
            for m in ("scored", "biased", "exped", "turned", "pt_out", "valued", "out"):
                sem(f"{n}_{m}")

        def attention_pe(pe, kind, score, value, scratch):
            prob, prT = attention_scratch(scratch)

            def scores(h):
                if h >= 2:
                    pe.wait_ge(sem(f"{kind}_biased"), h - 1)
                for t in range(T):
                    m = score(pe, h, t, bank[h % 2][:, t * S:(t + 1) * S])
                m.then_inc(sem(f"{kind}_scored"), 1)

            def turn(h):
                pe.wait_ge(sem(f"{kind}_exped"), h + 1)
                if h >= 2:
                    pe.wait_ge(sem(f"{kind}_pt_out"), h - 1)
                for kc in range(T):
                    for t in range(T):
                        m = pe.transpose(bank[2 + h % 2][:, kc * S + t * P:kc * S + (t + 1) * P],
                                         prob[:, h % 2, t, kc * P:(kc + 1) * P], ident[:, :])
                m.then_inc(sem(f"{kind}_turned"), 1)

            def values(h):
                pe.wait_ge(sem(f"{kind}_pt_out"), h + 1)
                if h >= 2:
                    pe.wait_ge(sem(f"{kind}_out"), h - 1)
                for t in range(T):
                    for kc in range(T):
                        m = pe.matmul(bank[4 + h % 2][:, t * P:(t + 1) * P], prT[:, h % 2, kc, t * P:(t + 1) * P],
                                      value(kc, h), start=(kc == 0), stop=(kc == T - 1))
                m.then_inc(sem(f"{kind}_valued"), 1)

            scores(0)
            for h in range(NH):
                if h + 1 < NH:
                    scores(h + 1)
                turn(h)
                if h:
                    values(h - 1)
            values(NH - 1)

        def attention_scratch(scratch):
            prob = scratch[:, 0:1024].rearrange("p (b t k) -> p b t k", b=2, t=T)
            prT = scratch[:, 1024:2048].rearrange("p (b c q) -> p b c q", b=2, c=T)
            return prob, prT

        def by_row(ap):
            return ap.rearrange("p (r c) -> p r c", c=GRID_W)

        def attention_dve(v, steps, kind, bias, scale, out, scratch):
            prob, prT = attention_scratch(scratch)

            def biased(h):
                v.wait_ge(sem(f"{kind}_scored"), h + 1)
                if h >= 2:
                    v.wait_ge(sem(f"{kind}_turned"), h - 1)
                for t in range(T):
                    i = v.scalar_tensor_tensor(out=by_row(prob[:, h % 2, t, :]),
                                               in0=by_row(bank[h % 2][:, t * S:(t + 1) * S]),
                                               scalar=scale, in1=bias(h, t), op0=ALU.mult, op1=ALU.add)
                    if t == T - 1:
                        i.then_inc(sem(f"{kind}_biased"), 1)
                    else:
                        steps.mark(i)
                steps.wait()
                v.wait_ge(sem(f"{kind}_biased"), h + 1)
                steps.link(v.tensor_reduce(mxs[:, h % 2, 0:T], prob[:, h % 2, :, :], AXX, ALU.max))
                v.tensor_scalar(mxs[:, h % 2, T:2 * T], mxs[:, h % 2, 0:T], -1.0, None, ALU.mult).then_inc(
                    sem(f"{kind}_negmax"), 1)

            def result(h):
                v.wait_ge(sem(f"{kind}_exped"), h + 1)
                steps.link(v.reciprocal(den[:, h % 2, T:2 * T], den[:, h % 2, 0:T]))
                v.wait_ge(sem(f"{kind}_valued"), h + 1)
                for t in range(T):
                    i = v.tensor_scalar(out(h, t), bank[4 + h % 2][:, t * P:(t + 1) * P],
                                        den[:, h % 2, T + t:T + t + 1], None, ALU.mult)
                    if t == T - 1:
                        i.then_inc(sem(f"{kind}_out"), 1)
                    else:
                        steps.mark(i)
                steps.wait()

            for h in range(NH):
                biased(h)
                if h >= 2:
                    result(h - 2)
            result(NH - 2)
            result(NH - 1)
            v.wait_ge(sem(f"{kind}_out"), NH)

        def attention_act(a, kind, scratch):
            prob, prT = attention_scratch(scratch)

            def exps(h):
                a.wait_ge(sem(f"{kind}_negmax"), h + 1)
                if h >= 2:
                    a.wait_ge(sem(f"{kind}_out"), h - 1)
                for t in range(T):
                    i = a.activation(prob[:, h % 2, t, :], prob[:, h % 2, t, :], ACT.Exp,
                                     bias=mxs[:, h % 2, T + t:T + t + 1], accum_out=den[:, h % 2, t:t + 1])
                i.then_inc(sem(f"{kind}_exped"), 1)

            def turned(h):
                a.wait_ge(sem(f"{kind}_turned"), h + 1)
                if h >= 2:
                    a.wait_ge(sem(f"{kind}_valued"), h - 1)
                a.activation(prT[:, h % 2, :, :].rearrange("p c q -> p (c q)"), bank[2 + h % 2][:, :], ACT.Copy)\
                    .then_inc(sem(f"{kind}_pt_out"), 1)

            exps(0)
            for h in range(NH):
                if h + 1 < NH:
                    exps(h + 1)
                turned(h)

        for n in KINDS:
            sem(f"{n}_negmax")

        def split_products(out, hi, lo, x_hi, x_lo, start, stop):
            nc.tensor.matmul(out, hi, x_hi, start=start, stop=False)
            nc.tensor.matmul(out, hi, x_lo, start=False, stop=False)
            return nc.tensor.matmul(out, lo, x_hi, start=False, stop=stop)

        def split_turn_pe(pe, name, n, src):
            for k in range(n):
                if k >= 4:
                    pe.wait_ge(sem(f"{name}_lo_out"), k - 3)
                for t in range(T):
                    m = pe.transpose(bank[4 + k % 4][:, t * P:(t + 1) * P], src(k, t), ident[:, :])
                m.then_inc(sem(f"{name}_turned"), 1)

        def split_turn_hi(a, name, n, hi, scale):
            for k in range(n):
                a.wait_ge(sem(f"{name}_turned"), k + 1)
                a.activation(hi[:, k, :], bank[4 + k % 4][:, 0:S], ACT.Copy, scale=scale(k)).then_inc(
                    sem(f"{name}_hi_out"), 1)

        def split_turn_hi_mod(a, name, n, hi):
            for k in range(n):
                a.wait_ge(sem(f"{name}_turned"), k + 1)
                a.activation(hi[:, k, :], bank[4 + k % 4][:, 0:S], ACT.Identity, scale=modc[:, 0, k:k + 1],
                             bias=modc[:, 1, k:k + 1]).then_inc(sem(f"{name}_hi_out"), 1)

        def split_turn_lo_mod(v, name, n, hi, lo, tmp, done):
            for k in range(n):
                v.wait_ge(sem(f"{name}_hi_out"), k + 1)
                done.link(v.tensor_scalar(tmp[:, k % 2, :], bank[4 + k % 4][:, 0:S], modc[:, 0, k:k + 1],
                                          modc[:, 1, k:k + 1], ALU.mult, ALU.add))
                v.tensor_tensor(lo[:, k, :], tmp[:, k % 2, :], hi[:, k, :].bitcast(F32), ALU.subtract).then_inc(
                    sem(f"{name}_lo_out"), 1)
            v.wait_ge(sem(f"{name}_lo_out"), n)

        def split_turn_lo(v, name, n, hi, lo, scale):
            for k in range(n):
                v.wait_ge(sem(f"{name}_hi_out"), k + 1)
                v.scalar_tensor_tensor(out=lo[:, k, :], in0=bank[4 + k % 4][:, 0:S], scalar=scale(k),
                                       in1=hi[:, k, :].bitcast(F32), op0=ALU.mult, op1=ALU.subtract).then_inc(
                    sem(f"{name}_lo_out"), 1)
            v.wait_ge(sem(f"{name}_lo_out"), n)

        wst = io["stream"]

        @block.sync
        def _(sp_):
            for t in range(T):
                sp_.dma_start(resid[:, t, :], io["x"][0, t * P:(t + 1) * P, :]).then_inc(sem("x_in"), 16)

            def load(phase, j, it=None):
                s = slot_of(phase, j)
                small = PLAN[phase]["small"] + j
                chunk = PLAN[phase]["chunk"] + j
                if it is None or isinstance(it, int):
                    sp_.dma_start(ring[:, s * CH:(s + 1) * CH], wst[small]).then_inc(slot_loaded[s], 16)
                else:
                    sp_.dma_start(ring[:, s * CH:(s + 1) * CH],
                                  wst[bass.ds(small + it * SLOTS, 1)].rearrange("n p c -> (n p) c"))\
                        .then_inc(slot_loaded[s], 16)

            def stream(phase, n, j0=0):
                rounds = n // SLOTS
                assert n % SLOTS == 0
                if rounds == 1:
                    for j in range(SLOTS):
                        sp_.wait_ge(multiplied, PLAN[phase]["chunk"] + j0 + j - SLOTS + 1)
                        load(phase, j0 + j)
                    return
                with loop(sp_, rounds) as it:
                    for j in range(SLOTS):
                        sp_.wait_ge(multiplied, PLAN[phase]["chunk"] + j0 + j - SLOTS + 1 + it * SLOTS)
                        load(phase, j0 + j, it)

            for j in range(SLOTS):
                load("xr", j)
            stream("yg", 8)
            stream("q", 8)
            stream("k", 8)
            stream("v", 8)
            stream("wout", 8)

            def ada_load(j, g):
                s = 2 * j % ADA_SLOTS
                sp_.wait_ge(sem("ada_used"), KD * g + 2 * j + 2)
                sp_.dma_start(ada_ring[:, s:s + 2, :],
                              io["w_ada"][2 * j * P:(2 * j + 2) * P, bass.ds(g * ADA_W, ADA_W)]
                              .rearrange("(k p) c -> p k c", p=P)).then_inc(ada_loaded[s // 2], 16)

            def ada_group(g):
                for j in range(8):
                    ada_load(j, g)

            for j in range(8):
                sp_.wait_ge(multiplied, PLAN["wout"]["chunk"] + j + 1)
                load("wout", SLOTS + j)
                if j in (1, 3, 7):
                    ada_group(j // 2 if j < 7 else 2)
            ada_group(3)

            gu_end = PLAN["down"]["chunk"]
            assert slot_of("gateup", 0) == 0
            for j in range(RAW):
                sp_.wait_ge(multiplied, PLAN["gateup"]["chunk"] - SLOTS + j + 1)
                sp_.dma_start(ffn_raw[j], io["gateup"][j]).then_inc(raw_loaded[j], 16)

            def gateup_round(it, loads):
                for j in range(8):
                    if j < loads:
                        sp_.wait_ge(sem("lo_ready"), j + 1 + 8 * it)
                        src = io["gateup"][RAW + j + 8 * it] if isinstance(it, int) else \
                            io["gateup"][bass.ds(RAW + j + 8 * it, 1)].rearrange("n p c -> (n p) c")
                        sp_.dma_start(ffn_raw[j % RAW], src).then_inc(raw_loaded[j % RAW], 16)
                    ada_load(j, ADA_EARLY + it)

            with loop(sp_, KF // 4 - 1) as it:
                gateup_round(it, 8)
            gateup_round(KF // 4 - 1, RAW)

            def load_big(c, it=0):
                s = c % BSLOTS
                src = io["down"][c] if isinstance(it, int) else \
                    io["down"][bass.ds(c + it * 8, 1)].rearrange("n p c -> (n p) c")
                sp_.dma_start(ring[:, s * BCH:(s + 1) * BCH], src).then_inc(big_loaded[s], 16)

            sp_.wait_ge(sem("lo_ready"), 2 * KF - 1)
            load_big(0)
            sp_.wait_ge(sem("lo_ready"), 2 * KF)
            sp_.wait_ge(multiplied, gu_end - 2)
            load_big(1)
            ada_group(ADA_FFN)
            for c in range(2, 16):
                sp_.wait_ge(multiplied, gu_end + c - BSLOTS + 1)
                load_big(c)
                if ADA_FFN + c - 1 < ADA_G:
                    ada_group(ADA_FFN + c - 1)
            down_end = PLAN["pproj"]["chunk"]
            assert PLAN["pproj"]["small"] % SLOTS == 0
            first = [("pproj", 0), ("pproj", 1)] + [("pgate", j) for j in range(6)]
            for n, (ph, j) in enumerate(first):
                if n == 0:
                    sp_.wait_ge(multiplied, down_end - 1)
                if n == 2:
                    sp_.wait_ge(multiplied, down_end)
                load(ph, j)

            def rest(phase, j0, n):
                for j in range(j0, j0 + n):
                    sp_.wait_ge(multiplied, PLAN[phase]["chunk"] + j - SLOTS + 1)
                    load(phase, j)

            rest("pgate", 6, 10)
            rest("lat", 0, 8)
            rest("kr", 0, 1)
            stream("qk2", 16)
            stream("v2", 8)
            rest("mla", 0, 7)

            for j in range(RAW):
                sp_.wait_ge(multiplied, PLAN["wo"]["chunk"] - SLOTS + j + 1)
                sp_.dma_start(raw[j], io["wo_pq"][j]).then_inc(raw_loaded[j], 16)

            def raw_chunks(table, row0, before, rounds):
                with loop(sp_, rounds) as it:
                    for j in range(RAW):
                        sp_.wait_ge(sem("lo_ready"), before - RAW + j + 1 + RAW * it)
                        row = bass.ds(row0 + j + RAW * it, 1)
                        sp_.dma_start(raw[j], io[table][row].rearrange("n p c -> (n p) c")).then_inc(raw_loaded[j], 16)

            raw_chunks("wo_pq", RAW, SPLIT_WO + RAW, 32 // RAW - 1)
            raw_chunks("u_table", 0, SPLIT_EXP, NEB // RAW)
            raw_chunks("v_table", 0, SPLIT_EXP + NEB, NEB // RAW)

            for t in range(T):
                sp_.wait_ge(sem("out_ready"), t + 1)
                sp_.dma_start(io["out"][0, t * P:(t + 1) * P, :], resid[:, t, :]).then_inc(sem("out_done"), 16)
            sp_.wait_ge(sem("out_done"), 16 * T)

        @block.tensor
        def _(pe):
            pe.wait_ge(sem("consts_in"), 16 * 3)
            pe.wait_ge(sem("ones_set"), 1)
            pe.wait_ge(sem("hn_ready"), 1)
            turn_pe(pe, "n1", KD, lambda k, t: nat[:, t, k * P:(k + 1) * P])
            wait_turned_out(pe, "n1", KD)
            for j in range(RB):
                product_t(pe, "xr", j, j)
            for j in range(RB):
                product_t(pe, "yg", j, j)

            def gates(z):
                if z == 0:
                    pe.wait_ge(sem("rg_in"), 16)
                for b in range(RB):
                    pe.wait_ge(sem("conv_done"), b + 1)
                    n = z * RB + b
                    if n >= 4:
                        pe.wait_ge(sem("gates_taken"), n - 3)
                    for g in range(2):
                        m = pe.matmul(bank[4 + n % 4][:, g * S:(g + 1) * S], rg_w[:, z, g, b, :], xcT[:, b, :],
                                      start=True, stop=True)
                    m.then_inc(sem("gates"), 1)

            gates(0)
            for j in range(RB):
                product_t(pe, "q", j, j)
            gates(1)
            for j in range(RB):
                product_t(pe, "k", j, j)
            for c in range(2):
                product_n(pe, "v", 4 * c, 2 * c, 4, 4, x_lhs)
            pe.wait_ge(sem("bias_masked"), 4)
            pe.wait_ge(taken, out_no("wout", 0))
            pe.wait_ge(sem("gates_taken"), 2 * RB)

            def score1(pe, h, t, ps):
                return pe.matmul(ps, qkT[:, h, t * P:(t + 1) * P], qkT[:, NH + h, :], start=True, stop=True)

            attention_pe(pe, "at1", score1, lambda kc, h: v1n[:, kc, h * HD:(h + 1) * HD], scratch1)
            pe.wait_ge(sem("attn1_ready"), 1)
            pe.wait_ge(sem("at1_out"), NH)
            turn_pe(pe, "n2", 8, lambda k, t: attn1[:, t, k * P:(k + 1) * P])
            wait_turned_out(pe, "n2", 8)
            pe.wait_ge(sem("rec_sq"), 1)
            for b in range(RB):
                m = pe.matmul(bank[4][:, 0:S], ones[:, :], nat[:, 0, b * S:(b + 1) * S], start=(b == 0),
                              stop=(b == RB - 1))
            m.then_inc(sem("rec_norm"), 1)
            pe.wait_ge(sem("rec_normed"), RB)
            def ada_sum(g):
                pe.wait_ge(sem("ada_sum"), g + 1)
                m = pe.matmul(bank[4][0:1, 0:ADA_W], ones[:, 0:1], ada_acc, start=True, stop=True)
                m.then_inc(sem("ada_rowsum"), 1)

            with loop(pe, 2) as it:
                for c in range(2):
                    product_n(pe, "wout", 4 * c, 2 * c, 4, 4, x_lhs, it=it, per_out=4)
                    ada_sum(2 * it + c)
            pe.wait_ge(sem("hn_ready"), 2)
            split_turn_pe(pe, "h3", KD, lambda k, t: nat[:, t, k * P:(k + 1) * P])

            def gateup_round(it, first=False):
                for j in range(8):
                    if j == 1 and not first:
                        ada_sum(ADA_EARLY - 1 + it)
                    pe.wait_ge(sem("lo_ready"), j + 1 + 8 * it)
                    wait_bank(pe, "gateup", j, it, 8)
                    for k in range(KD):
                        ks = slice(k * P, (k + 1) * P)
                        m = split_products(out_bank("gateup", j)[:, 0:S], ffn_hi[j % PARTS][:, ks], ffn_lo[j % 2][:, ks],
                                           h3_hi[:, k, :], h3_lo[:, k, :], k == 0, k == KD - 1)
                    m.then_inc(multiplied, 1)

            gateup_round(0, True)
            with loop(pe, KF // 4 - 1) as it:
                gateup_round(it + 1)
            pe.wait_ge(taken, out_no("down", 0))
            for c in range(4):
                for q in range(4):
                    n = 4 * c + q
                    pe.wait_ge(big_loaded[n % BSLOTS], 16 * (n // BSLOTS + 1))
                    if q == 0:
                        wait_bank(pe, "down", 2 * c + 1)
                    for k in range(11):
                        for t in range(T):
                            m = pe.matmul(out_bank("down", 2 * c + t)[:, :],
                                          hidT[:, 11 * q + k, t * P:(t + 1) * P],
                                          ring[:, (n % BSLOTS) * BCH + k * BAND:(n % BSLOTS) * BCH + (k + 1) * BAND],
                                          start=(q == 0 and k == 0), stop=(q == 3 and k == 10))
                    m.then_inc(multiplied, 1)
                    if ADA_FFN - 1 + n < ADA_G:
                        ada_sum(ADA_FFN - 1 + n)
            for c in range(4):
                product_n(pe, "pproj", c // 2, 2 * c, 1, 2, lambda k, t: pT[:, k, t * P:(t + 1) * P], sub=c % 2,
                          last=(c % 2 == 1))
            pe.wait_ge(sem("hn_ready"), 3)
            turn_pe(pe, "n4", KD, lambda k, t: nat[:, t, k * P:(k + 1) * P])
            wait_turned_out(pe, "n4", KD)
            with loop(pe, 2) as it:
                for c in range(2):
                    product_n(pe, "pgate", 4 * c, 2 * c, 4, 4, x_lhs, it=it, per_out=4)

            pe.wait_ge(sem("hn_ready"), 4)
            turn_pe(pe, "n5", KD, lambda k, t: nat[:, t, k * P:(k + 1) * P])
            wait_turned_out(pe, "n5", KD)
            for c in range(2):
                product_n(pe, "lat", 4 * c, 2 * c, 4, 4, x_lhs)
            product_n(pe, "kr", 0, 0, 1, KD, x_lhs, width=64)
            with loop(pe, 2) as it:
                for c in range(2):
                    product_n(pe, "qk2", 4 * c, 2 * c, 4, 4, x_lhs, it=it, per_out=4)
            pe.wait_ge(sem("lat_ready"), 1)
            turn_pe(pe, "n6", 2 * KL, lambda k, t: lat[:, t, k * P:(k + 1) * P])
            for c in range(2):
                product_n(pe, "v2", 4 * c, 2 * c, 4, 4, x_lhs)
            pe.wait_ge(sem("rope_done"), 1)
            wait_turned_out(pe, "n6", 2 * KL)
            turn_pe(pe, "tq", 2 * NH, lambda k, t: qkv2[:, t, k * P:(k + 1) * P])
            for c in range(2):
                for s in range(4):
                    product_t(pe, "mla", c, 4 * c + s, kk=KL, x=lambda k: latT[:, k, :], sub=s, last=(s == 3))
            product_n(pe, "mla", 2, 8, 1, KL, lambda k, t: latT[:, k, t * P:(t + 1) * P])
            for c in range(2):
                for s in range(4):
                    product_t(pe, "mla", 3 + c, 10 + 4 * c + s, kk=KL, x=lambda k: latT[:, KL + k, :], sub=s,
                              last=(s == 3))
            for c in range(2):
                product_n(pe, "mla", 5 + c, 18 + 2 * c, 1, KL, lambda k, t: latT[:, KL + k, t * P:(t + 1) * P])
            wait_turned_out(pe, "tq", 2 * NH)
            pe.wait_ge(sem("rotq_ready"), 1)
            turn_pe(pe, "tr", 9, lambda k, t: rot[:, t, k * 64:(k + 1) * 64], width=64)
            wait_turned_out(pe, "tr", 9)
            pe.wait_ge(taken, out_no("wo", 0))

            def score2(pe, h, t, ps):
                return pe.matmul(ps, natT[:, h, t * P:(t + 1) * P], natT[:, NH + h, :], start=True, stop=True)

            def score3(pe, h, t, ps):
                pe.matmul(ps, aux[:, 0, h * S + t * P:h * S + (t + 1) * P], aux[:, 1, h * S:(h + 1) * S],
                          start=True, stop=False)
                return pe.matmul(ps, rotT[0:64, h, t * P:(t + 1) * P], rotT[0:64, 8, :], start=False, stop=True)

            pe.wait_ge(sem("misc_in"), 16)
            attention_pe(pe, "at2", score2, lambda kc, h: qkv2[:, kc, 2 * DA + h * HD:2 * DA + (h + 1) * HD], scratch2)
            pe.wait_ge(sem("at2_out"), NH)
            attention_pe(pe, "at3", score3, lambda kc, h: v2n[:, kc, h * HD:(h + 1) * HD], scratch2)
            pe.wait_ge(sem("at3_out"), NH)
            pe.wait_ge(sem("o_ready"), 1)
            split_turn_pe(pe, "mix", KD, lambda k, t: o2[:, t, k * P:(k + 1) * P])
            pe.wait_ge(sem("mix_lo_out"), KD)

            def wo_panel(c, it):
                for q in range(4):
                    n = 4 * c + q
                    pe.wait_ge(sem("lo_ready"), SPLIT_WO + n + 1 + 8 * it)
                    if q == 0:
                        wait_bank(pe, "wo", 2 * c + 1, it, 4)
                    for k in range(4):
                        ks = slice(k * BAND, (k + 1) * BAND)
                        for t in range(T):
                            ts = slice(t * P, (t + 1) * P)
                            m = split_products(out_bank("wo", 2 * c + t)[:, :], mix_hi[:, 4 * q + k, ts],
                                               mix_lo[:, 4 * q + k, ts], part_hi[n % PARTS][:, ks], wo_lo[n % 2][:, ks],
                                               q == 0 and k == 0, q == 3 and k == 3)
                    m.then_inc(multiplied, 1)

            with loop(pe, 2) as it:
                for c in range(2):
                    wo_panel(c, it)
            pe.wait_ge(sem("h2_ready"), 1)
            split_turn_pe(pe, "h2", KD, lambda k, t: normed2[:, t, k * P:(k + 1) * P])
            pe.wait_ge(sem("h2_lo_out"), KD)
            pe.wait_ge(sem("sk_in"), 16)

            with loop(pe, 2) as it:
                def key_scores(j):
                    pe.wait_ge(taken, out_no("pq", j) + 1 + it * 8)
                    pe.wait_ge(sem("score_out"), it * 8 + j + 1)
                    for t in range(T):
                        m = pe.matmul(bank[4 + j % 2][:, t * P:(t + 1) * P], qb[:, j % 2, t * P:(t + 1) * P],
                                      subk[:, j % 2, :], start=True, stop=True)
                    m.then_inc(sem("scores"), 1)

                for j in range(8):
                    pe.wait_ge(sem("lo_ready"), SPLIT_PQ + j + 1 + 8 * it)
                    wait_bank(pe, "pq", j, it, 8)
                    for k in range(KD):
                        ks = slice(k * P, (k + 1) * P)
                        m = split_products(out_bank("pq", j)[:, 0:S], part_hi[j % PARTS][:, ks], part_lo[j % 2][:, ks],
                                           h2_hi[:, k, :], h2_lo[:, k, :], k == 0, k == KD - 1)
                    m.then_inc(multiplied, 1)
                    if j:
                        key_scores(j - 1)
                key_scores(7)

            pe.wait_ge(taken, out_no("pq", 16))

            def dots_of_block(j, it, first=False):
                pe.wait_ge(sem("lo_ready"), SPLIT_EXP + j + 1 + PARTS * it)
                if not first:
                    pe.wait_ge(sem("gelu_done"), j - 3 + PARTS * it)
                for k in range(KD):
                    ks = slice(k * P, (k + 1) * P)
                    m = split_products(bank[j % 4][:, 0:S], part_hi[j % PARTS][:, ks], part_lo[j % PARTS][:, ks],
                                       h2_hi[:, k, :], h2_lo[:, k, :], k == 0, k == KD - 1)
                m.then_inc(sem("expert_used"), 1)

            for j in range(PARTS):
                dots_of_block(j, 0, True)
            with loop(pe, NEB // PARTS - 1) as it:
                for j in range(PARTS):
                    dots_of_block(j + PARTS, it)

            pe.wait_ge(sem("gelu_done"), NEB)
            pe.wait_ge(sem("score_out"), 2 + 16)

            def values_of_block(j, it, start=False, stop=False):
                pe.wait_ge(sem("lo_ready"), SPLIT_EXP + NEB + j + 1 + PARTS * it)
                if j % 2 == 0:
                    pe.wait_ge(sem("coef_ready"), j // 2 + 1 + PARTS // 2 * it)
                for t in range(T):
                    for c in range(D // BAND):
                        ts = slice((j % 2) * S + t * P, (j % 2) * S + (t + 1) * P)
                        cs = slice(c * BAND, (c + 1) * BAND)
                        b = j // 2 % 2
                        m = split_products(bank[4 * t + c][:, :], coef_hi[:, b, ts], coef_lo[:, b, ts],
                                           part_hi[j % PARTS][:, cs], part_lo[j % PARTS][:, cs], start, stop)
                m.then_inc(sem("expert_used"), 1)

            for j in range(PARTS):
                values_of_block(j, 0, start=j == 0)
            with loop(pe, NEB // PARTS - 2) as it:
                for j in range(PARTS):
                    values_of_block(PARTS + j, it)
            for j in range(NEB - PARTS, NEB):
                values_of_block(j, 0, stop=j == NEB - 1)

        @block.scalar
        def _(a):
            steps = Steps(a, "act_step")
            a.wait_ge(sem("cols_in"), 16)
            a.wait_ge(sem("softplus_in"), 1)
            a.activation(sp[:, 1, :], sp[:, 0, :], ACT.Exp, scale=-1.0).then_inc(sem("softplus_exp"), 1)

            def root(n):
                a.wait_ge(sem("rms_in"), n)
                a.activation(st[:, 2:4], st[:, 0:2], ACT.Sqrt).then_inc(sem("root_out"), 1)

            def copy_out(phase, o, dst, it=0, per_chunks=0, chunk=0, func=ACT.Copy, width=BAND, signal=True):
                wait_multiplied(a, phase, chunk, it, per_chunks)
                i = a.activation(dst, out_bank(phase, o)[:, 0:width], func)
                if signal:
                    i.then_inc(taken, 1)
                return i

            root(1)
            turn_out(nc.scalar, "n1", KD, lambda k: xT[:, k, :], gain("g_mix_pre"))
            a.wait_ge(sem("xr_padded"), 1)
            for j in range(RB):
                copy_out("xr", j, xrT[:, j, 2:2 + S], chunk=j, width=S)
            for j in range(RB):
                copy_out("yg", j, ygT[:, j, :], chunk=j, width=S, func=ACT.Gelu_apprx_tanh)

            recA, recB = nat[:, 0, :], nat[:, 1, :]
            recU, recH = aux[:, 0, :], aux[:, 1, :]
            a.wait_ge(sem("n1_turned"), KD)

            def gate_out(z):
                if z:
                    a.wait_ge(sem("rec_scan"), 1)
                for b in range(RB):
                    n = z * RB + b
                    a.wait_ge(sem("gates"), n + 1)
                    steps.mark(a.activation(recA[:, b * S:(b + 1) * S], bank[4 + n % 4][:, 0:S], ACT.Sigmoid,
                                            bias=cols[:, COLS["b_rg_a"] + n:COLS["b_rg_a"] + n + 1]))
                    a.activation(recU[:, b * S:(b + 1) * S], bank[4 + n % 4][:, S:2 * S], ACT.Sigmoid,
                                 bias=cols[:, COLS["b_rg_i"] + n:COLS["b_rg_i"] + n + 1]).then_inc(
                        sem("gates_taken"), 1)
                steps.wait()
                if z == 0:
                    a.wait_ge(sem("softplus_in"), 2)
                for b in range(RB):
                    n = z * RB + b
                    i = a.activation(recA[:, b * S:(b + 1) * S], recA[:, b * S:(b + 1) * S], ACT.Tanh,
                                     scale=sp[:, 3, n:n + 1])
                    if b == RB - 1:
                        i.then_inc(sem("gates_ready"), 1)
                    else:
                        steps.mark(i)

            def rec_root(z):
                a.wait_ge(sem("rec_b2"), z + 1)
                a.activation(recB, recB, ACT.Sqrt, scale=-1.0).then_inc(sem("rec_root"), 1)

            gate_out(0)
            for j in range(RB):
                copy_out("q", j, qkT[:, j, :], chunk=j, width=S)
            rec_root(0)
            gate_out(1)
            for j in range(RB):
                copy_out("k", j, qkT[:, NH + j, :], chunk=j, width=S)
            rec_root(1)
            for c in range(2):
                for t in range(T):
                    copy_out("v", 2 * c + t, v1n[:, t, c * BAND:(c + 1) * BAND], chunk=4 * c + 3)
            attention_act(a, "at1", scratch1)
            root(2)
            turn_out(nc.scalar, "n2", 8, lambda k: xT[:, k, :], gain("g_attn_out"))
            a.wait_ge(sem("rec_sum"), 1)
            a.activation(recA, recH, ACT.Square).then_inc(sem("rec_sq"), 1)
            a.wait_ge(sem("rec_norm"), 2)
            a.activation(conv_tmp[:, 0, :], conv_tmp[:, 0, :], ACT.Sqrt).then_inc(sem("rec_norm"), 1)

            def panels(phase, n, squares=True, func=ACT.Copy, dst=None):
                dst = nat if dst is None else dst
                with loop(a, 2) as it:
                    for c in range(2):
                        for t in range(T):
                            wait_multiplied(a, phase, 4 * c + 3, it, 8)
                            ps = out_bank(phase, 2 * c + t)
                            i = a.activation(dst[:, t, bass.ds(c * BAND + it * 2 * BAND, BAND)], ps[:, :], func)
                            if squares:
                                a.wait_ge(taken, out_no(phase, 2 * c + t) + 4 * it)
                                a.activation(silu_junk, ps[:, :], ACT.Square,
                                             accum_out=ssq[:, t, bass.ds(c + it * 2, 1)]).then_inc(taken, 1)
                            else:
                                i.then_inc(taken, 1)

            silu_junk = bank[6][:, :]

            def resid_squares(n0):
                for t in range(T):
                    for c in range(4):
                        a.wait_ge(sem("resid_piece"), n0 + t * 4 + c + 1)
                        if n0 + t + c:
                            a.wait_ge(sem("ssq_in"), n0 + t * 4 + c)
                        i = a.activation(bank[6][:, :], resid[:, t, c * BAND:(c + 1) * BAND], ACT.Square,
                                         accum_out=ssq[:, t, c:c + 1])
                        i.then_inc(sem("ssq_in"), 1)

            a.activation(cact[:, :], cols[:, COLS["c"]:COLS["c"] + KD], ACT.Silu).then_inc(sem("cact_ready"), 1)
            panels("wout", 0)
            root(3)
            resid_squares(0)
            root(4)
            split_turn_hi(a, "h3", KD, h3_hi, gain("g_ffn_pre"))

            def ffn_upper(j, it=0, first=False):
                a.wait_ge(raw_loaded[j % RAW], 16 * (j // RAW + 1) + 32 * it)
                if not first:
                    wait_multiplied(a, "gateup", j - PARTS, it, 8)
                a.activation(ffn_hi[j % PARTS], ffn_raw[j % RAW], ACT.Copy).then_inc(sem("hi_ready"), 1)

            def gated(it, uppers):
                for j in range(4):
                    if 2 * j < uppers:
                        ffn_upper(PARTS + 2 * j, it)
                    wait_multiplied(a, "gateup", 2 * j, it, 8)
                    a.wait_ge(taken, out_no("gateup", 0) + 2 * (j - 1) + it * 8)
                    a.activation(silu_g[:, j % 2, :], out_bank("gateup", 2 * j)[:, 0:S], ACT.Silu).then_inc(
                        sem("silu_done"), 1)
                    if 2 * j < uppers:
                        ffn_upper(PARTS + 2 * j + 1, it)

            wait_multiplied(a, "wout", 15)
            for j in range(PARTS):
                ffn_upper(j, first=True)
            with loop(a, KF // 4 - 1) as it:
                gated(it, 8)
            gated(KF // 4 - 1, 4)

            for c in range(4):
                for t in range(T):
                    wait_multiplied(a, "down", 4 * c + 3)
                    ps = out_bank("down", 2 * c + t)
                    a.activation(nat[:, t, c * BAND:(c + 1) * BAND], ps[:, :], ACT.Copy)
                    a.wait_ge(taken, out_no("down", 2 * c + t))
                    a.activation(silu_junk, ps[:, :], ACT.Square, accum_out=ssq[:, t, c:c + 1]).then_inc(taken, 1)
            for c in range(4):
                for t in range(T):
                    copy_out("pproj", 2 * c + t, ple[:, t, c * BAND:(c + 1) * BAND], chunk=c // 2)
            root(5)
            resid_squares(8)
            root(6)
            turn_out(nc.scalar, "n4", KD, lambda k: xT[:, k, :], gain("g_ple_pre"))
            with loop(a, 2) as it:
                for c in range(2):
                    for t in range(T):
                        wait_multiplied(a, "pgate", 4 * c + 3, it, 8)
                        a.activation(nat[:, t, bass.ds(c * BAND + it * 2 * BAND, BAND)],
                                     out_bank("pgate", 2 * c + t)[:, :], ACT.Sigmoid).then_inc(taken, 1)
            root(7)

            root(8)
            a.wait_ge(sem("modc_ready"), 1)
            turn_out(nc.scalar, "n5", KD, lambda k: xT[:, k, :], lambda k: modc[:, 0, k:k + 1],
                     lambda k: modc[:, 1, k:k + 1])
            for c in range(2):
                for t in range(T):
                    wait_multiplied(a, "lat", 4 * c + 3)
                    ps = out_bank("lat", 2 * c + t)
                    a.activation(lat[:, t, c * LAT:(c + 1) * LAT], ps[:, :], ACT.Copy)
                    a.wait_ge(taken, out_no("lat", 2 * c + t))
                    a.activation(silu_junk, ps[:, :], ACT.Square, accum_out=ssq[:, t, c:c + 1]).then_inc(taken, 1)
            for t in range(T):
                copy_out("kr", t, rot[:, t, 8 * 64:9 * 64], chunk=0, width=64)
            a.wait_ge(sem("rms_in"), 9)
            a.activation(st[:, 8:12], st[:, 4:8], ACT.Sqrt).then_inc(sem("root_out"), 1)
            with loop(a, 2) as it:
                for c in range(2):
                    for t in range(T):
                        wait_multiplied(a, "qk2", 4 * c + 3, it, 8)
                        a.activation(qkv2[:, t, bass.ds(c * BAND + it * 2 * BAND, BAND)],
                                     out_bank("qk2", 2 * c + t)[:, :], ACT.Copy).then_inc(taken, 1)
            turn_out(nc.scalar, "n6", 2 * KL, lambda k: latT[:, k, :], gain("g_q_lat"))
            for c in range(2):
                for t in range(T):
                    copy_out("v2", 2 * c + t, qkv2[:, t, 2 * DA + c * BAND:2 * DA + (c + 1) * BAND], chunk=4 * c + 3)
            turn_out(nc.scalar, "tq", 2 * NH, lambda k: natT[:, k, :])
            a.wait_ge(sem("rope_done"), 1)
            for h in range(NH):
                copy_out("mla", h, aux[:, 0, h * S:(h + 1) * S], chunk=h // 4, width=S)
            for t in range(T):
                copy_out("mla", 8 + t, rot[:, t, 0:512], chunk=2)
            for h in range(NH):
                copy_out("mla", 10 + h, aux[:, 1, h * S:(h + 1) * S], chunk=3 + h // 4, width=S)
            for c in range(2):
                for t in range(T):
                    copy_out("mla", 18 + 2 * c + t, v2n[:, t, c * BAND:(c + 1) * BAND], chunk=5 + c)
            turn_out(nc.scalar, "tr", 9, lambda k: rotT[0:64, k, :], width=64)
            attention_act(a, "at2", scratch2)
            a.wait_ge(sem("at2_out"), NH)
            attention_act(a, "at3", scratch2)
            a.wait_ge(sem("rms_in"), 10)
            a.activation(st[:, 8:12], st[:, 4:8], ACT.Sqrt).then_inc(sem("root_out"), 1)

            def upper_wo(n, it=0, per=0, first=False):
                a.wait_ge(raw_loaded[n % RAW], 16 * (SPLIT_WO // RAW + n // RAW + 1) + 16 * (per // RAW) * it)
                if not first:
                    wait_multiplied(a, "wo", n - PARTS, it, per)
                a.activation(part_hi[n % PARTS], raw[n % RAW], ACT.Copy).then_inc(sem("hi_ready"), 1)

            wait_multiplied(a, "wo", -1)
            for n in range(PARTS):
                upper_wo(n, first=True)
            split_turn_hi(a, "mix", KD, mix_hi, gain("g_out_a"))
            with loop(a, 4) as it:
                for n in range(PARTS):
                    upper_wo(PARTS + n, it, PARTS)
            root(11)
            root(12)
            a.wait_ge(sem("modc_ready"), 2)
            split_turn_hi_mod(a, "h2", KD, h2_hi)

            def query(j, it):
                wait_multiplied(a, "pq", j, it, 8)
                if j >= 2:
                    a.wait_ge(sem("scores"), it * 8 + j - 1)
                a.activation(qb[:, j % 2, :], out_bank("pq", j)[:, 0:S], ACT.Copy).then_inc(taken, 1)

            def score_copy(j, it):
                a.wait_ge(sem("scores"), it * 8 + j + 1)
                to = score[:, j, :] if isinstance(it, int) else \
                    score[:, bass.ds(it * 8 + j, 1), :].rearrange("p o c -> p (o c)")
                a.activation(to, bank[4 + j % 2][:, 0:S], ACT.Copy).then_inc(sem("score_out"), 1)

            with loop(a, 2) as it:
                for j in range(8):
                    upper_wo(16 + PARTS + j, it, 8)
                    query(j, it)
                    if j:
                        score_copy(j - 1, it)
                score_copy(7, it)

            def upper(j, it=0, first=False):
                a.wait_ge(raw_loaded[j % RAW], 16 * (SPLIT_EXP // RAW + j // RAW + 1) + 16 * it)
                if not first:
                    a.wait_ge(sem("expert_used"), j - PARTS + 1 + PARTS * it)
                a.activation(part_hi[j % PARTS], raw[j % RAW], ACT.Copy).then_inc(
                    sem("hi_ready"), 1)

            def gelu(j, it=0, first=False):
                a.wait_ge(sem("expert_used"), j + 1 + PARTS * it)
                if j % 2 == 0 and not first:
                    a.wait_ge(gelu_stored[j // 2 % 2], 16 * (j // 4) + 16 * it)
                a.activation(gelu_out[:, j // 2 % 2, (j % 2) * S:(j % 2 + 1) * S], bank[j % 4][:, 0:S], ACT.Gelu)\
                    .then_inc(sem("gelu_done"), 1)
                if j % 2:
                    a.wait_ge(sem("gelu_done"), j + 1 + PARTS * it)
                    if isinstance(it, int):
                        a.dma_start(gelu_dram[:, (j - 1) * S:(j + 1) * S], gelu_out[:, j // 2 % 2, :]).then_inc(
                            gelu_stored[j // 2 % 2], 16)
                    else:
                        a.dma_start(gelu_dram[:, bass.ds(((j - 1) + PARTS * it) * S, 2 * S)],
                                    gelu_out[:, j // 2 % 2, :]).then_inc(gelu_stored[j // 2 % 2], 16)

            def choice_exp(n):
                a.wait_ge(sem("topk_exp_in"), n + 1)
                a.activation(tk_val.rearrange("p t h k -> p (t h k)"),
                             tk_abf[:, 0].rearrange("p t h k -> p (t h k)"), ACT.Exp).then_inc(sem("topk_exp_out"), 1)

            choice_exp(0)
            for j in range(PARTS):
                upper(PARTS + j)
                gelu(j, first=True)
            with loop(a, POOL_LOW // PARTS - 2) as it:
                for j in range(PARTS):
                    upper(2 * PARTS + j, it)
                    gelu(PARTS + j, it)
            choice_exp(1)
            done = POOL_LOW // PARTS - 2
            with loop(a, NEB // PARTS - 2 - done) as it:
                for j in range(PARTS):
                    upper((2 + done) * PARTS + j, it)
                    gelu((1 + done) * PARTS + j, it)

            def coefficients_hi(q, it=0, first=False):
                a.wait_ge(sem("coef_raw"), q + 1 + PARTS // 2 * it)
                if not first:
                    a.wait_ge(sem("expert_used"), NEB + 2 * q - 2 + PARTS * it)
                a.activation(coef_hi[:, q % 2, :], weight_in[:, q % 2, :], ACT.Copy).then_inc(sem("coef_hi_ready"), 1)

            coefficients_hi(0, first=True)
            for j in range(PARTS):
                upper(NEB + j)
                gelu(NEB - PARTS + j)
            coefficients_hi(1, first=True)
            for j in range(2):
                upper(NEB + PARTS + j)
            with loop(a, NEB // PARTS - 2) as it:
                for q in range(2):
                    coefficients_hi(2 + q, it)
                    for j in (2 * q, 2 * q + 1):
                        upper(NEB + PARTS + 2 + j, it)
            coefficients_hi(NEB // 2 - 2)
            for j in range(2):
                upper(2 * NEB - 2 + j)
            coefficients_hi(NEB // 2 - 1)
            for t in range(T):
                root(13 + t)

        @block.vector
        def _(v):
            steps = Steps(v, "dve_step")
            link, mark, wait = steps.link, steps.mark, steps.wait
            rms_n = [0]

            def roots(count, eps, n=2, src=0, dst=16, parts=None):
                rms_n[0] += 1
                v.tensor_scalar(st[:, src:src + n], st[:, src:src + n], 1.0 / count, eps, ALU.mult, ALU.add)\
                    .then_inc(sem("rms_in"), 1)
                v.wait_ge(sem("root_out"), rms_n[0])
                got = st[:, 2:4] if n == 2 else st[:, 8:12]
                link(v.reciprocal(st[:, dst:dst + n], got))

            v.memset(ones[:, :], 1.0).then_inc(sem("ones_set"), 1)
            mark(v.memset(xrT[:, :, 0:2], 0.0))
            v.memset(xrT[:, :, 2 + S:XP], 0.0).then_inc(sem("xr_padded"), 1)
            v.wait_ge(sem("cols_in"), 16)
            lam = cols[:, COLS["lam"]:COLS["lam"] + 2 * RB]
            link(v.tensor_scalar(sp[:, 0, :], lam, -1.0, None, ALU.mult))
            v.tensor_tensor(sp[:, 0, :], sp[:, 0, :], lam, ALU.max).then_inc(sem("softplus_in"), 1)
            v.wait_ge(sem("x_in"), 16 * T)
            for t in range(T):
                mark(v.tensor_tensor_reduce(nat[:, t, :], resid[:, t, :], resid[:, t, :], 1.0, 0.0, ALU.mult, ALU.add,
                                            st[:, t:t + 1]))
            wait()
            roots(D, EPS)
            mark(v.tensor_scalar(nat[:, 0, :], resid[:, 0, :], st[:, 16:17], None, ALU.mult))
            wait()
            v.tensor_scalar(nat[:, 1, :], resid[:, 1, :], st[:, 17:18], None, ALU.mult).then_inc(sem("hn_ready"), 1)
            v.wait_ge(sem("softplus_exp"), 1)
            link(v.tensor_scalar(sp[:, 2, :], sp[:, 1, :], 2.0, None, ALU.add))
            link(v.reciprocal(sp[:, 2, :], sp[:, 2, :]))
            link(v.tensor_tensor(sp[:, 1, :], sp[:, 1, :], sp[:, 2, :], ALU.mult))
            link(v.tensor_tensor(sp[:, 2, :], sp[:, 1, :], sp[:, 1, :], ALU.mult))
            link(v.tensor_scalar(sp[:, 3, :], sp[:, 2, :], 1.0 / 17, 1.0 / 15, ALU.mult, ALU.add))
            for m in (13, 11, 9, 7, 5, 3, 1):
                link(v.tensor_tensor(sp[:, 3, :], sp[:, 3, :], sp[:, 2, :], ALU.mult))
                link(v.tensor_scalar(sp[:, 3, :], sp[:, 3, :], 1.0 / m, None, ALU.add))
            link(v.tensor_tensor(sp[:, 3, :], sp[:, 3, :], sp[:, 1, :], ALU.mult))
            link(v.tensor_scalar(sp[:, 3, :], sp[:, 3, :], 8.0, None, ALU.mult))
            link(v.tensor_scalar(sp[:, 0, :], lam, -4.0, 0.0, ALU.mult, ALU.max))
            v.tensor_tensor(sp[:, 3, :], sp[:, 3, :], sp[:, 0, :], ALU.add).then_inc(sem("softplus_in"), 1)
            turn_out(nc.vector, "n1", KD, lambda k: xT[:, k, :], gain("g_mix_pre"))

            cw = lambda j, b: cols[:, COLS["conv_w"] + j * RB + b:COLS["conv_w"] + j * RB + b + 1]
            v.wait_ge(sem("xr_padded"), 1)
            for b in range(RB):
                v.wait_ge(taken, out_no("xr", b) + 1)
                tmp = conv_tmp[:, b % 2, :]
                link(v.tensor_scalar(tmp, xrT[:, b, 0:S], cw(0, b), cols[:, COLS["conv_b"] + b:COLS["conv_b"] + b + 1],
                                     ALU.mult, ALU.add))
                for j in (1, 2):
                    link(v.scalar_tensor_tensor(out=tmp, in0=xrT[:, b, j:j + S], scalar=cw(j, b), in1=tmp,
                                                op0=ALU.mult, op1=ALU.add))
                v.scalar_tensor_tensor(out=xcT[:, b, :], in0=xrT[:, b, 3:3 + S], scalar=cw(3, b), in1=tmp,
                                       op0=ALU.mult, op1=ALU.add).then_inc(sem("conv_done"), 1)
                v.wait_ge(sem("conv_done"), b + 1)

            recA, recB = nat[:, 0, :], nat[:, 1, :]
            recU, recH = aux[:, 0, :], aux[:, 1, :]
            xc2 = xcT.rearrange("p b s -> p (b s)")

            def rec_gates(z):
                v.wait_ge(sem("gates_ready"), z + 1)
                link(v.tensor_scalar(recB, recA, 1.0, None, ALU.add))
                link(v.reciprocal(recB, recB))
                link(v.scalar_tensor_tensor(out=recA, in0=recA, scalar=2.0, in1=recB, op0=ALU.mult, op1=ALU.mult))
                v.scalar_tensor_tensor(out=recB, in0=recA, scalar=-2.0, in1=recA, op0=ALU.add, op1=ALU.mult)\
                    .then_inc(sem("rec_b2"), 1)
                v.wait_ge(sem("rec_b2"), z + 1)
                link(v.tensor_scalar(recA, recA, -1.0, 1.0, ALU.mult, ALU.add))
                link(v.tensor_tensor(recU, recU, xc2, ALU.mult))
                first = 0 if z == 0 else S - 1
                link(v.memset(recA.rearrange("p (b s) -> p b s", b=RB)[:, :, first:first + 1], 0.0))

            def rec_scan(z):
                v.wait_ge(sem("rec_root"), z + 1)
                link(v.tensor_tensor(recB, recB, recU, ALU.mult))
                if z == 0:
                    v.tensor_tensor_scan(recH, recA, recB, 0.0, ALU.mult, ALU.add).then_inc(sem("rec_scan"), 1)
                else:
                    v.tensor_tensor_scan(recU[:, ::-1], recA[:, ::-1], recB[:, ::-1], 0.0, ALU.mult, ALU.add)\
                        .then_inc(sem("rec_scan"), 1)
                v.wait_ge(sem("rec_scan"), z + 1)

            rec_gates(0)
            rec_scan(0)
            rec_gates(1)
            rec_scan(1)
            link(v.tensor_tensor(recH, recH, recU, ALU.add))
            v.wait_ge(taken, out_no("q", 0))
            v.tensor_tensor(recH, recH, ygT.rearrange("p b s -> p (b s)"), ALU.mult).then_inc(sem("rec_sum"), 1)
            v.wait_ge(sem("rec_sum"), 1)

            v.wait_ge(sem("bias_masked"), 4)

            def bias_1(h, t):
                at = 2 - 2 * t
                return bias1[:, h, at:at + 4, ::-1]

            attention_dve(v, steps, "at1", bias_1, float(HD) ** -0.5,
                          lambda h, t: attn1[:, t, h * HD:(h + 1) * HD], scratch1)
            for t in range(T):
                link(v.tensor_tensor_reduce(recB.rearrange("p (a c) -> p a c", a=2)[:, 0, :], attn1[:, t, :],
                                            attn1[:, t, :], 1.0, 0.0, ALU.mult, ALU.add, st[:, t:t + 1]))
            roots(DA, EPS)
            for t in range(T):
                i = v.tensor_scalar(attn1[:, t, :], attn1[:, t, :], st[:, 16 + t:17 + t], None, ALU.mult)
                if t == 0:
                    link(i)
            i.then_inc(sem("attn1_ready"), 1)
            turn_out(nc.vector, "n2", 8, lambda k: xT[:, k, :], gain("g_attn_out"))
            v.wait_ge(sem("rec_norm"), 1)
            v.tensor_scalar(conv_tmp[:, 0, :], bank[4][:, 0:S], 1.0 / DA, EPS, ALU.mult, ALU.add).then_inc(
                sem("rec_norm"), 1)
            v.wait_ge(sem("rec_norm"), 3)
            link(v.reciprocal(conv_tmp[:, 1, :], conv_tmp[:, 0, :]))
            for b in range(RB):
                v.scalar_tensor_tensor(out=xT[:, 8 + b, :], in0=recH[:, b * S:(b + 1) * S], scalar=gain("g_rec_out")(b),
                                       in1=conv_tmp[:, 1, :], op0=ALU.mult, op1=ALU.mult).then_inc(
                    sem("rec_normed"), 1)
            v.wait_ge(sem("rec_normed"), RB)
            v.memset(conv_tmp[:, :, :], 0.0).then_inc(sem("zeros_set"), 1)
            v.memset(mxs[:, 0, 0:1], 0.0).then_inc(sem("ada_used"), ADA_SLOTS)
            v.wait_ge(sem("ada_used"), ADA_SLOTS)
            v.memset(mxs[:, 0, 0:1], 0.0).then_inc(sem("aux_free"), 1)
            v.wait_ge(sem("aux_free"), 1)
            v.memset(mxs[:, 0, 0:1], 0.0).then_inc(sem("ada_rowsum"), 1)

            def sum_ssq():
                link(v.tensor_reduce(st[:, 0:2], ssq[:, :, :], AXX, ALU.add))

            def add_normed(row, n0):
                for t in range(T):
                    for c in range(4):
                        s = slice(c * BAND, (c + 1) * BAND)
                        link(v.scalar_tensor_tensor(out=nat[:, t, s], in0=nat[:, t, s], scalar=st[:, 16 + t:17 + t],
                                                    in1=row[:, s], op0=ALU.mult, op1=ALU.mult))
                        v.tensor_tensor(resid[:, t, s], resid[:, t, s], nat[:, t, s], ALU.add).then_inc(
                            sem("resid_piece"), 1)
                v.wait_ge(sem("resid_piece"), n0 + 8)

            def normed(n, name, g):
                v.wait_ge(sem("ssq_in"), n)
                sum_ssq()
                roots(D, EPS)
                link(v.tensor_scalar(nat[:, 0, :], resid[:, 0, :], st[:, 16:17], None, ALU.mult))
                v.tensor_scalar(nat[:, 1, :], resid[:, 1, :], st[:, 17:18], None, ALU.mult).then_inc(sem("hn_ready"), 1)
                if name == "h3":
                    split_turn_lo(v, "h3", KD, h3_hi, h3_lo, gain(g))
                else:
                    turn_out(nc.vector, name, KD, lambda k: xT[:, k, :], gain(g))

            v.wait_ge(sem("cact_ready"), 1)

            def ada(k, g):
                s = k % ADA_SLOTS
                v.wait_ge(ada_loaded[s // 2], 16 * (KD // ADA_SLOTS) * g + 16 * (k // ADA_SLOTS + 1))
                if k == 0:
                    v.wait_ge(sem("ada_rowsum"), g + 1)
                    i = v.tensor_scalar(ada_acc, ada_ring[:, s, :], cact[:, k:k + 1], None, ALU.mult)
                else:
                    v.wait_ge(sem("ada_used"), ADA_SLOTS + KD * g + k)
                    i = v.scalar_tensor_tensor(out=ada_acc, in0=ada_ring[:, s, :], scalar=cact[:, k:k + 1],
                                               in1=ada_acc, op0=ALU.mult, op1=ALU.add)
                i.then_inc(sem("ada_used"), 1)

            def ada_end(g):
                v.wait_ge(sem("ada_used"), ADA_SLOTS + KD * g + KD)
                v.memset(mxs[:, 0, 1:2], 0.0).then_inc(sem("ada_sum"), 1)

            def ada_row(g):
                v.wait_ge(sem("ada_rowsum"), g + 2)
                v.wait_ge(sem("mod_b_in"), 16 * g + 16)
                v.tensor_tensor(mod_row[0:1, :], bank[4][0:1, 0:ADA_W], mod_row[0:1, :], ALU.add).then_inc(
                    sem("mod_ready"), 1)

            with steps.loop(ADA_EARLY, 0) as it:
                for k in range(KD):
                    ada(k, it)
                ada_end(it)
                ada_row(it)

            v.wait_ge(taken, out_no("gateup", 0))
            sum_ssq()
            roots(D, EPS)
            v.wait_ge(sem("row_in"), 16)
            add_normed(aux[:, 0, :], 0)
            normed(8, "h3", "g_ffn_pre")
            wait()

            def hidden(j, it):
                v.wait_ge(sem("silu_done"), it * 4 + j + 1)
                wait_multiplied(v, "gateup", 2 * j + 1, it, 8)
                v.tensor_tensor(big[:, bass.ds(j * S + it * 4 * S, S)], out_bank("gateup", 2 * j + 1)[:, 0:S],
                                silu_g[:, j % 2, :], ALU.mult).then_inc(taken, 2)

            def ffn_lower(j, it=0, first=False):
                v.wait_ge(sem("hi_ready"), j + 1 + 8 * it)
                if not first:
                    wait_multiplied(v, "gateup", j - 2, it, 8)
                v.tensor_tensor(ffn_lo[j % 2], ffn_raw[j % RAW], ffn_hi[j % PARTS].bitcast(F32), ALU.subtract)\
                    .then_inc(sem("lo_ready"), 1)

            def gateup_round(it, first=False, last=False):
                for c in range(8):
                    if not (last and c >= 6):
                        ffn_lower(2 + c, it)
                    if c % 2:
                        hidden(c // 2, it)
                    ada(2 * c, ADA_EARLY + it)
                    ada(2 * c + 1, ADA_EARLY + it)
                    if c == 1 and not first:
                        ada_row(ADA_EARLY - 1 + it)
                ada_end(ADA_EARLY + it)

            ffn_lower(0, first=True)
            ffn_lower(1, first=True)
            gateup_round(0, first=True)
            with steps.loop(KF // 4 - 2, 0) as it:
                gateup_round(it + 1)
            gateup_round(KF // 4 - 1, last=True)
            ada_row(ADA_FFN - 1)
            for g in range(ADA_FFN, ADA_G):
                for k in range(KD):
                    ada(k, g)
                ada_end(g)
                ada_row(g)

            v.wait_ge(taken, out_no("pproj", 0))
            sum_ssq()
            roots(D, EPS)
            v.wait_ge(sem("row2_in"), 16)
            add_normed(aux[:, 1, :], 8)
            v.memset(mxs[:, 0, 0:1], 0.0).then_inc(row_used, 1)
            normed(16, "n4", "g_ple_pre")
            v.wait_ge(sem("row3_in"), 16)
            for c in range(4):
                for t in range(T):
                    s = slice(c * BAND, (c + 1) * BAND)
                    v.wait_ge(taken, out_no("pgate", 2 * c + t) + 1)
                    link(v.tensor_tensor(nat[:, t, s], nat[:, t, s], ple[:, t, s], ALU.mult))
                    link(v.tensor_tensor_reduce(ple[:, t, s], nat[:, t, s], nat[:, t, s], 1.0, 0.0, ALU.mult, ALU.add,
                                                ssq[:, t, c:c + 1]))
                    mark(v.tensor_tensor(nat[:, t, s], nat[:, t, s], aux[:, 0, s], ALU.mult))
            wait()
            sum_ssq()
            roots(D, EPS)
            for t in range(T):
                link(v.scalar_tensor_tensor(out=resid[:, t, :], in0=nat[:, t, :], scalar=st[:, 16 + t:17 + t],
                                            in1=resid[:, t, :], op0=ALU.mult, op1=ALU.add))

            def layer_stats(n, t0=0, tn=T, stats_done=False):
                for t in range(t0, tn) if not stats_done else ():
                    for c in range(4):
                        mark(v.bn_stats(stats[:, t, c, :], resid[:, t, c * BAND:(c + 1) * BAND]))
                wait()
                for t in range(t0, tn):
                    mark(v.bn_aggr(mv[:, t, :], stats[:, t, :, :].rearrange("p c s -> p (c s)")))
                wait()
                rms_n[0] += 1
                v.tensor_scalar(st[:, 0:2], mv[:, :, 1:2].rearrange("p t o -> p (t o)"), EPS_LN, None, ALU.add)\
                    .then_inc(sem("rms_in"), 1)
                v.wait_ge(sem("root_out"), rms_n[0])
                link(v.reciprocal(st[:, 16:18], st[:, 2:4]))

            def layer_normed(dst, t):
                return v.tensor_scalar(dst[:, t, :], resid[:, t, :], mv[:, t, 0:1], st[:, 16 + t:17 + t],
                                       ALU.subtract, ALU.mult)

            v.wait_ge(sem("modc_in"), 32)
            v.tensor_scalar(modc[:, 0, :], modc[:, 0, :], 1.0, None, ALU.add).then_inc(sem("modc_ready"), 1)
            layer_stats(0)
            link(layer_normed(nat, 0))
            layer_normed(nat, 1).then_inc(sem("hn_ready"), 1)
            v.wait_ge(sem("modc_ready"), 1)
            turn_out(nc.vector, "n5", KD, lambda k: xT[:, k, :], lambda k: modc[:, 0, k:k + 1],
                     lambda k: modc[:, 1, k:k + 1])
            v.wait_ge(taken, out_no("kr", 0))
            link(v.tensor_copy(st[:, 4:8].rearrange("p (t c) -> p t c", t=T), ssq[:, :, 0:2]))
            rms_n[0] += 1
            v.tensor_scalar(st[:, 4:8], st[:, 4:8], 1.0 / LAT, EPS, ALU.mult, ALU.add).then_inc(sem("rms_in"), 1)
            v.wait_ge(sem("root_out"), rms_n[0])
            link(v.reciprocal(st[:, 20:24], st[:, 8:12]))
            for t in range(T):
                for c in range(2):
                    i = v.tensor_scalar(lat[:, t, c * LAT:(c + 1) * LAT], lat[:, t, c * LAT:(c + 1) * LAT],
                                        st[:, 20 + 2 * t + c:21 + 2 * t + c], None, ALU.mult)
                    if t == T - 1 and c == 1:
                        i.then_inc(sem("lat_ready"), 1)
                    else:
                        link(i)

            def rope(view, heads, half, tab, scr):
                n = heads * half
                for t in range(T):
                    x = view(t)
                    x1, x2 = x[:, :, 0:half], x[:, :, half:2 * half]
                    cos = rope_t[:, t, tab:tab + half].unsqueeze(1).to_broadcast([P, heads, half])
                    sin = rope_t[:, t, tab + half:tab + 2 * half].unsqueeze(1).to_broadcast([P, heads, half])
                    w = [scr[:, i * 288:i * 288 + n].rearrange("p (h c) -> p h c", h=heads) for i in range(4)]
                    for dst, p, q in ((w[0], x1, cos), (w[1], x2, sin), (w[2], x2, cos), (w[3], x1, sin)):
                        mark(v.tensor_tensor(dst, p, q, ALU.mult))
                    wait()
                    mark(v.tensor_tensor(x1, w[0], w[1], ALU.subtract))
                    mark(v.tensor_tensor(x2, w[2], w[3], ALU.add))
                    wait()

            turn_out(nc.vector, "n6", 2 * KL, lambda k: latT[:, k, :], gain("g_q_lat"))
            v.wait_ge(taken, out_no("v2", 0))
            rope(lambda t: qkv2[:, t, 0:2 * DA].rearrange("p (h c) -> p h c", h=2 * NH), 2 * NH, ROT_A, 0, auxf)
            v.memset(mxs[:, 0, 0:1], 0.0).then_inc(sem("rope_done"), 1)
            turn_out(nc.vector, "tq", 2 * NH, lambda k: natT[:, k, :])
            v.wait_ge(taken, out_no("mla", 10))
            rope(lambda t: rot[:, t, :].rearrange("p (h c) -> p h c", h=9), 9, ROT_B, 2 * ROT_A,
                 xT[:, :, :].rearrange("p k s -> p (k s)"))
            v.memset(mxs[:, 0, 0:1], 0.0).then_inc(sem("rotq_ready"), 1)
            turn_out(nc.vector, "tr", 9, lambda k: rotT[0:64, k, :], width=64)
            v.wait_ge(sem("misc_in"), 16)
            attention_dve(v, steps, "at2", lambda h, t: by_row(masks[:, 0, t, :]), float(HD) ** -0.5,
                          lambda h, t: o2[:, t, h * HD:(h + 1) * HD], scratch2)
            attention_dve(v, steps, "at3", lambda h, t: by_row(masks[:, 1, t, :]), float(HD + 64) ** -0.5,
                          lambda h, t: o2[:, t, DA + h * HD:DA + (h + 1) * HD], scratch2)
            for t in range(T):
                for c in range(2):
                    link(v.tensor_tensor_reduce(auxf[:, 0:DA], o2[:, t, c * DA:(c + 1) * DA],
                                                o2[:, t, c * DA:(c + 1) * DA], 1.0, 0.0, ALU.mult, ALU.add,
                                                st[:, 4 + 2 * t + c:5 + 2 * t + c]))
            rms_n[0] += 1
            v.tensor_scalar(st[:, 4:8], st[:, 4:8], 1.0 / DA, EPS, ALU.mult, ALU.add).then_inc(sem("rms_in"), 1)
            v.wait_ge(sem("root_out"), rms_n[0])
            link(v.reciprocal(st[:, 20:24], st[:, 8:12]))
            for t in range(T):
                for c in range(2):
                    link(v.tensor_scalar(o2[:, t, c * DA:(c + 1) * DA], o2[:, t, c * DA:(c + 1) * DA],
                                         st[:, 20 + 2 * t + c:21 + 2 * t + c], None, ALU.mult))
            v.memset(mxs[:, 0, 0:1], 0.0).then_inc(sem("o_ready"), 1)
            split_turn_lo(v, "mix", KD, mix_hi, mix_lo, gain("g_out_a"))

            def lower_wo(n):
                v.wait_ge(sem("hi_ready"), SPLIT_WO + n + 1)
                if n >= 2:
                    wait_multiplied(v, "wo", n - 2)
                v.tensor_tensor(wo_lo[n % 2], raw[n % RAW], part_hi[n % PARTS].bitcast(F32), ALU.subtract).then_inc(
                    sem("lo_ready"), 1)

            def deep_norm_piece(t, s, mix, row, dst, count=None):
                i = v.tensor_tensor(dst[:, t, s], mix, row[:, s], ALU.mult)
                if count is None:
                    link(i)
                else:
                    i.then_inc(taken, 1)
                    v.wait_ge(taken, count)
                link(v.scalar_tensor_tensor(out=resid[:, t, s], in0=resid[:, t, s], scalar=ALPHA, in1=dst[:, t, s],
                                            op0=ALU.mult, op1=ALU.add))
                mark(v.bn_stats(stats[:, t, s.start // BAND, :], resid[:, t, s]))

            lower_wo(0)
            lower_wo(1)
            v.wait_ge(sem("rows_in"), 16 * 3)
            for n in range(16):
                if n + 2 < 16:
                    lower_wo(n + 2)
                if n % 4 == 3:
                    for t in range(T):
                        c = n // 4
                        wait_multiplied(v, "wo", n)
                        deep_norm_piece(t, slice(c * BAND, (c + 1) * BAND), out_bank("wo", 2 * c + t)[:, :],
                                        rows[:, 0, :], o2, out_no("wo", 2 * c + t + 1))

            def scaled(t, r):
                link(layer_normed(resid, t))
                link(v.tensor_tensor(resid[:, t, :], resid[:, t, :], r[1], ALU.mult))
                return v.tensor_tensor(resid[:, t, :], resid[:, t, :], r[2], ALU.add)

            layer_stats(1, stats_done=True)
            for t in range(T):
                link(scaled(t, [rows[:, n, :] for n in range(3)]))
            v.wait_ge(sem("modc_in"), 64)
            v.tensor_scalar(modc[:, 0, :], modc[:, 0, :], 1.0, None, ALU.add).then_inc(sem("modc_ready"), 1)
            layer_stats(2)
            for t in range(T):
                link(layer_normed(normed2, t))
            v.memset(mxs[:, 0, 0:1], 0.0).then_inc(sem("h2_ready"), 1)
            v.wait_ge(sem("h2_ready"), 1)
            v.memset(mxs[:, 0, 0:1], 0.0).then_inc(sem("score_out"), 2)
            v.wait_ge(sem("modc_ready"), 2)
            split_turn_lo_mod(v, "h2", KD, h2_hi, h2_lo, mod_tmp, steps)

            def top16(vals, idxs, src, tmp):
                link(v.max(vals[:, 0:8], src))
                link(v.max_index(idxs[:, 0:8], vals[:, 0:8], src))
                link(v.match_replace(out=tmp, in_to_replace=vals[:, 0:8], in_values=src, imm_value=-3.0e38))
                link(v.max(vals[:, 8:16], tmp))
                return v.max_index(idxs[:, 8:16], vals[:, 8:16], tmp)

            v.wait_ge(sem("iota_done"), 2)
            for t in range(T):
                link(v.tensor_scalar(token[:, t:t + 1], tokbase, float(t * P), None, ALU.add))
            for it in range(2):
                for j in range(8):
                    v.wait_ge(sem("score_out"), 2 + it * 8 + j + 1)
                    for t in range(T):
                        link(top16(tk_v12[:, t, j // 2, j % 2, :], tk_i12[:, t, j // 2, j % 2, :],
                                   score[:, it * 8 + j, t * P:(t + 1) * P], tk_tmp[:, 0:P]))
                link(v.tensor_copy(auxf[:, 512:768], auxf[:, 256:512].bitcast(U32)))
                for t in range(T):
                    link(v.tensor_tensor(tk_cand, tk_v12[:, t, :, 0, :].unsqueeze(3).to_broadcast([P, 4, 16, 16]),
                                         tk_v12[:, t, :, 1, :].unsqueeze(2).to_broadcast([P, 4, 16, 16]), ALU.add))
                    for h in range(4):
                        link(top16(tk_val[:, t, h, :], tk_ci[:, t, h, :],
                                   tk_cand[:, h].rearrange("p i j -> p (i j)"), tk_tmp))
                ci = tk_ci.rearrange("p t h k -> p (t h k)")
                link(v.tensor_scalar(tk_ab[:, 0, :], ci, 4, None, ALU.logical_shift_right))
                link(v.tensor_scalar(tk_ab[:, 1, :], ci, 15, None, ALU.bitwise_and))
                link(v.tensor_copy(auxf[:, 2560:2816], auxf[:, 2304:2560].bitcast(U32)))
                for t in range(T):
                    for a_ in range(2):
                        link(v.tensor_tensor(tk_hot, tk_abf[:, a_, t].rearrange("p h k -> p (h k)").unsqueeze(2)
                                             .to_broadcast([P, 64, 16]),
                                             iota16.unsqueeze(1).to_broadcast([P, 64, 16]), ALU.is_equal))
                        hot4 = tk_hot.rearrange("p (h o) k -> p h o k", h=4)
                        link(v.tensor_tensor(hot4, hot4, tk_f12[:, t, :, a_, :].unsqueeze(2)
                                             .to_broadcast([P, 4, 16, 16]), ALU.mult))
                        link(v.tensor_reduce(tk_pick[:, a_, :], tk_hot, AXX, ALU.add))
                    link(v.tensor_scalar(tk_pick[:, 1, :], tk_pick[:, 1, :], float(NEB * S), token[:, t:t + 1],
                                         ALU.mult, ALU.add))
                    link(v.scalar_tensor_tensor(out=tk_pick[:, 0, :], in0=tk_pick[:, 0, :], scalar=float(S),
                                                in1=tk_pick[:, 1, :], op0=ALU.mult, op1=ALU.add))
                    link(v.tensor_copy(gidx[:, t, it * 64:it * 64 + 64], tk_pick[:, 0, :]))
                val8 = tk_val.rearrange("p t h k -> p (t h) k")
                v.tensor_tensor(tk_abf[:, 0].rearrange("p t h k -> p (t h) k"), val8,
                                val8[:, :, 0:1].to_broadcast([P, T * 4, 16]), ALU.subtract).then_inc(
                    sem("topk_exp_in"), 1)
                v.wait_ge(sem("topk_exp_out"), it + 1)
                link(v.tensor_reduce(tk_sum[:, 0:8], val8, AXX, ALU.add))
                link(v.reciprocal(tk_sum[:, 8:16], tk_sum[:, 0:8]))
                link(v.tensor_tensor(val8, val8, tk_sum[:, 8:16].unsqueeze(2).to_broadcast([P, 8, 16]), ALU.mult))
                link(v.tensor_copy(gwt[:, :, it * 64:it * 64 + 64], tk_val.rearrange("p t h k -> p t (h k)")))
            v.memset(mxs[:, 0, 0:1], 0.0).then_inc(sem("chosen"), 1)

            def lower(j, it=0):
                v.wait_ge(sem("hi_ready"), SPLIT_EXP + j + 1 + PARTS * it)
                v.tensor_tensor(part_lo[j % PARTS], raw[j % RAW],
                                part_hi[j % PARTS].bitcast(F32), ALU.subtract).then_inc(sem("lo_ready"), 1)

            def coefficients(q, it=0):
                v.wait_ge(pair_loaded[q % 2], 32 * (q // 2 + 1) + 32 * it)
                v.tensor_tensor(weight_in[:, q % 2, :], weight_in[:, q % 2, :], gelu_in[:, q % 2, :], ALU.mult)\
                    .then_inc(sem("coef_raw"), 1)

            def coefficients_lo(q, it=0):
                v.wait_ge(sem("coef_hi_ready"), q + 1 + PARTS // 2 * it)
                v.tensor_tensor(coef_lo[:, q % 2, :], weight_in[:, q % 2, :], coef_hi[:, q % 2, :].bitcast(F32),
                                ALU.subtract).then_inc(sem("coef_ready"), 1)

            v.wait_ge(sem("lo_ready"), SPLIT_EXP + POOL_LOW)
            with loop(v, (NEB - POOL_LOW) // PARTS) as it:
                for j in range(PARTS):
                    lower(POOL_LOW + j, it)
            coefficients(0)
            coefficients_lo(0)
            for j in range(PARTS):
                lower(NEB + j)
            with loop(v, NEB // PARTS - 1) as it:
                for q in range(2):
                    coefficients(q + 1, it)
                    coefficients_lo(q + 1, it)
                    lower(NEB + PARTS + 2 * q, it)
                    lower(NEB + PARTS + 2 * q + 1, it)
            coefficients(NEB // 2 - 1)
            coefficients_lo(NEB // 2 - 1)
            v.wait_ge(sem("expert_used"), 2 * NEB)
            v.wait_ge(sem("rows2_in"), 48)
            for t in range(T):
                for c in range(D // BAND):
                    deep_norm_piece(t, slice(c * BAND, (c + 1) * BAND), bank[4 * t + c][:, :], last_rows[0], result)
                layer_stats(3 + t, t, t + 1, stats_done=True)
                scaled(t, last_rows).then_inc(sem("out_ready"), 1)
                v.wait_ge(sem("out_ready"), t + 1)

        @block.gpsimd
        def _(g_):
            steps = Steps(g_, "pool_step")
            g_.dma_start(cols[:, :], io["cols"]).then_inc(sem("cols_in"), 16)
            g_.dma_start(ident[:, :], io["ident"]).then_inc(sem("consts_in"), 16)
            g_.dma_start(rope_t[:, :, :], io["rope"]).then_inc(sem("consts_in"), 16)
            g_.dma_start(pT[:, :, :], io["pT"]).then_inc(sem("consts_in"), 16)
            g_.dma_start(rg_w.rearrange("p z g b c -> p (z g b c)"), io["rg"]).then_inc(sem("rg_in"), 16)
            rp = io["rpb"]
            NR, NCC = 2 * WIN_R - 1, 2 * WIN_C - 1
            for half in range(2):
                for h in range(NH):
                    src = bass.AP(tensor=rp.tensor,
                                  offset=h * NR * NCC + (WIN_R - ROWS + 1 - half) * NCC + WIN_C - GRID_W,
                                  ap=[[1, GRID_W], [NCC, 6], [1, GRID_W]])
                    g_.dma_start(bias1[GRID_W * half:GRID_W * (half + 1), h], src).then_inc(sem("bias_in"), 16)
            g_.wait_ge(sem("bias_in"), 16 * 2 * NH)
            for half in range(2):
                q = slice(GRID_W * half, GRID_W * (half + 1))
                rest = GRID_W - WIN_C
                lo = bias1[q, :, :, WIN_C:GRID_W].rearrange("p h r c -> p (h r) c")
                hi = bias1[q, :, :, 0:rest].rearrange("p h r c -> p (h r) c")
                g_.affine_select(out=lo, in_=lo, compare_op=ALU.is_ge, fill=-1e9,
                                 base=rest - 1 + WIN_C // 2, pattern=[[0, NH * 6], [-1, rest]], channel_multiplier=-1).then_inc(
                    sem("bias_masked"), 1)
                g_.wait_ge(sem("bias_masked"), 2 * half + 1)
                g_.affine_select(out=hi, in_=hi, compare_op=ALU.is_ge, fill=-1e9,
                                 base=WIN_C // 2 - GRID_W, pattern=[[0, NH * 6], [1, rest]], channel_multiplier=1).then_inc(
                    sem("bias_masked"), 1)
                g_.wait_ge(sem("bias_masked"), 2 * half + 2)

            def row_in(dst, name, s, dram=None):
                src = io["rows"][ROW_NAMES.index(name):ROW_NAMES.index(name) + 1, :] if dram is None else dram
                g_.dma_start(dst, src.to_broadcast([P, D])).then_inc(s, 16)

            g_.wait_ge(sem("aux_free"), 1)
            row_in(aux[:, 0, :], "g_mix_post", sem("row_in"))

            def mod_piece(g):
                at = bass.ds(g * ADA_W, ADA_W) if not isinstance(g, int) else slice(g * ADA_W, (g + 1) * ADA_W)
                flat = mod_dram.rearrange("(o m) d -> o (m d)", o=1)
                if not isinstance(g, int):
                    g_.wait_ge(sem("mod_out"), 16 * g)
                    g_.nop(nofuse=True)
                g_.dma_start(mod_row[0:1, :], io["b_ada"][:, at]).then_inc(sem("mod_b_in"), 16)
                g_.wait_ge(sem("mod_ready"), g + 1)
                g_.nop(nofuse=True)
                g_.dma_start(flat[:, at], mod_row[0:1, :]).then_inc(sem("mod_out"), 16)

            mod_piece(0)
            with loop(g_, ADA_G - 1) as it:
                mod_piece(it + 1)
            g_.wait_ge(multiplied, PLAN["down"]["chunk"])
            row_in(aux[:, 1, :], "g_ffn_post", sem("row2_in"))
            g_.wait_ge(sem("mod_out"), 16 * ADA_G)
            with nc.allow_non_contiguous_dma(reason="two short vectors by channel"):
                for n, m in enumerate((SC1, SH1)):
                    g_.dma_start(modc[:, n, :], mod_dram[m].rearrange("(k p) -> p k", p=P)).then_inc(
                        sem("modc_in"), 16)
            g_.wait_ge(row_used, 1)
            row_in(aux[:, 0, :], "g_ple_post", sem("row3_in"))
            wait_turned_out(g_, "n5", KD)
            with nc.allow_non_contiguous_dma(reason="two short vectors by channel"):
                for n, m in enumerate((SC2, SH2)):
                    g_.dma_start(modc[:, n, :], mod_dram[m].rearrange("(k p) -> p k", p=P)).then_inc(
                        sem("modc_in"), 16)
            g_.wait_ge(sem("lat_ready"), 1)
            g_.dma_start(masks.rearrange("p m t k -> p (m t k)"), io["masks"]).then_inc(sem("misc_in"), 16)
            g_.wait_ge(sem("zeros_set"), 1)
            g_.dma_start(weight_dram.rearrange("p (a c) -> p a c", c=2 * S),
                         conv_tmp[:, :, :].rearrange("p a s -> p (a s)").unsqueeze(1)
                         .to_broadcast([P, NEB // 2, 2 * S])).then_inc(sem("scattered"), 16)
            g_.wait_ge(sem("at3_out"), NH)
            g_.dma_start(subk.rearrange("p a k -> p (a k)"), io["subk"]).then_inc(sem("sk_in"), 16)
            g_.iota(iota16, [[1, 16]], base=0, channel_multiplier=0, allow_small_or_imprecise_dtypes=True).then_inc(
                sem("iota_done"), 1)
            g_.iota(tokbase, [[0, 1]], base=0, channel_multiplier=1, allow_small_or_imprecise_dtypes=True).then_inc(
                sem("iota_done"), 1)
            for n, (name, m) in enumerate(((None, G1), ("ln1_g", 0), ("ln1_b", 0))):
                row_in(rows[:, n, :], name, sem("rows_in"), mod_dram[m:m + 1, :] if name is None else None)
            for j in range(16):
                g_.wait_ge(sem("hi_ready"), SPLIT_PQ + j + 1)
                wait_multiplied(g_, "pq", j - 2 if j >= 2 else -1)
                g_.tensor_tensor(part_lo[j % 2], raw[j % RAW], part_hi[j % PARTS].bitcast(F32), ALU.subtract).then_inc(
                    sem("lo_ready"), 1)
            g_.wait_ge(multiplied, N_CHUNKS)
            for j in range(POOL_LOW):
                g_.wait_ge(sem("hi_ready"), SPLIT_EXP + j + 1)
                g_.tensor_tensor(part_lo[j % PARTS], raw[j % RAW],
                                 part_hi[j % PARTS].bitcast(F32), ALU.subtract).then_inc(sem("lo_ready"), 1)

            g_.wait_ge(sem("chosen"), 1)
            places = weight_dram.rearrange("p (c o) -> (p c) o", o=1)
            with loop(g_, NH) as it:
                g_.wait_ge(sem("scattered"), 16 + 16 * T * TOPK * it)
                g_.nop(nofuse=True)
                for t in range(T):
                    of_head = bass.ds(it * TOPK, TOPK)
                    g_.tensor_copy(gstage[:, t, :], gidx[:, t, of_head]).then_inc(sem("staged"), 1)
                    g_.tensor_copy(wstage[:, t, :], gwt[:, t, of_head]).then_inc(sem("staged"), 1)
                g_.wait_ge(sem("staged"), 2 * T + 2 * T * it)
                g_.nop(nofuse=True)
                for t in range(T):
                    for k in range(TOPK):
                        g_.indirect_dma_start(
                            out=places, out_offset=bass.IndirectOffsetOnAxis(ap=gstage[:, t, k:k + 1], axis=0),
                            in_=wstage[:, t, k:k + 1], in_offset=None, compute_op=ALU.add).then_inc(
                                sem("scattered"), 16)

            g_.wait_ge(sem("scattered"), 16 + 16 * T * NSEL)

            def load_pair(q, it=0):
                at = slice(2 * q * S, (2 * q + 2) * S) if isinstance(it, int) else \
                    bass.ds((2 * q + PARTS * it) * S, 2 * S)
                g_.dma_start(weight_in[:, q % 2, :], weight_dram[:, at]).then_inc(pair_loaded[q % 2], 16)
                g_.dma_start(gelu_in[:, q % 2, :], gelu_dram[:, at]).then_inc(pair_loaded[q % 2], 16)

            for q in range(2):
                g_.wait_ge(gelu_stored[q], 16)
                load_pair(q)
            for b in range(2):
                g_.wait_ge(gelu_stored[b], 16 * NEB // 4)
            with loop(g_, NEB // PARTS - 1) as it:
                for q in range(2):
                    g_.wait_ge(sem("coef_ready"), q + 1 + PARTS // 2 * it)
                    g_.nop(nofuse=True)
                    load_pair(2 + q, it)

            g_.wait_ge(sem("lo_ready"), SPLIT_EXP + 2 * NEB)
            for n, (name, m) in enumerate(((None, G2), ("ln2_g", 0), ("ln2_b", 0))):
                row_in(last_rows[n], name, sem("rows2_in"), mod_dram[m:m + 1, :] if name is None else None)


def arrange(inputs):
    f = {k: np.asarray(v) for k, v in inputs.items()}

    def stationary(w):
        n = w.shape[1] // P
        return w.reshape(KD, P, n, P).transpose(2, 1, 0, 3).reshape(n, P, CH)

    def moving(w, kq=4):
        n = w.shape[1] // BAND
        q = w.shape[0] // (kq * P)
        return w.reshape(q, kq, P, n, BAND).transpose(3, 0, 2, 1, 4).reshape(n * q, P, kq * BAND)

    def stationary_lat(w):
        return w.reshape(KL, P, 2, 4, P).transpose(2, 1, 3, 0, 4).reshape(2, P, CH)

    w_in = f["w_in"][0]
    q, k, v, xr, yg = (w_in[:, i * DA:(i + 1) * DA] for i in range(5))
    gate_up = np.stack([stationary(f["w_ffn_gate"][0]), stationary(f["w_ffn_up"][0])], 1).reshape(-1, P, CH)
    pproj = f["w_ple_proj"][0].reshape(2, P, 2, 2, BAND).transpose(2, 1, 3, 0, 4).reshape(2, P, CH)
    w2 = f["w_in_2"][0]
    qkv2, lat, kr = w2[:, :3 * DA], w2[:, 3 * DA:3 * DA + 2 * LAT], w2[:, 3 * DA + 2 * LAT:]
    kr_chunk = np.zeros((1, P, CH), w2.dtype)
    kr_chunk[0, :, :KD * 64] = kr.reshape(KD, P, 64).transpose(1, 0, 2).reshape(P, KD * 64)
    uq = f["w_uq_2"][0].reshape(LAT, NH, HD + 64)
    parts = [stationary(xr), stationary(yg), stationary(q), stationary(k), moving(v), moving(f["w_out"][0]),
             pproj, moving(f["w_ple_gate"][0]), moving(lat), kr_chunk, moving(qkv2[:, :2 * DA]),
             moving(qkv2[:, 2 * DA:]), stationary_lat(uq[:, :, :HD].reshape(LAT, DA)),
             moving(uq[:, :, HD:].reshape(LAT, 512)), stationary_lat(f["w_uk_2"][0]), moving(f["w_uv_2"][0])]
    a = {"stream": np.concatenate(parts), "gateup": gate_up,
         "wo_pq": np.concatenate([moving(f["w_o_2"][0]), stationary(f["w_pq_2"][0])]),
         "down": moving(f["w_ffn_down"][0], 11)}
    vec = {"g_mix_pre": "g_mix_pre", "g_attn_out": "g_attn_out", "g_rec_out": "g_rec_out", "g_ffn_pre": "g_ffn_pre",
           "g_ple_pre": "g_ple_pre", "g_q_lat": "g_q_lat_2", "g_kv_lat": "g_kv_lat_2", "g_out_a": "g_out_a_2",
           "g_out_b": "g_out_b_2", "conv_w": "conv_w", "conv_b": "conv_b", "b_rg_a": "b_rg_a", "b_rg_i": "b_rg_i",
           "lam": "lam", "c": "c_2"}
    a["cols"] = np.ascontiguousarray(np.concatenate([f[vec[n]].reshape(-1, P) for n in COLS], 0).T)
    a["rows"] = np.concatenate([f[n if n in f else n + "_2"].reshape(1, D) for n in ROW_NAMES], 0)
    a["rg"] = np.ascontiguousarray(np.stack([f["w_rg_a"][0], f["w_rg_i"][0]], 1).transpose(3, 0, 1, 2, 4)).reshape(P, -1)
    a["rpb"] = f["rpb"][0][:, :, ::-1]
    a["pT"] = np.ascontiguousarray(f["p"][0, 0].T.reshape(2, P, S).transpose(1, 0, 2))
    a["x"] = f["x"]
    a["w_ada"] = f["w_ada_2"][0]
    a["b_ada"] = f["b_ada_2"]
    a["subk"] = np.ascontiguousarray(np.stack([f["sub_key_1_2"][0].T, f["sub_key_2_2"][0].T], 1)).reshape(P, -1)
    a["u_table"] = stationary(f["u_table_2"][0].T)
    a["v_table"] = f["v_table_2"][0].reshape(NEB, P, D)
    a.update(shape_tables())
    return {k: np.ascontiguousarray(v) for k, v in a.items()}


def shape_tables():
    pos = np.arange(S, dtype=np.float32)
    rope = []
    for half in (ROT_A, ROT_B):
        inv = np.float32(500000.0) ** (-np.arange(half, dtype=np.float32) * np.float32(2.0) / np.float32(2 * half))
        ang = (pos[:, None] * inv[None, :].astype(np.float32)).astype(np.float32)
        rope += [np.cos(ang), np.sin(ang)]
    rope = np.concatenate(rope, 1).astype(np.float32).reshape(T, P, -1).transpose(1, 0, 2)
    dist = np.arange(S)[:, None] - np.arange(S)[None, :]
    count = sum(((dist >= 0) & (dist % dil == 0) & (dist <= window)).astype(np.int64)
                for window, dil in ((128, 1), (512, 4), (2048, 16)))
    log_count = np.where(count > 0, np.log(np.maximum(count, 1)), NEG)
    causal = np.where(dist >= 0, 0.0, NEG)
    masks = np.stack([log_count, causal]).astype(np.float32).reshape(2, T, P, S).transpose(2, 0, 1, 3)
    return {"ident": np.eye(P, dtype=np.float32), "rope": np.ascontiguousarray(rope),
            "masks": np.ascontiguousarray(masks).reshape(P, -1)}


def kernel(**inputs):
    import concourse.bacc as bacc
    from concourse.bass_utils import run_bass_kernel_spmd

    nc = bacc.Bacc("TRN2", target_bir_lowering=False, num_devices=1)
    arrays = {f"in_{n}": a for n, a in arrange(inputs).items()}
    io = {n[3:]: nc.dram_tensor(n, a.shape, mybir.dt.from_np(a.dtype), kind="ExternalInput").ap()
          for n, a in arrays.items()}
    io["out"] = nc.dram_tensor("out", (1, S, D), F32, kind="ExternalOutput").ap()
    build_program(nc, io)
    r = run_bass_kernel_spmd(nc, [arrays], core_ids=[0])
    return r.results[0]["out"]
```
